# Optimizing a Trainium2 kernel written in Bass

```python
import jax, jax.numpy as jnp
from jax import lax
import numpy as np
import math

D_MODEL = 1024
BATCH = 1
SEQ = 256
DEPTH = 2

HEAD_DIM = 64
N_ATTN_HEADS = 8
N_KV_GROUPS = 2
GQA_RATIO = N_ATTN_HEADS // N_KV_GROUPS
ATTN_WIDTH = N_ATTN_HEADS * HEAD_DIM
N_MLP_GROUPS = 8
MLP_WIDTH = N_MLP_GROUPS * HEAD_DIM
MIX_WIDTH = ATTN_WIDTH + MLP_WIDTH
KV_WIDTH = N_KV_GROUPS * HEAD_DIM
N_BRANCH = 3
GATE_WIDTH = N_ATTN_HEADS * N_BRANCH
IN_SIZES = [ATTN_WIDTH] + [KV_WIDTH] * 6 + [GATE_WIDTH, MLP_WIDTH, MLP_WIDTH]
IN_WIDTH = ATTN_WIDTH + 6 * KV_WIDTH + GATE_WIDTH + 2 * MLP_WIDTH
ROT_DIM = HEAD_DIM // 4
ROPE_THETA = 500000.0
CMP_LEN = 32
CMP_STRIDE = 16
CMP_HIDDEN = 256
SEL_LEN = 64
N_SELECT = 16
WINDOW = 512
Q_BLOCK = 128
CHUNK = 128
D_FF = 2816
CONV_WIDTH = 3
PLE_DIM = 256
NORM_EPS = 1e-6
NEG = -1e30
FORCED = 1e9


def rms_norm(x, gain):
    xf = x.astype(jnp.float32)
    y = xf * lax.rsqrt(jnp.mean(xf * xf, axis=-1, keepdims=True) + NORM_EPS)
    return (y * gain.astype(jnp.float32)).astype(x.dtype)

def layer_norm(x, gain, bias):
    xf = x.astype(jnp.float32)
    mu = jnp.mean(xf, axis=-1, keepdims=True)
    var = jnp.mean(jnp.square(xf - mu), axis=-1, keepdims=True)
    y = (xf - mu) * lax.rsqrt(var + NORM_EPS) * gain.astype(jnp.float32) + bias.astype(jnp.float32)
    return y.astype(x.dtype)

def rope_partial(x, pos):
    half = ROT_DIM // 2
    inv = ROPE_THETA ** (-jnp.arange(half, dtype=jnp.float32) / half)
    ang = pos.astype(jnp.float32)[:, None] * inv[None, :]
    cos = jnp.cos(ang)[:, None, :]
    sin = jnp.sin(ang)[:, None, :]
    xr = x[..., :ROT_DIM].astype(jnp.float32)
    x1, x2 = xr[..., :half], xr[..., half:]
    rot = jnp.concatenate([x1 * cos - x2 * sin, x2 * cos + x1 * sin], axis=-1).astype(x.dtype)
    return jnp.concatenate([rot, x[..., ROT_DIM:]], axis=-1)

def masked_softmax(s, mask):
    s = jnp.where(mask, s, NEG)
    m = jnp.max(s, axis=-1, keepdims=True)
    e = jnp.exp(s - m) * mask
    return e / jnp.maximum(jnp.sum(e, axis=-1, keepdims=True), 1e-30)

def compress(t, pe, w1, b1, w2, b2):
    B, S, G, D = t.shape
    r = CMP_LEN // CMP_STRIDE
    nch = S // CMP_STRIDE
    nc = nch - r + 1
    ch = t.reshape(B, nch, CMP_STRIDE, G, D)
    blocks = jnp.concatenate([ch[:, j:j + nc] for j in range(r)], axis=2)
    blocks = blocks + pe[None, None, :, None, :]
    flat = blocks.transpose(0, 1, 3, 2, 4).reshape(B, nc, G, CMP_LEN * D)
    h = jax.nn.gelu(flat @ w1 + b1)
    return h @ w2 + b2

def nsa_attention(q, kc, vc, ks, vs, kw, vw, gates):
    B, S, H, D = q.shape
    G = kc.shape[2]
    R = H // G
    nc = kc.shape[1]
    ns = S // SEL_LEN
    n_sel = min(N_SELECT, ns)
    scale = D ** -0.5
    cmp_start = jnp.arange(nc) * CMP_STRIDE
    cmp_end = cmp_start + CMP_LEN - 1
    sel_start = jnp.arange(ns) * SEL_LEN
    overlap = ((cmp_end[:, None] >= sel_start[None, :]) &
               (cmp_start[:, None] <= sel_start[None, :] + SEL_LEN - 1)).astype(jnp.float32)
    ks_blk = ks.reshape(B, ns, SEL_LEN, G, D).transpose(0, 3, 1, 2, 4)
    vs_blk = vs.reshape(B, ns, SEL_LEN, G, D).transpose(0, 3, 1, 2, 4)
    kw_pad = jnp.pad(kw, ((0, 0), (WINDOW, 0), (0, 0), (0, 0)))
    vw_pad = jnp.pad(vw, ((0, 0), (WINDOW, 0), (0, 0), (0, 0)))
    qg = q.reshape(B, S, G, R, D)
    gg = gates.reshape(B, S, G, R, N_BRANCH)
    bi = jnp.arange(B)[:, None, None, None]
    gi = jnp.arange(G)[None, :, None, None]
    blk = jnp.arange(ns)
    f32 = jnp.float32

    def block(qi):
        t0 = qi * Q_BLOCK
        tq = t0 + jnp.arange(Q_BLOCK)
        qb = lax.dynamic_slice_in_dim(qg, t0, Q_BLOCK, axis=1)
        gb = lax.dynamic_slice_in_dim(gg, t0, Q_BLOCK, axis=1)
        s_c = jnp.einsum('bqgrd,bngd->bgrqn', qb, kc, preferred_element_type=f32) * scale
        p_c = masked_softmax(s_c, cmp_end[None, :] <= tq[:, None])
        o_c = jnp.einsum('bgrqn,bngd->bqgrd', p_c.astype(vc.dtype), vc)
        imp = jnp.einsum('bgrqn,nj->bgqj', p_c, overlap)
        cur = tq // SEL_LEN
        valid = blk[None, :] <= cur[:, None]
        forced = valid & ((blk[None, :] == 0) | (blk[None, :] == cur[:, None]) | (blk[None, :] == cur[:, None] - 1))
        score = jnp.where(forced, FORCED, jnp.where(valid, imp, NEG))
        vals, idx = lax.top_k(score, n_sel)
        sel_ok = vals > NEG * 0.5
        k_g = ks_blk[bi, gi, idx].reshape(B, G, Q_BLOCK, n_sel * SEL_LEN, D)
        v_g = vs_blk[bi, gi, idx].reshape(B, G, Q_BLOCK, n_sel * SEL_LEN, D)
        kpos = idx[..., None] * SEL_LEN + jnp.arange(SEL_LEN)
        mask_s = ((kpos <= tq[:, None, None]) & sel_ok[..., None]).reshape(B, G, Q_BLOCK, n_sel * SEL_LEN)
        s_s = jnp.einsum('bqgrd,bgqkd->bgrqk', qb, k_g, preferred_element_type=f32) * scale
        p_s = masked_softmax(s_s, mask_s[:, :, None])
        o_s = jnp.einsum('bgrqk,bgqkd->bqgrd', p_s.astype(v_g.dtype), v_g)
        kwb = lax.dynamic_slice_in_dim(kw_pad, t0, Q_BLOCK + WINDOW, axis=1)
        vwb = lax.dynamic_slice_in_dim(vw_pad, t0, Q_BLOCK + WINDOW, axis=1)
        kpos_w = t0 - WINDOW + jnp.arange(Q_BLOCK + WINDOW)
        mask_w = ((kpos_w[None, :] <= tq[:, None]) & (kpos_w[None, :] > tq[:, None] - WINDOW)
                  & (kpos_w[None, :] >= 0))
        s_w = jnp.einsum('bqgrd,bkgd->bgrqk', qb, kwb, preferred_element_type=f32) * scale
        p_w = masked_softmax(s_w, mask_w)
        o_w = jnp.einsum('bgrqk,bkgd->bqgrd', p_w.astype(vwb.dtype), vwb)
        o = gb[..., 0:1] * o_c + gb[..., 1:2] * o_s + gb[..., 2:3] * o_w
        return o.reshape(B, Q_BLOCK, H * D)

    out = lax.map(block, jnp.arange(S // Q_BLOCK))
    return out.transpose(1, 0, 2, 3).reshape(B, S, H * D)

def spatial_gating(u, v, ln_g, ln_b, w_s, b_s):
    B, S, _ = u.shape
    u = jax.nn.gelu(u)
    v = layer_norm(jax.nn.gelu(v), ln_g, ln_b)
    vc = v.reshape(B, S // CHUNK, CHUNK, N_MLP_GROUPS, HEAD_DIM)
    causal = jnp.tril(jnp.ones((CHUNK, CHUNK), dtype=bool))
    ws = jnp.where(causal[None], w_s, 0)
    mixed = jnp.einsum('gts,bcsgd->bctgd', ws, vc) + b_s.T[None, None, :, :, None]
    return u * mixed.reshape(B, S, MLP_WIDTH)

def conv_ffn(x, w_up, conv_w, conv_b, w_down):
    S = x.shape[1]
    h = x @ w_up
    hp = jnp.pad(h, ((0, 0), (CONV_WIDTH - 1, 0), (0, 0)))
    hc = conv_b
    for k in range(CONV_WIDTH):
        hc = hc + hp[:, k:k + S] * conv_w[k]
    g, up = jnp.split(hc, 2, axis=-1)
    return (jax.nn.silu(g) * up) @ w_down

def first_inputs(seed: int = 0) -> dict:
    key = jax.random.key(seed)
    ks = jax.random.split(key, 32)
    L = DEPTH

    def nrm(k, shape, scale):
        return jax.random.normal(k, shape, dtype=jnp.float32) * scale

    def gain(k, shape):
        return 1.0 + nrm(k, shape, 0.05)

    return {
        "x": nrm(ks[0], (BATCH, SEQ, D_MODEL), 1.0),
        "p": nrm(ks[1], (DEPTH, BATCH, SEQ, PLE_DIM), 1.0),
        "pre_mix_g": gain(ks[2], (L, D_MODEL)),
        "w_in": nrm(ks[3], (L, D_MODEL, IN_WIDTH), D_MODEL ** -0.5),
        "cmp_pe": nrm(ks[4], (L, 2, CMP_LEN, HEAD_DIM), 0.1),
        "cmp_w1": nrm(ks[5], (L, 2, CMP_LEN * HEAD_DIM, CMP_HIDDEN), (CMP_LEN * HEAD_DIM) ** -0.5),
        "cmp_b1": nrm(ks[6], (L, 2, CMP_HIDDEN), 0.02),
        "cmp_w2": nrm(ks[7], (L, 2, CMP_HIDDEN, HEAD_DIM), CMP_HIDDEN ** -0.5),
        "cmp_b2": nrm(ks[8], (L, 2, HEAD_DIM), 0.02),
        "gmlp_ln_g": gain(ks[9], (L, MLP_WIDTH)),
        "gmlp_ln_b": nrm(ks[10], (L, MLP_WIDTH), 0.02),
        "gmlp_ws": nrm(ks[11], (L, N_MLP_GROUPS, CHUNK, CHUNK), 0.5 * CHUNK ** -0.5),
        "gmlp_bs": 1.0 + nrm(ks[12], (L, N_MLP_GROUPS, CHUNK), 0.1),
        "attn_out_g": gain(ks[13], (L, ATTN_WIDTH)),
        "mlp_out_g": gain(ks[14], (L, MLP_WIDTH)),
        "w_o": nrm(ks[15], (L, MIX_WIDTH, D_MODEL), MIX_WIDTH ** -0.5),
        "post_mix_g": gain(ks[16], (L, D_MODEL)),
        "pre_ffn_g": gain(ks[17], (L, D_MODEL)),
        "w_up": nrm(ks[18], (L, D_MODEL, 2 * D_FF), D_MODEL ** -0.5),
        "conv_w": nrm(ks[19], (L, CONV_WIDTH, 2 * D_FF), CONV_WIDTH ** -0.5),
        "conv_b": nrm(ks[20], (L, 2 * D_FF), 0.02),
        "w_down": nrm(ks[21], (L, D_FF, D_MODEL), D_FF ** -0.5),
        "post_ffn_g": gain(ks[22], (L, D_MODEL)),
        "ple_norm_g": gain(ks[23], (L, D_MODEL)),
        "w_ple_gate": nrm(ks[24], (L, D_MODEL, D_MODEL), D_MODEL ** -0.5),
        "w_ple_proj": nrm(ks[25], (L, PLE_DIM, D_MODEL), PLE_DIM ** -0.5),
    }

def first_block(x, p, pre_mix_g, w_in, cmp_pe, cmp_w1, cmp_b1, cmp_w2, cmp_b2,
              gmlp_ln_g, gmlp_ln_b, gmlp_ws, gmlp_bs, attn_out_g, mlp_out_g, w_o,
              post_mix_g, pre_ffn_g, w_up, conv_w, conv_b, w_down, post_ffn_g,
              ple_norm_g, w_ple_gate, w_ple_proj):
    B, S, _ = x.shape
    pos = jnp.arange(S)
    split_at = [int(o) for o in np.cumsum(IN_SIZES)[:-1]]
    nc = S // CMP_STRIDE - CMP_LEN // CMP_STRIDE + 1
    cmp_pos = jnp.arange(nc) * CMP_STRIDE + CMP_LEN - 1
    h = x
    for i in range(DEPTH):
        a = rms_norm(h, pre_mix_g[i])
        z = a @ w_in[i]
        zq, zkc, zvc, zks, zvs, zkw, zvw, zg, zu, zv = jnp.split(z, split_at, axis=-1)
        kv = lambda t: t.reshape(B, S, N_KV_GROUPS, HEAD_DIM)
        q = rope_partial(zq.reshape(B, S, N_ATTN_HEADS, HEAD_DIM), pos)
        kc = compress(kv(zkc), cmp_pe[i, 0], cmp_w1[i, 0], cmp_b1[i, 0], cmp_w2[i, 0], cmp_b2[i, 0])
        vc = compress(kv(zvc), cmp_pe[i, 1], cmp_w1[i, 1], cmp_b1[i, 1], cmp_w2[i, 1], cmp_b2[i, 1])
        kc = rope_partial(kc, cmp_pos)
        k_sel = rope_partial(kv(zks), pos)
        k_win = rope_partial(kv(zkw), pos)
        gates = jax.nn.sigmoid(zg.reshape(B, S, N_ATTN_HEADS, N_BRANCH))
        attn = nsa_attention(q, kc, vc, k_sel, kv(zvs), k_win, kv(zvw), gates)
        mlp = spatial_gating(zu, zv, gmlp_ln_g[i], gmlp_ln_b[i], gmlp_ws[i], gmlp_bs[i])
        mix = jnp.concatenate([rms_norm(attn, attn_out_g[i]), rms_norm(mlp, mlp_out_g[i])], axis=-1) @ w_o[i]
        h = h + rms_norm(mix, post_mix_g[i])
        f = conv_ffn(rms_norm(h, pre_ffn_g[i]), w_up[i], conv_w[i], conv_b[i], w_down[i])
        h = h + rms_norm(f, post_ffn_g[i])
        gate = jax.nn.sigmoid(rms_norm(h, ple_norm_g[i]) @ w_ple_gate[i])
        h = h + gate * (p[i] @ w_ple_proj[i])
    return h


POOL_WIDTH = 512
POOL_WINDOWS = (2, 4, 8, 16)
POOL_GROUPS = len(POOL_WINDOWS)
POOL_GROUP_DIM = POOL_WIDTH // POOL_GROUPS
GLA_HEADS = 4
GLA_DK = 64
GLA_DV = 128
GLA_KEY_WIDTH = GLA_HEADS * GLA_DK
GLA_VAL_WIDTH = GLA_HEADS * GLA_DV
GLA_GATE_RANK = 16
GLA_GATE_TAU = 16.0
GLA_CHUNK = 64
MLA_HEADS = 8
MLA_Q_RANK = 384
MLA_KV_RANK = 256
MLA_NOPE = 64
MLA_ROPE = 32
MLA_V = 64
MLA_QK = MLA_NOPE + MLA_ROPE
MLA_VAL_WIDTH = MLA_HEADS * MLA_V
ROPE_BASE = 10000.0
D_FF_2 = -(-8 * D_MODEL // (3 * 256)) * 256
EPS = 1e-6

IN_SIZES_2 = (POOL_WIDTH, GLA_KEY_WIDTH, GLA_KEY_WIDTH, GLA_VAL_WIDTH, GLA_VAL_WIDTH, GLA_GATE_RANK,
            MLA_Q_RANK, MLA_KV_RANK, MLA_ROPE, N_BRANCH * D_MODEL)
IN_WIDTH_2 = sum(IN_SIZES_2)
IN_OFFSETS = tuple(int(v) for v in np.cumsum(IN_SIZES_2)[:-1])


def rms_norm_2(x, g):
    xf = x.astype(jnp.float32)
    y = xf * lax.rsqrt(jnp.mean(xf * xf, axis=-1, keepdims=True) + EPS)
    return (y * g.astype(jnp.float32)).astype(x.dtype)

def rope_tables(positions):
    inv_freq = ROPE_BASE ** (-jnp.arange(0, MLA_ROPE, 2, dtype=jnp.float32) / MLA_ROPE)
    ang = positions.astype(jnp.float32)[..., None] * inv_freq
    return jnp.cos(ang), jnp.sin(ang)

def apply_rope(x, cos, sin):
    half = x.shape[-1] // 2
    x1, x2 = x[..., :half], x[..., half:]
    return jnp.concatenate([x1 * cos - x2 * sin, x2 * cos + x1 * sin], axis=-1).astype(x.dtype)

def pool_mixer(u, w_pool, pool_scale):
    b, s, _ = u.shape
    uf = u.astype(jnp.float32).reshape(b, s, POOL_GROUPS, POOL_GROUP_DIM)
    cs = jnp.cumsum(uf, axis=1)
    t = jnp.arange(s)
    means = []
    for g, w in enumerate(POOL_WINDOWS):
        c = cs[:, :, g]
        prev = jnp.pad(c, ((0, 0), (w, 0), (0, 0)))[:, :s]
        cnt = jnp.minimum(t + 1, w).astype(jnp.float32)[None, :, None]
        means.append((c - prev) / cnt)
    pooled = jnp.stack(means, axis=2)
    diff = (pooled - uf).astype(u.dtype)
    y = jnp.einsum('bsgc,gcd->bsgd', diff, w_pool).reshape(b, s, POOL_WIDTH)
    return y * pool_scale

def gla_mixer(q, k, v, r, a1, w_a2, b_a, g_norm):
    b, s, _ = q.shape
    n = s // GLA_CHUNK
    f32 = jnp.float32
    log_a = jax.nn.log_sigmoid((a1 @ w_a2 + b_a).astype(f32)) / GLA_GATE_TAU

    def heads(t, d):
        return t.astype(f32).reshape(b, n, GLA_CHUNK, GLA_HEADS, d).transpose(0, 3, 1, 2, 4)

    qh = heads(q, GLA_DK) * (GLA_DK ** -0.5)
    kh = heads(k, GLA_DK)
    vh = heads(v, GLA_DV)
    cum = jnp.cumsum(heads(log_a, GLA_DK), axis=3)
    cum_last = cum[:, :, :, -1:, :]
    q_dec = qh * jnp.exp(cum)
    k_inv = kh * jnp.exp(-cum)
    k_end = kh * jnp.exp(cum_last - cum)
    mask = jnp.tril(jnp.ones((GLA_CHUNK, GLA_CHUNK), dtype=bool))
    att = jnp.where(mask, jnp.einsum('bhntd,bhnsd->bhnts', q_dec, k_inv), 0.0)
    o_intra = jnp.einsum('bhnts,bhnse->bhnte', att, vh)
    kv = jnp.einsum('bhnsd,bhnse->bhnde', k_end, vh)
    decay = jnp.exp(cum_last[:, :, :, 0, :])

    def step(state, inp):
        dec, kv_n = inp
        return dec[..., None] * state + kv_n, state

    s0 = jnp.zeros((b, GLA_HEADS, GLA_DK, GLA_DV), f32)
    _, states = lax.scan(step, s0, (jnp.moveaxis(decay, 2, 0), jnp.moveaxis(kv, 2, 0)))
    states = jnp.moveaxis(states, 0, 2)
    o_inter = jnp.einsum('bhntd,bhnde->bhnte', q_dec, states)
    o = (o_intra + o_inter).transpose(0, 2, 3, 1, 4).reshape(b, s, GLA_HEADS, GLA_DV)
    o = o * lax.rsqrt(jnp.mean(o * o, axis=-1, keepdims=True) + EPS)
    o = o * g_norm.astype(f32).reshape(GLA_HEADS, GLA_DV)
    o = o.reshape(b, s, GLA_VAL_WIDTH) * jax.nn.silu(r.astype(f32))
    return o.astype(q.dtype)

def mla_mixer(cq, ckv, kr, cos, sin, q_norm, w_uq, kv_norm, w_ukv):
    b, s, _ = cq.shape
    qf = (rms_norm_2(cq, q_norm) @ w_uq).reshape(b, s, MLA_HEADS, MLA_QK)
    kvf = (rms_norm_2(ckv, kv_norm) @ w_ukv).reshape(b, s, MLA_HEADS, MLA_NOPE + MLA_V)
    q_nope, q_rope = qf[..., :MLA_NOPE], qf[..., MLA_NOPE:]
    k_nope, v = kvf[..., :MLA_NOPE], kvf[..., MLA_NOPE:]
    q_rope = apply_rope(q_rope, cos[:, :, None], sin[:, :, None])
    k_rope = apply_rope(kr, cos, sin)
    q = jnp.concatenate([q_nope, q_rope], axis=-1)
    k = jnp.concatenate([k_nope, jnp.broadcast_to(k_rope[:, :, None], (b, s, MLA_HEADS, MLA_ROPE))], axis=-1)
    nb = s // Q_BLOCK
    qb = q.reshape(b, nb, Q_BLOCK, MLA_HEADS, MLA_QK).transpose(1, 0, 2, 3, 4)
    starts = jnp.arange(nb) * Q_BLOCK
    kpos = jnp.arange(s)
    scale = MLA_QK ** -0.5

    def attend(args):
        q_blk, start = args
        sc = jnp.einsum('bqhd,bkhd->bhqk', q_blk, k).astype(jnp.float32) * scale
        qpos = start + jnp.arange(Q_BLOCK)
        sc = jnp.where(qpos[:, None] >= kpos[None, :], sc, jnp.finfo(jnp.float32).min)
        p = jax.nn.softmax(sc, axis=-1)
        return jnp.einsum('bhqk,bkhe->bqhe', p.astype(v.dtype), v)

    o = lax.map(attend, (qb, starts))
    return o.transpose(1, 0, 2, 3, 4).reshape(b, s, MLA_VAL_WIDTH)

def hybrid_layer(x, cos, sin, n_pre_mix, n_post_mix, n_pre_ffn, n_post_ffn, w_in, w_pool, pool_scale, w_a,
                 w_gla_a2, b_gla_a, gla_norm, w_b, mla_q_norm, w_mla_uq, mla_kv_norm, w_mla_ukv, w_c, w_o,
                 w_ffn_gu, w_ffn_down):
    b, s, d = x.shape
    h = rms_norm_2(x, n_pre_mix)
    proj = h @ w_in
    (u_pool, g_q, g_k, g_v, g_r, g_a1, m_cq, m_ckv, m_kr, gate_logits) = jnp.split(proj, IN_OFFSETS, axis=-1)
    y_a = pool_mixer(u_pool, w_pool, pool_scale) @ w_a
    y_b = gla_mixer(g_q, g_k, g_v, g_r, g_a1, w_gla_a2, b_gla_a, gla_norm) @ w_b
    y_c = mla_mixer(m_cq, m_ckv, m_kr, cos, sin, mla_q_norm, w_mla_uq, mla_kv_norm, w_mla_ukv) @ w_c
    gates = jax.nn.sigmoid(gate_logits.astype(jnp.float32)).astype(x.dtype).reshape(b, s, N_BRANCH, d)
    merged = gates[:, :, 0] * y_a + gates[:, :, 1] * y_b + gates[:, :, 2] * y_c
    x = x + rms_norm_2(merged @ w_o, n_post_mix)
    h = rms_norm_2(x, n_pre_ffn)
    gu = h @ w_ffn_gu
    ffn = (jax.nn.silu(gu[..., :D_FF_2]) * gu[..., D_FF_2:]) @ w_ffn_down
    return x + rms_norm_2(ffn, n_post_ffn)

def second_inputs(seed: int = 0) -> dict:
    key = jax.random.key(seed)
    ks = jax.random.split(key, 24)
    f32 = jnp.float32

    def dense(k, shape, fan_in):
        return jax.random.normal(k, shape, f32) * (fan_in ** -0.5)

    def gain(k, shape):
        return 1.0 + 0.02 * jax.random.normal(k, shape, f32)

    x = jax.random.normal(ks[0], (BATCH, SEQ, D_MODEL), f32)
    offsets = jax.random.randint(ks[1], (BATCH, 1), 0, 4096, dtype=jnp.int32)
    positions = offsets + jnp.arange(SEQ, dtype=jnp.int32)[None, :]
    return {
        "x": x,
        "positions": positions,
        "norm_pre_mix": gain(ks[2], (DEPTH, D_MODEL)),
        "norm_post_mix": gain(ks[3], (DEPTH, D_MODEL)),
        "norm_pre_ffn": gain(ks[4], (DEPTH, D_MODEL)),
        "norm_post_ffn": gain(ks[5], (DEPTH, D_MODEL)),
        "w_in": dense(ks[6], (DEPTH, D_MODEL, IN_WIDTH_2), D_MODEL),
        "w_pool": dense(ks[7], (DEPTH, POOL_GROUPS, POOL_GROUP_DIM, POOL_GROUP_DIM), POOL_GROUP_DIM),
        "pool_scale": gain(ks[8], (DEPTH, POOL_WIDTH)),
        "w_a": dense(ks[9], (DEPTH, POOL_WIDTH, D_MODEL), POOL_WIDTH),
        "w_gla_a2": dense(ks[10], (DEPTH, GLA_GATE_RANK, GLA_KEY_WIDTH), GLA_GATE_RANK),
        "b_gla_a": 0.1 * jax.random.normal(ks[11], (DEPTH, GLA_KEY_WIDTH), f32),
        "gla_norm": gain(ks[12], (DEPTH, GLA_VAL_WIDTH)),
        "w_b": dense(ks[13], (DEPTH, GLA_VAL_WIDTH, D_MODEL), GLA_VAL_WIDTH),
        "mla_q_norm": gain(ks[14], (DEPTH, MLA_Q_RANK)),
        "w_mla_uq": dense(ks[15], (DEPTH, MLA_Q_RANK, MLA_HEADS * MLA_QK), MLA_Q_RANK),
        "mla_kv_norm": gain(ks[16], (DEPTH, MLA_KV_RANK)),
        "w_mla_ukv": dense(ks[17], (DEPTH, MLA_KV_RANK, MLA_HEADS * (MLA_NOPE + MLA_V)), MLA_KV_RANK),
        "w_c": dense(ks[18], (DEPTH, MLA_VAL_WIDTH, D_MODEL), MLA_VAL_WIDTH),
        "w_o": dense(ks[19], (DEPTH, D_MODEL, D_MODEL), D_MODEL),
        "w_ffn_gu": dense(ks[20], (DEPTH, D_MODEL, 2 * D_FF_2), D_MODEL),
        "w_ffn_down": dense(ks[21], (DEPTH, D_FF_2, D_MODEL), D_FF_2),
    }

def second_block(x, positions, norm_pre_mix, norm_post_mix, norm_pre_ffn, norm_post_ffn, w_in, w_pool,
              pool_scale, w_a, w_gla_a2, b_gla_a, gla_norm, w_b, mla_q_norm, w_mla_uq, mla_kv_norm,
              w_mla_ukv, w_c, w_o, w_ffn_gu, w_ffn_down):
    cos, sin = rope_tables(positions)
    for l in range(DEPTH):
        x = hybrid_layer(x, cos, sin, norm_pre_mix[l], norm_post_mix[l], norm_pre_ffn[l], norm_post_ffn[l],
                         w_in[l], w_pool[l], pool_scale[l], w_a[l], w_gla_a2[l], b_gla_a[l], gla_norm[l],
                         w_b[l], mla_q_norm[l], w_mla_uq[l], mla_kv_norm[l], w_mla_ukv[l], w_c[l], w_o[l],
                         w_ffn_gu[l], w_ffn_down[l])
    return x


def setup_inputs(seed=0):
    out = dict(first_inputs(seed))
    for name, value in second_inputs(seed + 1).items():
        if name != "x":
            out[name + "_2"] = value
    return out


def reference(
    x, p, pre_mix_g, w_in, cmp_pe, cmp_w1, cmp_b1, cmp_w2, cmp_b2, gmlp_ln_g, gmlp_ln_b,
    gmlp_ws, gmlp_bs, attn_out_g, mlp_out_g, w_o, post_mix_g, pre_ffn_g, w_up, conv_w, conv_b,
    w_down, post_ffn_g, ple_norm_g, w_ple_gate, w_ple_proj, positions_2, norm_pre_mix_2,
    norm_post_mix_2, norm_pre_ffn_2, norm_post_ffn_2, w_in_2, w_pool_2, pool_scale_2, w_a_2,
    w_gla_a2_2, b_gla_a_2, gla_norm_2, w_b_2, mla_q_norm_2, w_mla_uq_2, mla_kv_norm_2,
    w_mla_ukv_2, w_c_2, w_o_2, w_ffn_gu_2, w_ffn_down_2,
):
    x = first_block(
        x, p, pre_mix_g, w_in, cmp_pe, cmp_w1, cmp_b1, cmp_w2, cmp_b2, gmlp_ln_g, gmlp_ln_b,
        gmlp_ws, gmlp_bs, attn_out_g, mlp_out_g, w_o, post_mix_g, pre_ffn_g, w_up, conv_w,
        conv_b, w_down, post_ffn_g, ple_norm_g, w_ple_gate, w_ple_proj,
    )
    return second_block(
        x, positions_2, norm_pre_mix_2, norm_post_mix_2, norm_pre_ffn_2, norm_post_ffn_2,
        w_in_2, w_pool_2, pool_scale_2, w_a_2, w_gla_a2_2, b_gla_a_2, gla_norm_2, w_b_2,
        mla_q_norm_2, w_mla_uq_2, mla_kv_norm_2, w_mla_ukv_2, w_c_2, w_o_2, w_ffn_gu_2,
        w_ffn_down_2,
    )


_drawn_inputs = setup_inputs


def setup_inputs(seed=0):
    import zlib

    import numpy as np

    out = dict(_drawn_inputs(seed))
    spreads = {}
    factors = {'gmlp_ln_g': 3.928,
     'gmlp_ln_b': 8.0,
     'ple_norm_g': 5.652,
     'norm_pre_mix_2': 3.129,
     'norm_post_mix_2': 4.731,
     'norm_pre_ffn_2': 3.718,
     'norm_post_ffn_2': 5.557,
     'pool_scale_2': 6.243,
     'b_gla_a_2': 2.696,
     'gla_norm_2': 8.0,
     'mla_q_norm_2': 8.0,
     'mla_kv_norm_2': 8.0}
    for name, (base, spread) in spreads.items():
        noise = np.random.default_rng([zlib.crc32(name.encode()), seed]).standard_normal(out[name].shape)
        drawn = base * np.exp(spread * noise) if base else spread * noise
        out[name] = __import__('jax').numpy.asarray(drawn.astype(out[name].dtype))
    for name, factor in factors.items():
        out[name] = (out[name] * factor).astype(out[name].dtype)
    return out
```

```python
import concourse.bass as bass
from concourse import mybir
from contextlib import ExitStack

F32 = mybir.dt.float32
F32R = mybir.dt.float32r
I32 = mybir.dt.int32
ALU = mybir.AluOpType
ACT = mybir.ActivationFunctionType
AX = mybir.AxisListType

P = 128
SEQ, DM, DEPTH = 256, 1024, 2
TT = SEQ // P
EPS = 1e-6
NEG = -1e30
BLK = 512
UNIT = 2048
RING = 3
KC8 = DM // P

HEADS, HD, GROUPS = 8, 64, 2
W1 = 2328
GATE1, U1, V1 = 1280, 1304, 1816
CMP_N, CMP_HID = 15, 256
ROPE_UNITS = 20
W2 = 5808
Z2 = 2736
GQ, GK, GV, GR, GA, CQ, CKV, KR = 512, 768, 1024, 1536, 2048, 2064, 2448, 2704
QK = 96
D_FF = 2816
FB = 256
FSTEPS = D_FF // FB
FUNITS = 3 * FSTEPS
NVEC1 = 252
NVEC2 = 29


class Seen:

    def __init__(self):
        self.n = {}

    def __call__(self, sem, k=1):
        self.n[id(sem)] = self.n.get(id(sem), 0) + k
        return self.n[id(sem)]

    def now(self, sem):
        return self.n.get(id(sem), 0)


def blocks_of(lo, hi):
    return [(a, min(BLK, hi - a)) for a in range(lo, hi, BLK)]


def unit_plan(A):
    units, ffn = [], {}

    def cols(w, k0, k1, c0, n):
        return (w[k0 * P:k1 * P, c0:c0 + n].rearrange("(k p) n -> p k n", p=P), k1 - k0, n)

    def matrix(w, nk, blocks):
        for c0, n in blocks:
            for k0 in range(0, nk, 4):
                units.append(cols(w, k0, min(k0 + 4, nk), c0, n))

    def ffn_units(key, up, down):
        ffn[key] = (len(units), up, down)
        units.extend([None] * FUNITS)

    for l in range(DEPTH):
        matrix(A["w_in"][l], KC8, blocks_of(0, W1))
        for kv in range(2):
            for half in range(2):
                units.append(cols(A["cmp_w1"][l, kv], half * 8, half * 8 + 8, 0, CMP_HID))
        matrix(A["w_o"][l], KC8, blocks_of(0, DM))
        ffn_units(("first", l), A["w_up"][l], A["w_down"][l])
        matrix(A["w_ple_gate"][l], KC8, blocks_of(0, DM))
        units.append(cols(A["w_ple_proj"][l], 0, 2, 0, DM))
    for l in range(DEPTH):
        matrix(A["w_in_2"][l], KC8, blocks_of(0, Z2) + blocks_of(Z2, W2))
        matrix(A["w_a_2"][l], 4, blocks_of(0, DM))
        matrix(A["w_b_2"][l], 4, blocks_of(0, DM))
        matrix(A["w_mla_uq_2"][l], 3, [(0, 384), (384, 384)])
        units.append(cols(A["w_mla_ukv_2"][l], 0, 2, 0, DM))
        matrix(A["w_c_2"][l], 4, blocks_of(0, DM))
        matrix(A["w_o_2"][l], KC8, blocks_of(0, DM))
        ffn_units(("second", l), A["w_ffn_gu_2"][l], A["w_ffn_down_2"][l])
    return units, ffn


def two_blocks(nc, A, out):
    units, ffn = unit_plan(A)
    ffn_starts = sorted(u for u, _, _ in ffn.values())

    with ExitStack() as ctx:
        def sb(name, shape, dt=F32):
            return ctx.enter_context(nc.sbuf_tensor(name, shape, dt))

        def sem(name):
            return ctx.enter_context(nc.semaphore(name))

        raw = sb("w_raw", [P, RING, UNIT])
        whi = sb("w_hi", [P, RING, UNIT], F32R)
        wlo = sb("w_lo", [P, RING, UNIT], F32R)
        xhi = sb("x_hi", [P, KC8, SEQ], F32R)
        xlo = sb("x_lo", [P, KC8, SEQ], F32R)
        fhi = sb("ffn_hi", [P, 2, 2, SEQ], F32R)
        flo = sb("ffn_lo", [P, 2, 2, SEQ], F32R)
        h = sb("h", [P, TT, DM])
        normed = sb("normed", [P, TT, DM])
        merged = sb("merged", [P, TT, DM])
        z = sb("z", [P, TT, Z2])
        area = sb("area", [P, 12288])
        vecs = sb("vecs", [P, DEPTH * (NVEC1 + NVEC2)])
        post_g = sb("post_g", [P, 2, DM])
        ident = sb("ident", [P, P])
        keep_le = sb("keep_le", [P, P])
        causal = sb("causal", [P, P])
        chunk_le = sb("chunk_le", [P, P])
        chunk_gt = sb("chunk_gt", [P, P])
        chunk_of = sb("chunk_of", [P, 2])
        cmp_mask = sb("cmp_mask", [P, 2, TT, CMP_N])
        rope2 = sb("rope2", [P, 2, TT, 16])
        b_gla = sb("b_gla", [P, 256])
        ssq = sb("ssq", [P, 8])
        rstd = sb("rstd", [P, 8])
        half_neg = sb("half_neg", [P, 8])
        stat = sb("stat", [P, TT, 6])
        mean_var = sb("mean_var", [P, TT, 2])
        nmax = sb("nmax", [P, 2, 2])
        esum = sb("esum", [P, TT, HEADS, 3])
        cmax = sb("cmax", [P, TT, HEADS])
        m_sum = sb("m_sum", [P, TT, HEADS])
        w_a2 = sb("w_a2", [16, 256])
        zero_row = sb("zero_row", [1, BLK], mybir.dt.bfloat16)
        acc_banks = ctx.enter_context(nc.psum_tensor("acc", [P, 2, TT, BLK], F32))
        acc = acc_banks[:].rearrange("p b t n -> p t b n")
        aux = ctx.enter_context(nc.psum_tensor("aux", [P, 4, BLK], F32))

        def carve(start, n, parts=P):
            return area[0:parts, start:start + n]

        qT = carve(0, 2048, HD).rearrange("p (h s) -> p h s", h=HEADS)
        kT = carve(2048, 1024, HD).rearrange("p (u s) -> p u s", u=4)
        e_buf = carve(3072, 1024).rearrange("p (b n) -> p b n", b=2)
        pT = carve(4096, 1024).rearrange("p (b n) -> p b n", b=2)
        ecT = carve(3072, 2048, CMP_N).rearrange("p (t h q) -> p t h q", t=TT, h=HEADS)
        attn = carve(6144, 1024).rearrange("p (t n) -> p t n", t=TT)
        zc2 = carve(6144, 1024).rearrange("p (t u a d) -> p t u a d", t=TT, u=4, a=2)
        ws_raw = carve(7168, 1024).rearrange("p (g s) -> p g s", g=8)
        wsT = carve(8192, 1024).rearrange("p (g s) -> p g s", g=8)
        mlp = carve(9216, 1024).rearrange("p (t n) -> p t n", t=TT)
        x_cmp = carve(10240, 960).rearrange("p (k c g n) -> p k c g n", k=2, c=16, g=GROUPS)
        part = carve(10240, 1024).rearrange("p (a n) -> p a n", a=2)
        hT = carve(11776, 120).rearrange("p (k c n) -> p k c n", k=2, c=2)
        kcT = carve(11896, 30, HD).rearrange("p (g n) -> p g n", g=GROUPS)
        ec = carve(11264, 240).rearrange("p (t h n) -> p t h n", t=TT, h=HEADS)
        factor = carve(11936, 48).rearrange("p (t h b) -> p t h b", t=TT, h=HEADS)
        kcv = carve(12032, 256, CMP_N).rearrange("p (k g d) -> p k g d", k=2, g=GROUPS)
        ple_gate = carve(0, 2048).rearrange("p (t n) -> p t n", t=TT)
        mflat = merged[:].rearrange("p t n -> p (t n)")
        ln_gb = mflat[:, 0:1024].rearrange("p (a n) -> p a n", a=2)
        cmp_w2 = mflat[:, 1024:1280].rearrange("p (k c d) -> p k c d", k=2, c=2)
        cmp_b2 = mflat[0:CMP_N, 1280:1536].rearrange("p (k g d) -> p k g d", k=2, g=GROUPS)
        p_in = mflat[:, 1536:2048].rearrange("p (t n) -> p t n", t=TT)
        zflat = z[:].rearrange("p t n -> p (t n)")
        rope1_cols = z[:, :, W1:W1 + 320]
        rope1 = rope1_cols.rearrange("p t (a u f) -> p t a u f", a=2, u=ROPE_UNITS)
        rope_c = sb("rope_c", [CMP_N, 2, GROUPS, 8])
        rt = carve(3072, 1280).rearrange("p (a t u f) -> p a t u f", a=4, t=TT, u=ROPE_UNITS)
        rt_c = carve(11504, 64, CMP_N).rearrange("p (a g f) -> p a g f", a=4, g=GROUPS)
        vrow = carve(0, 512).rearrange("p (a n) -> p a n", a=4)
        gates = carve(0, 6144).rearrange("p (t b n) -> p t b n", t=TT, b=3)
        pool_mat = carve(6144, 2048).rearrange("p (s g t) -> p s g t", s=TT, g=4)
        diffT = carve(8192, 1024).rearrange("p (g t) -> p g t", g=4)
        w_pool = carve(9216, 512).rearrange("p (g d) -> p g d", g=4)
        la, e_cum, e_suf, e_inv = (normed[:].rearrange("p t n -> p (t n)")[:, i * 512:(i + 1) * 512]
                                   .rearrange("p (t n) -> p t n", t=TT) for i in range(4))
        qdT = carve(6144, 1024, HD).rearrange("p (h s) -> p h s", h=4)
        kiT = carve(7168, 1024, HD).rearrange("p (h s) -> p h s", h=4)
        attM = carve(8192, 1024).rearrange("p (t h s) -> p t h s", t=TT, h=4)
        state = carve(9216, 1536, HD).rearrange("p (n h e) -> p n h e", n=3, h=4)
        a1T = carve(10752, 256, 16)
        decay = carve(11008, 16, HD).rearrange("p (h n) -> p h n", h=4)
        o_gla = carve(11264, 1024).rearrange("p (t n) -> p t n", t=TT)
        sq_gla = carve(6144, 1024).rearrange("p (t n) -> p t n", t=TT)
        qf = zflat[:, 0:1536].rearrange("p (t h d) -> p t h d", t=TT, h=HEADS)
        kf = zflat[:, Z2:Z2 + 1536].rearrange("p (t h d) -> p t h d", t=TT, h=HEADS)
        mqT = carve(6144, 2048, QK).rearrange("p (h s) -> p h s", h=HEADS)
        mkT = carve(8192, 2048, QK).rearrange("p (h s) -> p h s", h=HEADS)
        m_v = carve(10240, 1024).rearrange("p (t h d) -> p t h d", t=TT, h=HEADS)
        m_e = carve(11264, 1024).rearrange("p (b n) -> p b n", b=2)
        m_pT = normed[:, :, 0:512]
        rt2 = zflat[:, 1536:2064]
        hc = carve(0, 2048).rearrange("p (a w c s) -> p a w c s", a=2, w=2, c=2)
        sg = carve(2048, 512).rearrange("p (c s) -> p c s", c=2)
        f_act = carve(2560, 512).rearrange("p (c s) -> p c s", c=2)

        w_loaded = [sem(f"w_loaded{i}") for i in range(RING)]
        hi_ready, lo_ready, unit_done = sem("hi_ready"), sem("lo_ready"), sem("unit_done")
        consts_in, h_in, vrows_in, out_done = sem("consts_in"), sem("h_in"), sem("vrows_in"), sem("out_done")
        small1_in, small2_in, post_in = sem("small1_in"), sem("small2_in"), sem("post_in")
        ple_in, pool_in, pos_in = sem("ple_in"), sem("pool_in"), sem("pos_in")
        vt_ready, vecs_ready, setup_done = sem("vt_ready"), sem("vecs_ready"), sem("setup_done")
        sumsq_ready, rstd_ready, normed_ready = sem("sumsq_ready"), sem("rstd_ready"), sem("normed_ready")
        tp_ready, xhi_ready, x_split = sem("tp_ready"), sem("xhi_ready"), sem("x_split")
        acc_out, h_ready = sem("acc_out"), sem("h_ready")
        zc2_done = sem("zc2_done")
        rope_done, gelu_done, ct_ready, xc_sum, xc_hi = (
            sem("rope_done"), sem("gelu_done"), sem("ct_ready"), sem("xc_sum"), sem("xc_hi"))
        xc_split, qk_ready, qk_out = sem("xc_split"), sem("qk_ready"), sem("qk_out")
        hT_out, kcv_ready, kcv_out, kcT_ready, kcT_out = (
            sem(s) for s in ("hT_out", "kcv_ready", "kcv_out", "kcT_ready", "kcT_out"))
        ws_ready, ws_out, ln_done, mix_ready = sem("ws_ready"), sem("ws_out"), sem("ln_done"), sem("mix_ready")
        ln_var = sem("ln_var")
        sc_ready, sc_shift, sc_exp, ec_ready, ect_ready, ect_out = (
            sem(s) for s in ("sc_ready", "sc_shift", "sc_exp", "ec_ready", "ect_ready", "ect_out"))
        cpv_done, cmp_out, gmlp_out, gate_done = sem("cpv_done"), sem("cmp_out"), sem("gmlp_out"), sem("gate_done")
        s_ready, max_ready, e_ready, pt_ready, pts_ready, pts_ready_dve, pv_done, mixed_ready = (
            sem(s) for s in ("s_ready", "max_ready", "e_ready", "pt_ready", "pts_ready", "pts_ready_dve", "pv_done", "mixed_ready"))
        gu_ready, hc_ready, hc_conv, sg_ready, fa_ready, fhi_ready, f_split = (
            sem(s) for s in ("gu_ready", "hc_ready", "hc_conv", "sg_ready", "fa_ready", "fhi_ready", "f_split"))
        yp_hi, yp_split = sem("yp_hi"), sem("yp_split")
        diff_ready, diff_out, ypool_ready = sem("diff_ready"), sem("diff_out"), sem("ypool_ready")
        a1_ready, a1_out, la_pre, la_x, la_ln, la_ready, cum_ready, exps_ready, qk_dec = (
            sem(s) for s in ("a1_ready", "a1_out", "la_pre", "la_x", "la_ln", "la_ready", "cum_ready",
                             "exps_ready", "qk_dec"))
        gT_ready, gT_out, att_ready, kv_ready, att_out, states_ready, og_ready, sq_out, og_silu = (
            sem(s) for s in ("gT_ready", "gT_out", "att_ready", "kv_ready", "att_out", "states_ready",
                             "og_ready", "sq_out", "og_silu"))
        mrope_done, mT_ready, mT_out = sem("mrope_done"), sem("mT_ready"), sem("mT_out")
        ang_ready, trig_done = sem("ang_ready"), sem("trig_done")

        g_of = {}
        c = 0
        for l in range(DEPTH):
            for name, n in (("pre_mix", 8), ("attn_out", 4), ("mlp_out", 4), ("pre_ffn", 8), ("ple", 8),
                            ("cmp_pe", 32), ("cmp_b1", 4), ("gmlp_bs", 8), ("conv_b", 44), ("conv_w", 132)):
                g_of["first", l, name] = c
                c += n
        for l in range(DEPTH):
            for name, n in (("pre_mix", 8), ("pre_ffn", 8), ("pool_scale", 4), ("gla_norm", 4),
                            ("q_norm", 3), ("kv_norm", 2)):
                g_of["second", l, name] = c
                c += n

        def vec(key, i):
            return vecs[:, g_of[key] + i:g_of[key] + i + 1]

        xhi_flat, xlo_flat = (t[:].rearrange("p k s -> p (k s)") for t in (xhi, xlo))

        def x_cmp_split(flat, kv):
            return flat[:, kv * 1024:kv * 1024 + 480]

        def first_steps():
            steps = []
            for qt in range(TT):
                for hd in range(HEADS):
                    g = hd // (HEADS // GROUPS)
                    lanes = [dict(q=qT[:, hd, qt * P:(qt + 1) * P], k=kT[:, 2 * br + g, :],
                                  v=z[:, :, 896 + 256 * br + g * HD:896 + 256 * br + (g + 1) * HD],
                                  o=aux[:, (1 + br, (3, 0)[br])[qt], hd * HD:(hd + 1) * HD],
                                  sums=esum[:, qt, hd, 1 + br:2 + br]) for br in range(2)]
                    steps.append(dict(qt=qt, nk=(qt + 1) * P, lanes=lanes))
            return steps

        def second_steps():
            steps = []
            for qt in range(TT):
                for h2 in range(0, HEADS, 2):
                    lanes = [dict(q=mqT[:, hd, qt * P:(qt + 1) * P], k=mkT[:, hd, :], v=m_v[:, :, hd, :],
                                  o=aux[:, 1 + qt, hd * HD:(hd + 1) * HD], sums=m_sum[:, qt, hd:hd + 1])
                             for hd in (h2, h2 + 1)]
                    steps.append(dict(qt=qt, nk=(qt + 1) * P, lanes=lanes))
            return steps

        def lanes_of(bank):
            return bank.rearrange("p (a n) -> p a n", a=2)

        def arrival(i, unit):
            return i * 32 + 16 * (unit // RING + 1)

        block = ctx.enter_context(nc.Block())

        @block.sync
        def _(sp):
            def load(u, view, kc, n):
                s = u % RING
                if u >= RING:
                    sp.wait_ge(lo_ready, u - RING + 1)
                sp.dma_start(raw[:, s, 0:kc * n].rearrange("p (k n) -> p k n", k=kc), view).then_inc(w_loaded[s], 16)

            def ffn_loads(u0, up, down):
                def hidden(j, part):
                    return up[:, bass.ds(j * FB + part * D_FF, FB)].rearrange("(k p) n -> p k n", p=P)

                def load_at(u, first, view, kc, n):
                    s = first % RING
                    sp.wait_ge(lo_ready, u - RING + 1)
                    sp.dma_start(raw[:, s, 0:kc * n].rearrange("p (k n) -> p k n", k=kc), view).then_inc(w_loaded[s], 16)

                for part in range(2):
                    load(u0 + part, up[:, part * D_FF:part * D_FF + FB].rearrange("(k p) n -> p k n", p=P), KC8, FB)
                with sp.Fori(0, FSTEPS // 2) as i:
                    for s in range(2):
                        first = u0 + 2 + 3 * s
                        u = i * 6 + first
                        for part in range(2):
                            load_at(u + part, first + part, hidden(i * 2 + (1 + s), part), KC8, FB)
                        load_at(u + 2, first + 2,
                                down[bass.ds((i * 2 + s) * FB, FB), :].rearrange("(k p) n -> p k n", p=P), 2, DM)
                load(u0 + FUNITS - 1, down[(FSTEPS - 1) * FB:D_FF, :].rearrange("(k p) n -> p k n", p=P), 2, DM)

            starts = {u: (up, down) for u, up, down in ffn.values()}
            for u, unit in enumerate(units):
                if unit is not None:
                    load(u, *unit)
                elif u in starts:
                    ffn_loads(u, *starts[u])
            sp.wait_ge(h_ready, 5 * DEPTH * TT)
            sp.dma_start(out.rearrange("(t p) n -> p t n", p=P), h[:]).then_inc(out_done, 16)
            sp.wait_ge(out_done, 16)

        @block.gpsimd
        def _(pool):
            seen = Seen()
            pool.dma_start(h[:], A["x"].rearrange("(t p) n -> p t n", p=P)).then_inc(h_in, 16)
            for tile, name in ((ident, "c_ident"), (keep_le, "c_keep_le"), (causal, "c_causal"),
                               (chunk_le, "c_chunk_le"), (chunk_gt, "c_chunk_gt"), (chunk_of, "c_chunk_of"),
                               (cmp_mask, "c_cmp_mask"), (rope1_cols, "c_rope1"), (rope_c, "c_rope_c")):
                pool.dma_start(tile[:], A[name]).then_inc(consts_in, 16)
            pool.memset(half_neg[:], -0.5).then_inc(setup_done, 1)
            pool.memset(zero_row[:], 0.0).then_inc(setup_done, 1)
            for l in range(DEPTH):
                rows = [("pre_mix_g", 8), ("attn_out_g", 4), ("mlp_out_g", 4), ("pre_ffn_g", 8), ("ple_norm_g", 8),
                        ("cmp_pe", 32), ("cmp_b1", 4), ("gmlp_bs", 8), ("conv_b", 44)]
                at = 0
                if l:
                    pool.wait_ge(vt_ready, 4 * l)
                for name, n in rows:
                    pool.dma_start(vrow[at:at + n, 0, :], A["rows_" + name][l]).then_inc(vrows_in, 16)
                    at += n
                pool.dma_start(vrow[0:88, 1, :], A["rows_conv_w"][l, 0:88]).then_inc(vrows_in, 16)
                pool.dma_start(vrow[0:44, 2, :], A["rows_conv_w"][l, 88:132]).then_inc(vrows_in, 16)
                at = 0
                for name, n in (("norm_pre_mix_2", 8), ("norm_pre_ffn_2", 8), ("pool_scale_2", 4), ("gla_norm_2", 4),
                                ("mla_q_norm_2", 3), ("mla_kv_norm_2", 2)):
                    pool.dma_start(vrow[at:at + n, 3, :], A["rows_" + name][l]).then_inc(vrows_in, 16)
                    at += n

            def inverse_root(n, width, k):
                pool.wait_ge(sumsq_ready, seen(sumsq_ready, n))
                pool.tensor_scalar(rstd[:, 0:k], ssq[:, 0:k], 1.0 / width, EPS, ALU.mult, ALU.add)
                pool.drain()
                pool.tensor_tensor(rstd[:, 0:k], rstd[:, 0:k], half_neg[:, 0:k], ALU.pow).then_inc(rstd_ready, 1)

            def first_small(l):
                pool.dma_start(ws_raw, A["gmlp_ws"][l].rearrange("g t s -> t g s")).then_inc(small1_in, 16)
                for i, name in enumerate(("gmlp_ln_g", "gmlp_ln_b")):
                    pool.dma_start(ln_gb[:, i], A[name][l].partition_broadcast(P)).then_inc(small1_in, 16)
                pool.dma_start(cmp_w2, A["cmp_w2"][l].rearrange("k (c p) d -> p k c d", p=P)).then_inc(small1_in, 16)
                for kv in range(2):
                    for g in range(GROUPS):
                        pool.dma_start(cmp_b2[:, kv, g], A["cmp_b2"][l, kv].partition_broadcast(CMP_N)).then_inc(small1_in, 16)
                pool.dma_start(p_in, A["p"][l].rearrange("(t p) n -> p t n", p=P)).then_inc(small1_in, 16)

            def post_gains(a, b):
                pool.dma_start(post_g[:, 0], a.partition_broadcast(P)).then_inc(post_in, 16)
                pool.dma_start(post_g[:, 1], b.partition_broadcast(P)).then_inc(post_in, 16)

            pool.wait_ge(setup_done, 2)
            for l in range(DEPTH):
                if l:
                    pool.wait_ge(h_ready, 3 * TT * l)
                first_small(l)
                post_gains(A["post_mix_g"][l], A["post_ffn_g"][l])
                inverse_root(TT, DM, 2)
                pool.wait_ge(ln_var, seen(ln_var))
                pool.tensor_scalar(rstd[:, 4:6], mean_var[:, :, 1], 1.0, EPS, ALU.mult, ALU.add)
                pool.drain()
                pool.tensor_tensor(rstd[:, 4:6], rstd[:, 4:6], half_neg[:, 0:2], ALU.pow).then_inc(rstd_ready, 1)
                inverse_root(2 * TT, 512, 4)
                inverse_root(TT, DM, 2)
                inverse_root(TT, DM, 2)
                inverse_root(TT, DM, 2)
                inverse_root(TT, DM, 2)
            for l in range(DEPTH):
                pool.wait_ge(h_ready, (3 * DEPTH + 2 * l) * TT)
                if l == 0:
                    pool.dma_start(rt2[:, 0:1].bitcast(I32), A["positions_2"][0:P].rearrange("(p a) -> p a", a=1)).then_inc(pos_in, 16)
                    pool.dma_start(rt2[:, 1:2].bitcast(I32), A["positions_2"][P:SEQ].rearrange("(p a) -> p a", a=1)).then_inc(pos_in, 16)
                    pool.dma_start(rt2[:, 2:18], A["c_inv_freq"].partition_broadcast(P)).then_inc(pos_in, 16)
                post_gains(A["norm_post_mix_2"][l], A["norm_post_ffn_2"][l])
                pool.dma_start(b_gla[:], A["b_gla_a_2"][l].partition_broadcast(P)).then_inc(small2_in, 16)
                pool.dma_start(w_a2[:], A["w_gla_a2_2"][l]).then_inc(small2_in, 16)
                pool.dma_start(pool_mat, A["c_pool"]).then_inc(pool_in, 16)
                pool.dma_start(w_pool, A["w_pool_2"][l].rearrange("g c d -> c g d")).then_inc(pool_in, 16)
                inverse_root(TT, DM, 2)
                inverse_root(1, 128, 8)
                pool.wait_ge(sumsq_ready, seen(sumsq_ready, 2 * TT))
                pool.tensor_scalar(rstd[:, 0:2], ssq[:, 0:2], 1.0 / 384, EPS, ALU.mult, ALU.add)
                pool.tensor_scalar(rstd[:, 2:4], ssq[:, 2:4], 1.0 / 256, EPS, ALU.mult, ALU.add)
                pool.drain()
                pool.tensor_tensor(rstd[:, 0:4], rstd[:, 0:4], half_neg[:, 0:4], ALU.pow).then_inc(rstd_ready, 1)
                inverse_root(TT, DM, 2)
                inverse_root(TT, DM, 2)
                inverse_root(TT, DM, 2)

        @block.scalar
        def _(act):
            seen = Seen()
            st = {"split": 0, "unit": 0}

            def split(u):
                s = u % RING
                kc, n = (KC8, FB) if units[u] is None else units[u][1:]
                act.wait_ge(w_loaded[s], 16 * (u // RING + 1))
                if u >= RING:
                    act.wait_ge(unit_done, u - RING + 1)
                act.activation(whi[:, s, 0:kc * n], raw[:, s, 0:kc * n], ACT.Copy).then_inc(hi_ready, 1)

            def split_ahead(more=2):
                top = min(st["unit"] + more, len(units) - 1)
                for f in ffn_starts:
                    if st["split"] <= f + 2:
                        top = min(top, f + 1)
                while st["split"] <= top:
                    split(st["split"])
                    st["split"] += 1

            def sums_of_squares(src, width, at=0, junk=0):
                for t in range(TT):
                    dst = normed[:, t, junk:junk + width]
                    if src is None:
                        dst, row = dst.rearrange("p (a n) -> p a n", a=2), acc[:, t]
                    act.activation(dst, row if src is None else src(t), ACT.Square,
                                   accum_out=ssq[:, at + t:at + t + 1]).then_inc(sumsq_ready, 1)

            def x_high(nk, gain, at=0):
                for k in range(0, nk, 2):
                    act.wait_ge(tp_ready, seen(tp_ready))
                    bank = aux[:, (seen.now(tp_ready) - 1) % 2, :].rearrange("p (k s) -> p k s", k=2)
                    m = min(2, nk - k)
                    if gain is None:
                        last = act.activation(xhi[:, at + k:at + k + m, :], bank[:, 0:m], ACT.Copy)
                    else:
                        for j in range(m):
                            last = act.activation(xhi[:, at + k + j, :], bank[:, j], ACT.Copy, scale=gain(k + j))
                    last.then_inc(xhi_ready, 1)

            def next_block(n_units=2):
                st["unit"] += n_units
                split_ahead(1)
                act.wait_ge(unit_done, st["unit"])

            def residual_sums(n_blocks_units):
                for n in n_blocks_units:
                    st["unit"] += n
                    split_ahead(1)
                act.wait_ge(unit_done, st["unit"])
                sums_of_squares(None, DM)
                split_ahead()

            def ffn_steps(which, l):
                u0 = ffn[which, l][0]
                st["split"] = u0 + FUNITS
                gu0, cv0, fa0 = seen.now(gu_ready), seen.now(hc_conv), seen.now(fa_ready)
                cb, cw = (g_of["first", l, n] for n in ("conv_b", "conv_w")) if which == "first" else (0, 0)

                def split_at(i, first):
                    act.wait_ge(w_loaded[first % RING], arrival(i, first))
                    act.wait_ge(unit_done, i * 6 + (first - RING + 1))
                    act.activation(whi[:, first % RING], raw[:, first % RING], ACT.Copy).then_inc(hi_ready, 1)

                def hidden(j, par):
                    act.wait_ge(gu_ready, j + (gu0 + 1))
                    if which == "second":
                        act.activation(sg, aux[:, 2 * par].rearrange("p (c s) -> p c s", c=2), ACT.Silu).then_inc(sg_ready, 1)
                    else:
                        for w in range(2):
                            for c2 in range(2):
                                act.activation(hc[:, par, w, c2], aux[:, 2 * par + w, c2 * SEQ:(c2 + 1) * SEQ], ACT.Identity,
                                               scale=vecs[:, bass.ds(j * 2 + (cw + 88 + w * 22 + c2), 1)],
                                               bias=vecs[:, bass.ds(j * 2 + (cb + w * 22 + c2), 1)]).then_inc(hc_ready, 1)
                        act.wait_ge(hc_conv, j + (cv0 + 1))
                        act.activation(sg, hc[:, par, 0], ACT.Silu).then_inc(sg_ready, 1)
                    act.wait_ge(fa_ready, j + (fa0 + 1))
                    act.activation(fhi[:, par], f_act, ACT.Copy).then_inc(fhi_ready, 1)

                with act.Fori(0, FSTEPS // 2) as i:
                    for s in range(2):
                        first = u0 + 2 + 3 * s
                        split_at(i, first)
                        split_at(i, first + 1)
                        hidden(i * 2 + s, s)
                        split_at(i, first + 2)
                split(u0 + FUNITS - 1)
                hidden(FSTEPS - 1, (FSTEPS - 1) % 2)
                for sm in (gu_ready, hc_conv, fa_ready):
                    seen(sm, FSTEPS) if which == "first" or sm is not hc_conv else None
                st["unit"] = u0 + FUNITS
                act.wait_ge(unit_done, st["unit"])
                sums_of_squares(None, DM)
                split_ahead()

            def attention(steps, e, pt):
                b_max, b_pt, b_pv = seen.now(max_ready), seen.now(pt_ready), seen.now(pv_done)
                for i in range(len(steps) + 1):
                    if i < len(steps):
                        nk = steps[i]["nk"]
                        act.wait_ge(max_ready, b_max + i + 1)
                        if i >= 2:
                            act.wait_ge(pt_ready, b_pt + i - 1)
                        for a, lane in enumerate(steps[i]["lanes"]):
                            last = act.activation(e[:, i % 2, a * 256:a * 256 + nk], acc[:, 0, i % 2, a * 256:a * 256 + nk],
                                                  ACT.Exp, bias=nmax[:, i % 2, a:a + 1], accum_out=lane["sums"])
                        last.then_inc(e_ready, 1)
                    j = i - 1
                    if j >= 0 and j % 2 == 0:
                        nk = steps[j]["nk"]
                        act.wait_ge(pt_ready, b_pt + j + 1)
                        if j >= 2:
                            act.wait_ge(pv_done, b_pv + j - 1)
                        act.activation(pt(j % 2)[:, :, 0:nk], lanes_of(acc[:, 1, j % 2])[:, :, 0:nk], ACT.Copy).then_inc(pts_ready, 1)
                for sm in (max_ready, pt_ready, pv_done):
                    seen(sm, len(steps))

            for l in range(DEPTH):
                act.wait_ge(vt_ready, seen(vt_ready, 4))
                a, b = l * NVEC1, DEPTH * NVEC1 + l * NVEC2
                act.activation(vecs[:, a:a + NVEC1], aux[:, l, 0:NVEC1], ACT.Copy).then_inc(vecs_ready, 1)
                act.activation(vecs[:, b:b + NVEC2], aux[:, l, NVEC1:NVEC1 + NVEC2], ACT.Copy).then_inc(vecs_ready, 1)
            act.wait_ge(h_in, 16)
            act.wait_ge(vecs_ready, 2 * DEPTH)

            for l in range(DEPTH):
                key = lambda name: ("first", l, name)
                if l:
                    act.wait_ge(h_ready, seen(h_ready, TT))
                sums_of_squares(lambda t: h[:, t], DM)
                split_ahead()
                x_high(KC8, lambda k: vec(key("pre_mix"), k))
                for i, (c0, n) in enumerate(blocks_of(0, W1)):
                    next_block()
                    act.activation(z[:, :, c0:c0 + n], acc[:, :, i % 2, 0:n], ACT.Copy).then_inc(acc_out, 1)
                split_ahead()
                act.drain()
                for t in range(TT):
                    last = act.activation(zc2[:, t], z[:, t, 512:768].rearrange("p (u d) -> p u d", u=4).unsqueeze(2)
                                          .broadcast_to([P, 4, 2, HD]), ACT.Copy)
                last.then_inc(zc2_done, 1)
                act.activation(z[:, :, GATE1:U1], z[:, :, GATE1:U1], ACT.Tanh, scale=0.5).then_inc(gate_done, 1)
                act.activation(z[:, :, V1:W1], z[:, :, V1:W1], ACT.Gelu_apprx_tanh).then_inc(gelu_done, 1)
                for kv in range(2):
                    act.wait_ge(xc_sum, seen(xc_sum))
                    act.activation(x_cmp_split(xhi_flat, kv), x_cmp[:, kv].rearrange("p c g n -> p (c g n)"), ACT.Copy).then_inc(xc_hi, 1)
                for i in range(6):
                    act.wait_ge(qk_ready, seen(qk_ready))
                    t, which = i % 2, i // 2
                    src = aux[0:HD, 2 + i % 2, :].rearrange("p (h s) -> p h s", h=4)
                    dst = kT[:, :, t * P:(t + 1) * P] if which == 2 else qT[:, which * 4:which * 4 + 4, t * P:(t + 1) * P]
                    act.activation(dst, src, ACT.Copy, scale=1.0 if which == 2 else HD ** -0.5).then_inc(qk_out, 1)
                act.activation(z[:, :, U1:V1], z[:, :, U1:V1], ACT.Gelu_apprx_tanh).then_inc(gelu_done, 1)
                for kv in range(2):
                    next_block()
                for kv in range(2):
                    for c2 in range(2):
                        last = act.activation(hT[:, kv, c2], acc[:, c2, kv, 0:30], ACT.Gelu_apprx_tanh,
                                              bias=vec(key("cmp_b1"), kv * 2 + c2))
                last.then_inc(hT_out, 1)
                act.wait_ge(kcT_ready, seen(kcT_ready))
                act.activation(kcT, aux[0:HD, 3, 0:30].rearrange("p (g n) -> p g n", g=2), ACT.Copy).then_inc(kcT_out, 1)
                split_ahead()

                act.wait_ge(sc_shift, seen(sc_shift))
                act.activation(ec, ec, ACT.Exp).then_inc(sc_exp, 1)
                act.wait_ge(ect_ready, seen(ect_ready))
                for qt in range(TT):
                    last = act.activation(ecT[:, qt].rearrange("p (a h) q -> p a (h q)", a=2),
                                          acc[0:CMP_N, qt], ACT.Copy)
                last.then_inc(ect_out, 1)
                attention(first_steps(), e_buf, lambda b: lanes_of(pT[:, b]))
                act.wait_ge(mixed_ready, seen(mixed_ready))
                sums_of_squares(lambda t: attn[:, t], 512)
                sums_of_squares(lambda t: mlp[:, t], 512, at=2, junk=512)
                x_high(KC8, lambda k: vec(key("attn_out"), k) if k < 4 else vec(key("mlp_out"), k - 4))
                residual_sums([2, 2])
                act.wait_ge(h_ready, seen(h_ready, TT))
                sums_of_squares(lambda t: h[:, t], DM)
                split_ahead()
                x_high(KC8, lambda k: vec(key("pre_ffn"), k))
                ffn_steps("first", l)
                act.wait_ge(h_ready, seen(h_ready, TT))
                sums_of_squares(lambda t: h[:, t], DM)
                x_high(KC8, lambda k: vec(key("ple"), k))
                for nb in range(2):
                    next_block()
                    act.activation(ple_gate[:, :, nb * BLK:(nb + 1) * BLK], acc[:, :, nb, :], ACT.Sigmoid).then_inc(acc_out, 1)
                x_high(2, None)
                st["unit"] += 1
                split_ahead()

            act.wait_ge(ang_ready, 1)
            act.activation(rope2[:].rearrange("p a t f -> p (a t f)"), rt2[:, 128:192], ACT.Sin).then_inc(trig_done, 1)
            for l in range(DEPTH):
                key = lambda name: ("second", l, name)
                act.wait_ge(h_ready, seen(h_ready, TT))
                sums_of_squares(lambda t: h[:, t], DM)
                split_ahead()
                x_high(KC8, lambda k: vec(key("pre_mix"), k))
                for i, (c0, n) in enumerate(blocks_of(0, Z2)):
                    next_block()
                    act.activation(z[:, :, c0:c0 + n], acc[:, :, i % 2, 0:n], ACT.Copy).then_inc(acc_out, 1)
                for i in range(6):
                    next_block()
                    act.activation(gates[:, :, i // 2, (i % 2) * BLK:(i % 2 + 1) * BLK], acc[:, :, i % 2, :],
                                   ACT.Sigmoid).then_inc(acc_out, 1)
                split_ahead()
                act.wait_ge(diff_ready, seen(diff_ready))
                act.activation(diffT.rearrange("p g t -> p (g t)"), aux[:, 0:2, :].rearrange("p a n -> p (a n)"), ACT.Copy).then_inc(diff_out, 1)
                act.wait_ge(ypool_ready, seen(ypool_ready))
                for g in range(4):
                    last = act.activation(xhi[:, g], aux[:, 2 + g // 2, (g % 2) * SEQ:(g % 2 + 1) * SEQ], ACT.Copy,
                                          scale=vec(key("pool_scale"), g))
                last.then_inc(yp_hi, 1)
                for nb in range(2):
                    st["unit"] += 1
                split_ahead()
                act.wait_ge(a1_ready, seen(a1_ready))
                act.activation(a1T, aux[0:16, 0, 0:SEQ], ACT.Copy).then_inc(a1_out, 1)
                act.wait_ge(la_x, seen(la_x))
                act.activation(e_cum, la, ACT.Abs)
                act.drain()
                act.activation(e_cum, e_cum, ACT.Exp, scale=-1.0)
                act.drain()
                act.activation(e_cum, e_cum, ACT.Ln, bias=1.0).then_inc(la_ln, 1)
                act.wait_ge(cum_ready, seen(cum_ready))
                cum = aux[:, 0, :].rearrange("p (t n) -> p t n", t=TT)
                act.activation(e_cum, cum, ACT.Exp, scale=1.0 / 16)
                act.activation(e_inv, cum, ACT.Exp, scale=-1.0 / 16)
                act.activation(e_suf, aux[:, 1, :].rearrange("p (t n) -> p t n", t=TT), ACT.Exp, scale=1.0 / 16)
                act.activation(decay, aux[0:HD, 2, 0:16].rearrange("p (h n) -> p h n", h=4), ACT.Exp,
                               scale=1.0 / 16).then_inc(exps_ready, 1)
                for i in range(4):
                    act.wait_ge(gT_ready, seen(gT_ready))
                    dst = (qdT, kiT)[i // 2]
                    act.activation(dst[:, :, (i % 2) * P:(i % 2 + 1) * P],
                                   aux[0:HD, i, :].rearrange("p (h s) -> p h s", h=4), ACT.Copy).then_inc(gT_out, 1)
                act.activation(z[:, :, GR:GA], z[:, :, GR:GA], ACT.Silu).then_inc(og_silu, 1)
                act.wait_ge(og_ready, seen(og_ready))
                act.activation(sq_gla, acc[:, :, 1, :], ACT.Square).then_inc(sq_out, 1)
                x_high(4, lambda k: vec(key("gla_norm"), k))
                for nb in range(2):
                    st["unit"] += 1
                split_ahead()
                sums_of_squares(lambda t: z[:, t, CQ:CKV], 384)
                sums_of_squares(lambda t: z[:, t, CKV:KR], 256, at=2, junk=384)
                x_high(5, lambda k: vec(key("q_norm"), k) if k < 3 else vec(key("kv_norm"), k - 3))
                for nb in range(2):
                    next_block(1)
                    act.activation(qf[:, :, nb * 4:nb * 4 + 4, :], acc[:, :, nb, 0:384].rearrange("p t (h d) -> p t h d", h=4),
                                   ACT.Copy).then_inc(acc_out, 1)
                next_block(1)
                for nb in range(2):
                    src = acc[:, :, nb, :].rearrange("p t (h d) -> p t h d", h=4)
                    act.activation(kf[:, :, nb * 4:nb * 4 + 4, 0:64], src[:, :, :, 0:64], ACT.Copy)
                    act.activation(m_v[:, :, nb * 4:nb * 4 + 4, :], src[:, :, :, 64:128], ACT.Copy).then_inc(acc_out, 1)
                for i in range(8):
                    act.wait_ge(mT_ready, seen(mT_ready))
                    t, hg, which = i % 2, i // 2 % 2, i // 4
                    dst = (mqT, mkT)[which]
                    act.activation(dst[:, hg * 4:hg * 4 + 4, t * P:(t + 1) * P],
                                   aux[0:QK, i % 4, :].rearrange("p (h s) -> p h s", h=4), ACT.Copy,
                                   scale=QK ** -0.5 if which == 0 else 1.0).then_inc(mT_out, 1)
                split_ahead()
                attention(second_steps(), m_e, lambda b: lanes_of(m_pT[:, b]))
                x_high(4, None)
                for nb in range(2):
                    st["unit"] += 1
                split_ahead()
                x_high(KC8, None)
                residual_sums([2, 2])
                act.wait_ge(h_ready, seen(h_ready, TT))
                sums_of_squares(lambda t: h[:, t], DM)
                split_ahead()
                x_high(KC8, lambda k: vec(key("pre_ffn"), k))
                ffn_steps("second", l)

        @block.vector
        def _(dve):
            seen = Seen()
            st = {"split": 0, "unit": 0}

            def split(u):
                s = u % RING
                kc, n = (KC8, FB) if units[u] is None else units[u][1:]
                dve.wait_ge(hi_ready, u + 1)
                dve.tensor_tensor(wlo[:, s, 0:kc * n], raw[:, s, 0:kc * n], whi[:, s, 0:kc * n].bitcast(F32),
                                  ALU.subtract).then_inc(lo_ready, 1)

            def split_ahead(more=2):
                top = min(st["unit"] + more, len(units) - 1)
                for f in ffn_starts:
                    if st["split"] <= f + 2:
                        top = min(top, f + 1)
                while st["split"] <= top:
                    split(st["split"])
                    st["split"] += 1

            def normalize(src, width, at=0, to=0):
                for t in range(TT):
                    last = dve.tensor_scalar(normed[:, t, to:to + width], src(t), rstd[:, at + t:at + t + 1], None, ALU.mult)
                return last

            def x_low(nk, gain, at=0):
                for k in range(0, nk, 2):
                    dve.wait_ge(xhi_ready, seen(xhi_ready))
                    bank = aux[:, (seen.now(xhi_ready) - 1) % 2, :].rearrange("p (k s) -> p k s", k=2)
                    m = min(2, nk - k)
                    hi = xhi[:, at + k:at + k + m, :].bitcast(F32)
                    if gain is None:
                        last = dve.tensor_tensor(xlo[:, at + k:at + k + m, :], bank[:, 0:m], hi, ALU.subtract)
                    else:
                        for j in range(m):
                            last = dve.scalar_tensor_tensor(xlo[:, at + k + j, :], bank[:, j], gain(k + j), hi[:, j],
                                                            ALU.mult, ALU.subtract)
                    last.then_inc(x_split, 1)

            def residual(i):
                dve.wait_ge(rstd_ready, seen(rstd_ready))
                for t in range(TT):
                    dve.scalar_tensor_tensor(normed[:, t].rearrange("p (a n) -> p a n", a=2), acc[:, t], rstd[:, t:t + 1],
                                             post_g[:, i].rearrange("p (a n) -> p a n", a=2),
                                             ALU.mult, ALU.mult).then_inc(acc_out, 1)
                dve.drain()
                for t in range(TT):
                    dve.tensor_tensor(h[:, t], h[:, t], normed[:, t], ALU.add).then_inc(h_ready, 1)

            def ffn_steps(which, l):
                u0 = ffn[which, l][0]
                st["split"] = u0 + FUNITS
                hc0, sg0, fh0 = seen.now(hc_ready), seen.now(sg_ready), seen.now(fhi_ready)
                cw = g_of["first", l, "conv_w"]

                def split_at(i, first):
                    dve.wait_ge(hi_ready, i * 6 + (first + 1))
                    s = first % RING
                    dve.tensor_tensor(wlo[:, s], raw[:, s], whi[:, s].bitcast(F32), ALU.subtract).then_inc(lo_ready, 1)

                def hidden(j, par):
                    if which == "first":
                        dve.wait_ge(hc_ready, j * 4 + (hc0 + 4))
                        for back in (1, 2):
                            for w in range(2):
                                for c2 in range(2):
                                    tile = hc[:, par, w, c2, back:SEQ]
                                    tap = vecs[:, bass.ds(j * 2 + (cw + (2 - back) * 44 + w * 22 + c2), 1)]
                                    last = dve.scalar_tensor_tensor(
                                        tile, aux[:, 2 * par + w, c2 * SEQ:(c2 + 1) * SEQ - back], tap, tile,
                                        ALU.mult, ALU.add)
                            if back == 1:
                                dve.drain()
                        last.then_inc(hc_conv, 1)
                        up = hc[:, par, 1]
                    else:
                        up = aux[:, 2 * par + 1].rearrange("p (c s) -> p c s", c=2)
                        dve.drain()
                    dve.wait_ge(sg_ready, j + (sg0 + 1))
                    dve.tensor_tensor(f_act, up, sg, ALU.mult).then_inc(fa_ready, 1)
                    dve.wait_ge(fhi_ready, j + (fh0 + 1))
                    dve.tensor_tensor(flo[:, par], f_act, fhi[:, par].bitcast(F32), ALU.subtract).then_inc(f_split, 1)

                with dve.Fori(0, FSTEPS // 2) as i:
                    for s in range(2):
                        first = u0 + 2 + 3 * s
                        split_at(i, first)
                        split_at(i, first + 1)
                        hidden(i * 2 + s, s)
                        split_at(i, first + 2)
                split(u0 + FUNITS - 1)
                hidden(FSTEPS - 1, (FSTEPS - 1) % 2)
                if which == "first":
                    seen(hc_ready, 4 * FSTEPS)
                seen(sg_ready, FSTEPS), seen(fhi_ready, FSTEPS)
                st["unit"] = u0 + FUNITS
                split_ahead()

            def attention(steps, pt, after=None):
                b_s, b_pt, b_pv = seen.now(s_ready), seen.now(pt_ready), seen.now(pv_done)
                for i in range(len(steps) + 1):
                    if i < len(steps):
                        nk, qt = steps[i]["nk"], steps[i]["qt"]
                        dve.wait_ge(s_ready, b_s + i + 1)
                        lanes = lanes_of(acc[:, 0, i % 2])
                        dve.tensor_tensor(lanes[:, :, qt * P:nk], lanes[:, :, qt * P:nk],
                                          causal[:].unsqueeze(1).broadcast_to([P, 2, P]), ALU.add)
                        dve.drain()
                        dve.tensor_reduce(nmax[:, i % 2], lanes[:, :, 0:nk], AX.X, ALU.max, negate=True).then_inc(max_ready, 1)
                    j = i - 1
                    if j >= 0 and j % 2 == 1:
                        nk = steps[j]["nk"]
                        dve.wait_ge(pt_ready, b_pt + j + 1)
                        if j >= 2:
                            dve.wait_ge(pv_done, b_pv + j - 1)
                        dve.tensor_copy(pt(j % 2)[:, :, 0:nk], lanes_of(acc[:, 1, j % 2])[:, :, 0:nk]).then_inc(pts_ready_dve, 1)
                for sm in (s_ready, pt_ready, pv_done):
                    seen(sm, len(steps))
                dve.wait_ge(pv_done, seen.now(pv_done))

            def rotate(x1, x2, cos, sin, temps):
                a, b, c, d = temps
                dve.tensor_tensor(a, x1, cos, ALU.mult)
                dve.tensor_tensor(b, x2, sin, ALU.mult)
                dve.tensor_tensor(c, x2, cos, ALU.mult)
                dve.tensor_tensor(d, x1, sin, ALU.mult)
                dve.drain()
                dve.tensor_tensor(x1, a, b, ALU.subtract)
                return dve.tensor_tensor(x2, c, d, ALU.add)

            dve.wait_ge(consts_in, 9 * 16)
            dve.wait_ge(h_in, 16)
            dve.wait_ge(vecs_ready, 2 * DEPTH)
            for l in range(DEPTH):
                key = lambda name: ("first", l, name)
                dve.wait_ge(rstd_ready, seen(rstd_ready))
                normalize(lambda t: h[:, t], DM).then_inc(normed_ready, 1)
                split_ahead()
                x_low(KC8, lambda k: vec(key("pre_mix"), k))
                for nb in range(5):
                    st["unit"] += 2
                    split_ahead(1)
                split_ahead()
                dve.wait_ge(acc_out, seen(acc_out, 5))
                dve.wait_ge(zc2_done, seen(zc2_done))
                heads = z[:, :, 0:ROPE_UNITS * HD].rearrange("p t (u d) -> p t u d", d=HD)
                for t in range(TT):
                    rotate(heads[:, t, :, 0:8], heads[:, t, :, 8:16], rope1[:, t, 0], rope1[:, t, 1],
                           [rt[:, a, t] for a in range(4)]).then_inc(rope_done, 1)
                pe0 = g_of["first", l, "cmp_pe"]
                for kv in range(2):
                    dve.wait_ge(ct_ready, seen(ct_ready))
                    for odd in range(2):
                        rows = slice(odd * HD, (odd + 1) * HD)
                        for g in range(GROUPS):
                            src = aux[rows, kv, g * SEQ:(g + 1) * SEQ].rearrange("p (m c i) -> p i c m", c=8, i=2)[:, odd]
                            for back in range(2):
                                pe = vecs[rows, pe0 + kv * 16 + back * 8:pe0 + kv * 16 + back * 8 + 8]
                                last = dve.tensor_tensor(x_cmp[rows, kv, back * 8:back * 8 + 8, g, :],
                                                         src[:, :, back:back + CMP_N],
                                                         pe.unsqueeze(2).broadcast_to([HD, 8, CMP_N]), ALU.add)
                    last.then_inc(xc_sum, 1)
                for kv in range(2):
                    dve.wait_ge(xc_hi, seen(xc_hi))
                    dve.tensor_tensor(x_cmp_split(xlo_flat, kv), x_cmp[:, kv].rearrange("p c g n -> p (c g n)"),
                                      x_cmp_split(xhi_flat, kv).bitcast(F32), ALU.subtract).then_inc(xc_split, 1)
                for kv in range(2):
                    st["unit"] += 2
                    split_ahead(1)
                dve.wait_ge(ws_ready, seen(ws_ready))
                for a in range(2):
                    last = dve.tensor_tensor(wsT[:, a * 4:a * 4 + 4], aux[:, a, :].rearrange("p (g s) -> p g s", g=4),
                                             keep_le[:].unsqueeze(1).broadcast_to([P, 4, P]), ALU.mult)
                last.then_inc(ws_out, 1)
                dve.wait_ge(small1_in, 16 * 9 * (l + 1))
                dve.wait_ge(gelu_done, seen(gelu_done))
                for t in range(TT):
                    dve.bn_stats(stat[:, t], z[:, t, V1:W1])
                dve.drain()
                for t in range(TT):
                    last = dve.bn_aggr(mean_var[:, t], stat[:, t])
                last.then_inc(ln_var, 1)
                dve.wait_ge(rstd_ready, seen(rstd_ready))
                for t in range(TT):
                    dve.tensor_scalar(z[:, t, V1:W1], z[:, t, V1:W1], mean_var[:, t, 0:1], rstd[:, 4 + t:5 + t],
                                      ALU.subtract, ALU.mult)
                dve.drain()
                v = z[:, :, V1:W1]
                dve.tensor_tensor(v, v, ln_gb[:, 0].unsqueeze(1).broadcast_to([P, TT, 512]), ALU.mult)
                dve.drain()
                dve.tensor_tensor(v, v, ln_gb[:, 1].unsqueeze(1).broadcast_to([P, TT, 512]), ALU.add).then_inc(ln_done, 1)
                dve.wait_ge(gate_done, seen(gate_done))
                dve.tensor_scalar(z[:, :, GATE1:U1], z[:, :, GATE1:U1], 0.5, 0.5, ALU.mult, ALU.add)
                dve.wait_ge(kcv_ready, seen(kcv_ready))
                dve.tensor_tensor(kcv, aux[0:CMP_N, 2, 0:256].rearrange("p (k g d) -> p k g d", k=2, g=GROUPS), cmp_b2, ALU.add)
                dve.drain()
                rotate(kcv[:, 0, :, 0:8], kcv[:, 0, :, 8:16], rope_c[:, 0], rope_c[:, 1],
                       [rt_c[:, a] for a in range(4)]).then_inc(kcv_out, 1)
                dve.wait_ge(mix_ready, seen(mix_ready))
                dve.wait_ge(gelu_done, seen(gelu_done))
                for g in range(8):
                    last = dve.scalar_tensor_tensor(
                        mlp[:, :, g * HD:(g + 1) * HD],
                        aux[:, g // 4, (g % 4) * P:(g % 4 + 1) * P].rearrange("p (t d) -> p t d", t=TT),
                        vec(key("gmlp_bs"), g), z[:, :, U1 + g * HD:U1 + (g + 1) * HD], ALU.add, ALU.mult)
                last.then_inc(gmlp_out, 1)
                dve.wait_ge(sc_ready, seen(sc_ready))
                for t in range(TT):
                    dve.tensor_tensor(ec[:, t], aux[:, 2, t * 120:(t + 1) * 120].rearrange("p (h n) -> p h n", h=HEADS),
                                      cmp_mask[:, 0, t].unsqueeze(1).broadcast_to([P, HEADS, CMP_N]), ALU.add)
                dve.drain()
                dve.tensor_reduce(cmax[:], ec, AX.X, ALU.max)
                dve.drain()
                dve.tensor_tensor(ec, ec, cmax[:].unsqueeze(3).broadcast_to([P, TT, HEADS, CMP_N]), ALU.subtract).then_inc(sc_shift, 1)
                dve.wait_ge(sc_exp, seen(sc_exp))
                for t in range(TT):
                    dve.tensor_tensor(ec[:, t], ec[:, t], cmp_mask[:, 1, t].unsqueeze(1).broadcast_to([P, HEADS, CMP_N]), ALU.mult)
                dve.drain()
                dve.tensor_reduce(esum[:, :, :, 0], ec, AX.X, ALU.add).then_inc(ec_ready, 1)
                dve.drain()
                gate = z[:, :, GATE1:U1].rearrange("p t (h b) -> p t h b", b=3)

                def gate_factor(b0, b1):
                    s, f = esum[:, :, :, b0:b1], factor[:, :, :, b0:b1]
                    dve.tensor_scalar(s, s, 1e-30, None, ALU.max)
                    dve.drain()
                    dve.reciprocal(f, s)
                    dve.drain()
                    dve.tensor_tensor(f, f, gate[:, :, :, b0:b1], ALU.mult)
                    dve.drain()

                def heads_of(ap):
                    return ap.rearrange("p (h d) -> p h d", d=HD)

                def factor_of(t, b):
                    return factor[:, t, :, b:b + 1].broadcast_to([P, HEADS, HD])

                gate_factor(0, 1)
                dve.wait_ge(cpv_done, seen(cpv_done))
                for t in range(TT):
                    last = dve.tensor_tensor(heads_of(attn[:, t]), heads_of(aux[:, 3 - t]), factor_of(t, 0), ALU.mult)
                last.then_inc(cmp_out, 1)
                attention(first_steps(), lambda b: lanes_of(pT[:, b]))
                gate_factor(1, 3)
                for t in range(TT):
                    for b in range(2):
                        o = heads_of(aux[:, (1 + b, (3, 0)[b])[t]])
                        dve.tensor_tensor(heads_of(part[:, b]), o, factor_of(t, 1 + b), ALU.mult)
                    dve.drain()
                    dve.tensor_tensor(attn[:, t], attn[:, t], part[:, 0], ALU.add)
                    dve.drain()
                    last = dve.tensor_tensor(attn[:, t], attn[:, t], part[:, 1], ALU.add)
                    if t == 0:
                        dve.drain()
                last.then_inc(mixed_ready, 1)
                split_ahead()
                dve.wait_ge(rstd_ready, seen(rstd_ready))
                normalize(lambda t: attn[:, t], 512)
                normalize(lambda t: mlp[:, t], 512, at=2, to=512).then_inc(normed_ready, 1)
                x_low(KC8, lambda k: vec(key("attn_out"), k) if k < 4 else vec(key("mlp_out"), k - 4))
                for nb in range(2):
                    st["unit"] += 2
                    split_ahead(1)
                dve.wait_ge(post_in, 32 * (l + 1))
                residual(0)
                split_ahead()
                dve.wait_ge(rstd_ready, seen(rstd_ready))
                normalize(lambda t: h[:, t], DM).then_inc(normed_ready, 1)
                x_low(KC8, lambda k: vec(key("pre_ffn"), k))
                ffn_steps("first", l)
                residual(1)
                dve.wait_ge(rstd_ready, seen(rstd_ready))
                normalize(lambda t: h[:, t], DM).then_inc(normed_ready, 1)
                x_low(KC8, lambda k: vec(key("ple"), k))
                for nb in range(2):
                    st["unit"] += 2
                    split_ahead(1)
                x_low(2, None)
                st["unit"] += 1
                for nb in range(2):
                    if nb:
                        split_ahead(1)
                    dve.wait_ge(unit_done, st["unit"] if nb else st["unit"])
                    cols = slice(nb * BLK, (nb + 1) * BLK)
                    dve.tensor_tensor(normed[:, :, cols], acc[:, :, nb, :], ple_gate[:, :, cols], ALU.mult).then_inc(acc_out, 1)
                dve.drain()
                for t in range(TT):
                    dve.tensor_tensor(h[:, t], h[:, t], normed[:, t], ALU.add).then_inc(h_ready, 1)
                seen(acc_out, 2 + TT * 2 + 2)
                split_ahead()

            dve.wait_ge(pos_in, 48)
            C1 = 6.28125
            C2 = 0.0019353071693331003
            C3 = 1.0253404e-11
            pos, ang, arg, turns = rt2[:, 20:22], rt2[:, 64:128], rt2[:, 128:192], rt2[:, 192:256]
            dve.tensor_copy(pos, rt2[:, 0:2].bitcast(I32))
            dve.drain()
            for a in range(2):
                for t in range(TT):
                    dve.tensor_scalar(ang[:, a * 32 + t * 16:a * 32 + t * 16 + 16], rt2[:, 2:18], pos[:, t:t + 1], None, ALU.mult)
            dve.drain()
            dve.tensor_scalar(turns[:, 0:32], ang[:, 0:32], 0.15915494309189535, 0.25, ALU.mult, ALU.add)
            dve.tensor_scalar(turns[:, 32:64], ang[:, 32:64], 0.15915494309189535, None, ALU.mult)
            dve.drain()
            dve.tensor_scalar(turns, turns, 12582912.0, None, ALU.add)
            dve.drain()
            dve.tensor_scalar(turns, turns, 12582912.0, None, ALU.subtract)
            dve.drain()
            dve.scalar_tensor_tensor(arg, turns, -C1, ang, ALU.mult, ALU.add)
            dve.drain()
            dve.scalar_tensor_tensor(arg, turns, -C2, arg, ALU.mult, ALU.add)
            dve.drain()
            dve.scalar_tensor_tensor(arg, turns, -C3, arg, ALU.mult, ALU.add)
            dve.drain()
            dve.tensor_scalar(arg[:, 0:32], arg[:, 0:32], 1.5707963267948966, None, ALU.add)
            dve.drain()
            dve.tensor_scalar(arg, arg, 3.1415925, -3.1415925, ALU.min, ALU.max).then_inc(ang_ready, 1)
            dve.wait_ge(trig_done, 1)

            for l in range(DEPTH):
                key = lambda name: ("second", l, name)

                def gated(nb, b, first):
                    st["unit"] += 1
                    split_ahead(1)
                    dve.wait_ge(unit_done, st["unit"])
                    cols = slice(nb * BLK, (nb + 1) * BLK)
                    if first:
                        dve.tensor_tensor(merged[:, :, cols], acc[:, :, nb, :], gates[:, :, b, cols], ALU.mult).then_inc(acc_out, 1)
                    else:
                        tmp = sq_gla
                        dve.tensor_tensor(tmp, acc[:, :, nb, :], gates[:, :, b, cols], ALU.mult).then_inc(acc_out, 1)
                        dve.drain()
                        dve.tensor_tensor(merged[:, :, cols], merged[:, :, cols], tmp, ALU.add)
                        dve.drain()

                dve.wait_ge(rstd_ready, seen(rstd_ready))
                normalize(lambda t: h[:, t], DM).then_inc(normed_ready, 1)
                split_ahead()
                x_low(KC8, lambda k: vec(key("pre_mix"), k))
                for nb in range(12):
                    st["unit"] += 2
                    split_ahead(1)
                split_ahead()
                dve.wait_ge(acc_out, seen(acc_out, 12))
                dve.wait_ge(yp_hi, seen(yp_hi))
                for g in range(4):
                    last = dve.scalar_tensor_tensor(xlo[:, g], aux[:, 2 + g // 2, (g % 2) * SEQ:(g % 2 + 1) * SEQ],
                                                    vec(key("pool_scale"), g), xhi[:, g].bitcast(F32), ALU.mult, ALU.subtract)
                last.then_inc(yp_split, 1)
                for nb in range(2):
                    gated(nb, 0, True)
                split_ahead()
                dve.wait_ge(la_pre, seen(la_pre))
                dve.tensor_tensor(la, aux[:, 1, :].rearrange("p (t n) -> p t n", t=TT),
                                  b_gla[:].unsqueeze(1).broadcast_to([P, TT, 256]), ALU.add).then_inc(la_x, 1)
                dve.wait_ge(la_ln, seen(la_ln))
                dve.scalar_tensor_tensor(la, la, 0.0, e_cum, ALU.min, ALU.subtract).then_inc(la_ready, 1)
                dve.memset(attM.rearrange("p t h s -> p (t h s)"), 0.0)
                dve.wait_ge(exps_ready, seen(exps_ready))
                q, k = z[:, :, GQ:GK], z[:, :, GK:GV]
                dve.scalar_tensor_tensor(q, q, 64 ** -0.5, e_cum, ALU.mult, ALU.mult)
                dve.tensor_tensor(e_inv, k, e_inv, ALU.mult)
                dve.tensor_tensor(e_suf, k, e_suf, ALU.mult).then_inc(qk_dec, 1)
                dve.wait_ge(att_ready, seen(att_ready))
                for t in range(TT):
                    last = dve.copy_predicated(attM[:, t], chunk_le[:].bitcast(I32).unsqueeze(1).broadcast_to([P, 4, P]),
                                               acc[:, t, 0].rearrange("p (h s) -> p h s", h=4))
                last.then_inc(att_out, 1)
                dve.wait_ge(kv_ready, seen(kv_ready))
                kv = [aux[0:HD, n, :].rearrange("p (h e) -> p h e", h=4) for n in range(3)]
                dve.tensor_copy(state[:, 0], kv[0])
                dve.drain()
                for n in (1, 2):
                    for hd in range(4):
                        last = dve.scalar_tensor_tensor(state[:, n, hd], state[:, n - 1, hd], decay[:, hd, n:n + 1],
                                                        kv[n][:, hd], ALU.mult, ALU.add)
                    if n == 1:
                        dve.drain()
                last.then_inc(states_ready, 1)
                dve.wait_ge(sq_out, seen(sq_out))
                dve.tensor_reduce(ssq[:, 0:8], sq_gla.rearrange("p t (h e) -> p (t h) e", h=4), AX.X, ALU.add).then_inc(sumsq_ready, 1)
                dve.wait_ge(rstd_ready, seen(rstd_ready))
                for t in range(TT):
                    dve.tensor_tensor(o_gla[:, t].rearrange("p (h e) -> p h e", h=4), acc[:, t, 1].rearrange("p (h e) -> p h e", h=4),
                                      rstd[:, t * 4:t * 4 + 4].unsqueeze(2).broadcast_to([P, 4, P]), ALU.mult)
                dve.drain()
                dve.wait_ge(og_silu, seen(og_silu))
                dve.tensor_tensor(normed[:, :, 0:512], o_gla, z[:, :, GR:GA], ALU.mult).then_inc(normed_ready, 1)
                x_low(4, lambda k: vec(key("gla_norm"), k))
                for nb in range(2):
                    gated(nb, 1, False)
                split_ahead()
                dve.wait_ge(rstd_ready, seen(rstd_ready))
                normalize(lambda t: z[:, t, CQ:CKV], 384)
                normalize(lambda t: z[:, t, CKV:KR], 256, at=2, to=384).then_inc(normed_ready, 1)
                x_low(5, lambda k: vec(key("q_norm"), k) if k < 3 else vec(key("kv_norm"), k - 3))
                nflat = normed[:].rearrange("p t n -> p (t n)")
                kr = z[:, :, KR:Z2]
                small = [nflat[:, 1024 + a * 32:1056 + a * 32].rearrange("p (t f) -> p t f", t=TT) for a in range(4)]
                rotate(kr[:, :, 0:16], kr[:, :, 16:32], rope2[:, 0], rope2[:, 1], small)
                dve.drain()
                for nb in range(2):
                    st["unit"] += 1
                    split_ahead(1)
                st["unit"] += 1
                split_ahead(1)
                dve.wait_ge(acc_out, seen(acc_out, 2 + 2 + 4))
                big = [nflat[:, a * 256:(a + 1) * 256].rearrange("p (t h f) -> p t h f", t=TT, h=HEADS) for a in range(4)]
                cos, sin = (rope2[:, a].unsqueeze(2).broadcast_to([P, TT, HEADS, 16]) for a in range(2))
                rotate(qf[:, :, :, 64:80], qf[:, :, :, 80:96], cos, sin, big)
                dve.tensor_copy(kf[:, :, :, 64:96], kr.unsqueeze(2).broadcast_to([P, TT, HEADS, 32])).then_inc(mrope_done, 1)
                split_ahead()
                attention(second_steps(), lambda b: lanes_of(m_pT[:, b]))
                dve.reciprocal(m_sum[:], m_sum[:])
                dve.drain()
                for t in range(TT):
                    last = dve.tensor_tensor(normed[:, t, 512:1024].rearrange("p (h d) -> p h d", d=HD),
                                             aux[:, 1 + t].rearrange("p (h d) -> p h d", d=HD),
                                             m_sum[:, t].unsqueeze(2).broadcast_to([P, HEADS, HD]), ALU.mult)
                last.then_inc(normed_ready, 1)
                x_low(4, None)
                for nb in range(2):
                    gated(nb, 2, False)
                dve.drain().then_inc(normed_ready, 1)
                split_ahead()
                x_low(KC8, None)
                for nb in range(2):
                    st["unit"] += 2
                    split_ahead(1)
                dve.wait_ge(post_in, 32 * (DEPTH + l + 1))
                residual(0)
                split_ahead()
                dve.wait_ge(rstd_ready, seen(rstd_ready))
                normalize(lambda t: h[:, t], DM).then_inc(normed_ready, 1)
                x_low(KC8, lambda k: vec(key("pre_ffn"), k))
                ffn_steps("second", l)
                residual(1)
                seen(acc_out, 2 + TT * 2)

        @block.tensor
        def _(pe):
            seen = Seen()
            st = {"unit": 0}
            out_n = {"n": 0}

            def weights(u):
                return whi[:, u % RING], wlo[:, u % RING]

            def three(o, xs, ws, start, stop, x_stationary=True, **kw):
                (xh, xl), (wh, wl) = xs, ws
                for n, (x, w) in enumerate(((xh, wh), (xh, wl), (xl, wh)) if x_stationary else ((xh, wh), (xl, wh), (xh, wl))):
                    a, b = (x, w) if x_stationary else (w, x)
                    last = pe.matmul(o, a, b, start=start and n == 0, stop=stop and n == 2, **kw)
                return last

            def project(blocks, at=0, pairs=None):
                base = out_n["n"]
                pe.wait_ge(acc_out, base) if base else None
                for i, unit_cols in enumerate(blocks):
                    if i >= 2:
                        pe.wait_ge(acc_out, base + i - 1)
                    nks = sum(kc for kc, n in unit_cols)
                    k = 0
                    for kc, n in unit_cols:
                        u = st["unit"]
                        pe.wait_ge(lo_ready, u + 1)
                        wh, wl = weights(u)
                        for c in range(kc):
                            if i == 0 and pairs and (k + c) % 2 == 0:
                                pe.wait_ge(pairs, seen(pairs))
                            for t in range(TT):
                                rows = slice(t * P, (t + 1) * P)
                                last = three(acc[:, t, i % 2, 0:n], (xhi[:, at + k + c, rows], xlo[:, at + k + c, rows]),
                                             (wh[:, c * n:(c + 1) * n], wl[:, c * n:(c + 1) * n]),
                                             k + c == 0, k + c == nks - 1, skip_group_check=True)
                        last.then_inc(unit_done, 1)
                        st["unit"] += 1
                        k += kc
                out_n["n"] += len(blocks)

            def two_blocks_unit(at, pairs, first_chunk_pairs=True):
                pe.wait_ge(acc_out, out_n["n"])
                u = st["unit"]
                pe.wait_ge(lo_ready, u + 1)
                wh, wl = weights(u)
                if pairs:
                    pe.wait_ge(pairs, seen(pairs))
                for nb in range(2):
                    for c in range(2):
                        cols = slice(c * DM + nb * BLK, c * DM + (nb + 1) * BLK)
                        for t in range(TT):
                            rows = slice(t * P, (t + 1) * P)
                            last = three(acc[:, t, nb, :], (xhi[:, at + c, rows], xlo[:, at + c, rows]),
                                         (wh[:, cols], wl[:, cols]), c == 0, c == 1, skip_group_check=True)
                last.then_inc(unit_done, 1)
                st["unit"] += 1
                out_n["n"] += 2

            def turn(src, nk, at=0):
                for k in range(0, nk, 2):
                    n = turned["n"]
                    if n >= 2:
                        pe.wait_ge(x_split, n - 1)
                    for j in range(min(2, nk - k)):
                        for t in range(TT):
                            c0 = at + (k + j) * P
                            last = pe.transpose(aux[:, n % 2, j * SEQ + t * P:j * SEQ + (t + 1) * P],
                                                src[:, t, c0:c0 + P], ident[:])
                    last.then_inc(tp_ready, 1)
                    turned["n"] += 1

            turned = {"n": 0}

            def full(nblocks, nunits_kc=4):
                return [[(4, BLK), (4, BLK)] for _ in range(nblocks)]

            def ffn_steps(which, l):
                u0 = ffn[which, l][0]
                fs0 = seen.now(f_split)
                pe.wait_ge(acc_out, out_n["n"])

                def up(j_unit, u, par):
                    for part in range(2):
                        pe.wait_ge(lo_ready, j_unit + (part + 1))
                        wh, wl = weights(u + part)
                        for c2 in range(2):
                            for k in range(KC8):
                                cols = slice(k * FB + c2 * P, k * FB + (c2 + 1) * P)
                                for n, (w, x) in enumerate(((wh, xhi), (wh, xlo), (wl, xhi))):
                                    last = pe.matmul(aux[:, 2 * par + part, c2 * SEQ:(c2 + 1) * SEQ], w[:, cols], x[:, k],
                                                     start=(k == 0 and n == 0), stop=(k == KC8 - 1 and n == 2),
                                                     skip_group_check=True)
                        last.then_inc(unit_done if part == 0 else gu_ready, 1)

                def down(j, j_unit, u, par, announce, stop=False):
                    pe.wait_ge(lo_ready, j_unit + 1)
                    pe.wait_ge(f_split, j + (fs0 + 1))
                    wh, wl = weights(u)
                    for c2 in range(2):
                        for t in range(TT):
                            rows = slice(t * P, (t + 1) * P)
                            for n, (x, w) in enumerate(((fhi, wh), (fhi, wl), (flo, wh))):
                                for nb in range(2):
                                    cols = slice(c2 * DM + nb * BLK, c2 * DM + (nb + 1) * BLK)
                                    last = pe.matmul(acc[:, t, nb, :], x[:, par, c2, rows], w[:, cols], start=False,
                                                     stop=stop and c2 == 1 and n == 2, skip_group_check=True)
                                    if announce and c2 == 0 and t == 0 and n == 0 and nb == 0:
                                        last.then_inc(unit_done, 1)
                    last.then_inc(unit_done, 1)

                for p in range(KC8 // 2):
                    pe.wait_ge(x_split, seen(x_split))
                up(u0, u0, 0)
                for t in range(TT):
                    for nb in range(2):
                        last = pe.matmul(acc[:, t, nb, :], zero_row[:, 0:P], zero_row[:], start=True, stop=False,
                                         skip_group_check=True)
                last.then_inc(unit_done, 1)
                with pe.Fori(0, FSTEPS // 2) as i:
                    for s in range(2):
                        first = u0 + 2 + 3 * s
                        up(i * 6 + first, first, (1 + s) % 2)
                        down(i * 2 + s, i * 6 + (first + 2), first + 2, s, True)
                down(FSTEPS - 1, u0 + FUNITS - 1, u0 + FUNITS - 1, (FSTEPS - 1) % 2, False, True)
                seen(f_split, FSTEPS)
                st["unit"] = u0 + FUNITS
                out_n["n"] += 2

            def attention(steps, e, pt):
                b_e, b_pts, b_dve = seen.now(e_ready), seen.now(pts_ready), seen.now(pts_ready_dve)
                n = len(steps)
                for i in range(n + 2):
                    if i < n:
                        if i >= 2:
                            pe.wait_ge(e_ready, b_e + i - 1)
                        nk = steps[i]["nk"]
                        for a, lane in enumerate(steps[i]["lanes"]):
                            last = pe.matmul(acc[:, 0, i % 2, a * 256:a * 256 + nk], lane["q"], lane["k"][:, 0:nk],
                                             start=True, stop=True)
                        last.then_inc(s_ready, 1)
                    j = i - 1
                    if 0 <= j < n:
                        pe.wait_ge(e_ready, b_e + j + 1)
                        for a in range(2):
                            for kt in range(steps[j]["nk"] // P):
                                c0 = a * 256 + kt * P
                                last = pe.transpose(acc[:, 1, j % 2, c0:c0 + P], e[:, j % 2, c0:c0 + P], ident[:])
                        last.then_inc(pt_ready, 1)
                    j = i - 2
                    if 0 <= j < n:
                        if j % 2 == 0:
                            pe.wait_ge(pts_ready, b_pts + j // 2 + 1)
                        else:
                            pe.wait_ge(pts_ready_dve, b_dve + j // 2 + 1)
                        nkt = steps[j]["nk"] // P
                        for a, lane in enumerate(steps[j]["lanes"]):
                            for kt in range(nkt):
                                last = pe.matmul(lane["o"], pt(j % 2)[:, a, kt * P:(kt + 1) * P], lane["v"][:, kt],
                                                 start=(kt == 0), stop=(kt == nkt - 1))
                        last.then_inc(pv_done, 1)
                seen(e_ready, n), seen(pts_ready, n // 2), seen(pts_ready_dve, n // 2)

            pe.wait_ge(consts_in, 9 * 16)
            pe.wait_ge(setup_done, 2)
            for l in range(DEPTH):
                pe.wait_ge(vrows_in, 16 * 17 * (l + 1))
                for i, (n, c0) in enumerate(((120, 0), (88, 120), (44, 208), (29, 252))):
                    pe.transpose(aux[:, l, c0:c0 + n], vrow[0:n, i, :], ident[0:n, 0:n]).then_inc(vt_ready, 1)
            pe.wait_ge(vecs_ready, 2 * DEPTH)

            for l in range(DEPTH):
                pe.wait_ge(normed_ready, seen(normed_ready))
                turn(normed, KC8)
                project([[(4, n), (4, n)] for c0, n in blocks_of(0, W1)], pairs=x_split)
                pe.wait_ge(acc_out, out_n["n"])
                pe.wait_ge(zc2_done, seen(zc2_done))
                for kv in range(2):
                    for g in range(GROUPS):
                        for t in range(TT):
                            last = pe.transpose(aux[:, kv, g * SEQ + t * P:g * SEQ + (t + 1) * P],
                                                zc2[:, t, kv * 2 + g].rearrange("p a d -> p (a d)"), ident[:])
                    last.then_inc(ct_ready, 1)
                pe.wait_ge(rope_done, seen(rope_done, TT))
                for i in range(6):
                    if i >= 2:
                        pe.wait_ge(qk_out, seen(qk_out))
                    t, which = i % 2, i // 2
                    for j in range(4):
                        c0 = (which * 4 + j) * HD if which < 2 else 768 + (j // 2) * 256 + (j % 2) * HD
                        last = pe.transpose(aux[0:HD, 2 + i % 2, j * P:(j + 1) * P], z[:, t, c0:c0 + HD], ident[:])
                    last.then_inc(qk_ready, 1)
                for kv in range(2):
                    pe.wait_ge(xc_split, seen(xc_split))
                    for half in range(2):
                        u = st["unit"]
                        pe.wait_ge(lo_ready, u + 1)
                        wh, wl = weights(u)
                        xs = [x_cmp_split(f, kv).rearrange("p (c r) -> p c r", c=16) for f in (xhi_flat, xlo_flat)]
                        for c in range(8):
                            for c2 in range(2):
                                cols = slice(c * CMP_HID + c2 * P, c * CMP_HID + (c2 + 1) * P)
                                last = three(acc[:, c2, kv, 0:30], (xs[0][:, half * 8 + c], xs[1][:, half * 8 + c]),
                                             (wh[:, cols], wl[:, cols]), half + c == 0, half == 1 and c == 7,
                                             x_stationary=False, skip_group_check=True)
                        last.then_inc(unit_done, 1)
                        st["unit"] += 1
                pe.wait_ge(small1_in, 16 * 9 * (l + 1))
                for g in range(8):
                    last = pe.transpose(aux[:, g // 4, (g % 4) * P:(g % 4 + 1) * P], ws_raw[:, g, :], ident[:])
                last.then_inc(ws_ready, 1)
                pe.wait_ge(hT_out, seen(hT_out))
                pe.wait_ge(qk_out, seen(qk_out, 2))
                for kv in range(2):
                    for g in range(GROUPS):
                        for c2 in range(2):
                            last = pe.matmul(aux[0:CMP_N, 2, (kv * 2 + g) * HD:(kv * 2 + g + 1) * HD],
                                             hT[:, kv, c2, g * CMP_N:(g + 1) * CMP_N], cmp_w2[:, kv, c2, :],
                                             start=(c2 == 0), stop=(c2 == 1))
                last.then_inc(kcv_ready, 1)
                pe.wait_ge(ws_out, seen(ws_out))
                pe.wait_ge(ln_done, seen(ln_done))
                for g in range(8):
                    last = pe.matmul(aux[:, g // 4, (g % 4) * P:(g % 4 + 1) * P], wsT[:, g, :],
                                     z[:, :, V1 + g * HD:V1 + (g + 1) * HD], start=True, stop=True)
                last.then_inc(mix_ready, 1)
                pe.wait_ge(kcv_out, seen(kcv_out))
                for g in range(GROUPS):
                    last = pe.transpose(aux[0:HD, 3, g * CMP_N:(g + 1) * CMP_N], kcv[:, 0, g, :], ident[0:CMP_N, 0:CMP_N])
                last.then_inc(kcT_ready, 1)
                pe.wait_ge(kcT_out, seen(kcT_out))
                for t in range(TT):
                    for hd in range(HEADS):
                        c0 = (t * HEADS + hd) * CMP_N
                        last = pe.matmul(aux[:, 2, c0:c0 + CMP_N], qT[:, hd, t * P:(t + 1) * P], kcT[:, hd // 4, :],
                                         start=True, stop=True)
                last.then_inc(sc_ready, 1)
                pe.wait_ge(ec_ready, seen(ec_ready))
                for t in range(TT):
                    for hd in range(HEADS):
                        last = pe.transpose(acc[0:CMP_N, t, hd // 4, (hd % 4) * P:(hd % 4 + 1) * P], ec[:, t, hd, :], ident[:])
                last.then_inc(ect_ready, 1)
                pe.wait_ge(ect_out, seen(ect_out))
                for t in range(TT):
                    for hd in range(HEADS):
                        last = pe.matmul(aux[:, 3 - t, hd * HD:(hd + 1) * HD], ecT[:, t, hd, :], kcv[:, 1, hd // 4, :],
                                         start=True, stop=True)
                last.then_inc(cpv_done, 1)
                pe.wait_ge(cmp_out, seen(cmp_out))
                pe.wait_ge(gmlp_out, seen(gmlp_out))
                attention(first_steps(), e_buf, lambda b: lanes_of(pT[:, b]))
                pe.wait_ge(normed_ready, seen(normed_ready))
                turn(normed, KC8)
                project(full(2), pairs=x_split)
                pe.wait_ge(normed_ready, seen(normed_ready))
                turn(normed, KC8)
                ffn_steps("first", l)
                pe.wait_ge(normed_ready, seen(normed_ready))
                turn(normed, KC8)
                project(full(2), pairs=x_split)
                turn(p_in, 2)
                two_blocks_unit(0, x_split)

            for l in range(DEPTH):
                pe.wait_ge(normed_ready, seen(normed_ready))
                turn(normed, KC8)
                project([[(4, n), (4, n)] for c0, n in blocks_of(0, Z2) + blocks_of(Z2, W2)], pairs=x_split)
                pe.wait_ge(acc_out, out_n["n"])
                pe.wait_ge(pool_in, 32 * (l + 1))
                for g in range(4):
                    for s in range(TT):
                        last = pe.matmul(aux[:, g // 2, (g % 2) * SEQ:(g % 2 + 1) * SEQ], z[:, s, g * P:(g + 1) * P],
                                         pool_mat[:, s, g, :], start=(s == 0), stop=(s == 1))
                last.then_inc(diff_ready, 1)
                pe.wait_ge(diff_out, seen(diff_out))
                for g in range(4):
                    last = pe.matmul(aux[:, 2 + g // 2, (g % 2) * SEQ:(g % 2 + 1) * SEQ], w_pool[:, g, :], diffT[:, g, :],
                                     start=True, stop=True)
                last.then_inc(ypool_ready, 1)
                pe.wait_ge(yp_split, seen(yp_split))
                project([[(4, BLK)], [(4, BLK)]])
                for t in range(TT):
                    last = pe.transpose(aux[0:16, 0, t * P:(t + 1) * P], z[:, t, GA:CQ], ident[:])
                last.then_inc(a1_ready, 1)
                pe.wait_ge(a1_out, seen(a1_out))
                pe.wait_ge(small2_in, 32 * (l + 1))
                for t in range(TT):
                    last = pe.matmul(aux[:, 1, t * 256:(t + 1) * 256], a1T[:, t * P:(t + 1) * P], w_a2[:], start=True, stop=True)
                last.then_inc(la_pre, 1)
                pe.wait_ge(la_ready, seen(la_ready))
                for i, mat in enumerate((chunk_le, chunk_gt)):
                    for t in range(TT):
                        pe.matmul(aux[:, i, t * 256:(t + 1) * 256], mat[:], la[:, t], start=True, stop=True)
                for hd in range(4):
                    for t in range(TT):
                        last = pe.matmul(aux[0:HD, 2, hd * 4 + t * 2:hd * 4 + t * 2 + 2], la[:, t, hd * HD:(hd + 1) * HD],
                                         chunk_of[:], start=True, stop=True)
                last.then_inc(cum_ready, 1)
                pe.wait_ge(qk_dec, seen(qk_dec))
                for i in range(4):
                    src = z[:, i % 2, GQ:GK] if i < 2 else e_inv[:, i % 2]
                    for hd in range(4):
                        last = pe.transpose(aux[0:HD, i, hd * P:(hd + 1) * P], src[:, hd * HD:(hd + 1) * HD], ident[:])
                    last.then_inc(gT_ready, 1)
                pe.wait_ge(gT_out, seen(gT_out, 4))
                pe.wait_ge(acc_out, out_n["n"])
                for t in range(TT):
                    rows = slice(t * P, (t + 1) * P)
                    for hd in range(4):
                        last = pe.matmul(acc[:, t, 0, hd * P:(hd + 1) * P], kiT[:, hd, rows], qdT[:, hd, rows], start=True, stop=True)
                last.then_inc(att_ready, 1)
                for n in range(3):
                    rows = slice((n % 2) * 64, (n % 2 + 1) * 64)
                    for hd in range(4):
                        last = pe.matmul(aux[0:HD, n, hd * P:(hd + 1) * P], e_suf[rows, n // 2, hd * HD:(hd + 1) * HD],
                                         z[rows, n // 2, GV + hd * P:GV + (hd + 1) * P], start=True, stop=True)
                last.then_inc(kv_ready, 1)
                pe.wait_ge(att_out, seen(att_out))
                pe.wait_ge(states_ready, seen(states_ready))
                for t in range(TT):
                    for hd in range(4):
                        cols = slice(hd * P, (hd + 1) * P)
                        pe.matmul(acc[:, t, 1, cols], attM[:, t, hd, :], z[:, t, GV + hd * P:GV + (hd + 1) * P],
                                  start=True, stop=False, skip_group_check=True)
                        for c in range(2):
                            n = 2 * t + c
                            if n:
                                last = pe.matmul(acc[c * 64:(c + 1) * 64, t, 1, cols], qdT[:, hd, n * 64:(n + 1) * 64],
                                                 state[:, n - 1, hd, :], start=False, stop=True, skip_group_check=True)
                last.then_inc(og_ready, 1)
                pe.wait_ge(normed_ready, seen(normed_ready))
                turn(normed, 4)
                project([[(4, BLK)], [(4, BLK)]], pairs=x_split)
                pe.wait_ge(normed_ready, seen(normed_ready))
                turn(normed, 5)
                project([[(3, 384)], [(3, 384)]], pairs=x_split)
                two_blocks_unit(3, x_split)
                pe.wait_ge(mrope_done, seen(mrope_done))
                for i in range(8):
                    if i >= 4:
                        pe.wait_ge(mT_out, seen(mT_out))
                    t, hg, which = i % 2, i // 2 % 2, i // 4
                    for j in range(4):
                        last = pe.transpose(aux[0:QK, i % 4, j * P:(j + 1) * P], (qf, kf)[which][:, t, hg * 4 + j, :], ident[:])
                    last.then_inc(mT_ready, 1)
                pe.wait_ge(mT_out, seen(mT_out, 4))
                pe.wait_ge(acc_out, out_n["n"])
                attention(second_steps(), m_e, lambda b: lanes_of(m_pT[:, b]))
                pe.wait_ge(normed_ready, seen(normed_ready))
                turn(normed, 4, at=512)
                project([[(4, BLK)], [(4, BLK)]], pairs=x_split)
                pe.wait_ge(normed_ready, seen(normed_ready))
                turn(merged, KC8)
                project(full(2), pairs=x_split)
                pe.wait_ge(normed_ready, seen(normed_ready))
                turn(normed, KC8)
                ffn_steps("second", l)


_ROWS = {"pre_mix_g": 8, "attn_out_g": 4, "mlp_out_g": 4, "pre_ffn_g": 8, "ple_norm_g": 8, "cmp_pe": 32, "cmp_b1": 4,
         "gmlp_bs": 8, "conv_b": 44, "conv_w": 132, "norm_pre_mix_2": 8, "norm_pre_ffn_2": 8, "pool_scale_2": 4,
         "gla_norm_2": 4, "mla_q_norm_2": 3, "mla_kv_norm_2": 2}


def shape_constants():
    import numpy as np
    f = np.float32
    i = np.arange(P)
    c = {"c_ident": np.eye(P, dtype=f), "c_keep_le": (i[:, None] <= i[None, :]).astype(f),
         "c_causal": np.where(i[None, :] <= i[:, None], 0, NEG).astype(f)}
    same = (i[:, None] // 64) == (i[None, :] // 64)
    c["c_chunk_le"] = (same & (i[:, None] <= i[None, :])).astype(f)
    c["c_chunk_gt"] = (same & (i[:, None] > i[None, :])).astype(f)
    c["c_chunk_of"] = ((i[:, None] // 64) == np.arange(2)[None, :]).astype(f)
    tok = np.arange(SEQ).reshape(TT, P)
    ok = (16 * np.arange(CMP_N) + 31)[None, None, :] <= tok.T[:, :, None]
    c["c_cmp_mask"] = np.stack([np.where(ok, 0, NEG), ok], axis=1).astype(f)
    inv = (f(500000.0) ** (-np.arange(8, dtype=f) / f(8))).astype(f)

    def table(pos):
        ang = pos.astype(f)[:, None] * inv[None, :]
        return np.cos(ang).astype(f), np.sin(ang).astype(f)

    cos, sin = table(np.arange(SEQ))
    t = np.zeros((P, 2, TT, ROPE_UNITS, 8), f)
    t[:, 0] = 1
    for u in list(range(8)) + [12, 13, 16, 17]:
        t[:, 0, :, u] = cos.reshape(TT, P, 8).transpose(1, 0, 2)
        t[:, 1, :, u] = sin.reshape(TT, P, 8).transpose(1, 0, 2)
    c["c_rope1"] = np.ascontiguousarray(t.transpose(0, 2, 1, 3, 4).reshape(P, TT, 320))
    cos, sin = table(np.arange(CMP_N) * 16 + 31)
    c["c_rope_c"] = np.ascontiguousarray(np.stack([np.stack([x, x], 1) for x in (cos, sin)], 1))
    c["c_inv_freq"] = (f(10000.0) ** (-np.arange(0, 32, 2, dtype=f) / f(32))).astype(f)
    s = np.arange(SEQ)
    mats = []
    for w in (2, 4, 8, 16):
        m = ((s[None, :] <= s[:, None]) & (s[None, :] > s[:, None] - w)) / np.minimum(s + 1, w)[:, None] - np.eye(SEQ)
        mats.append(m.T.astype(f))
    c["c_pool"] = np.ascontiguousarray(np.stack(mats, 1).reshape(TT, P, 4, SEQ).transpose(1, 0, 2, 3))
    return c


def kernel(**inputs):
    import numpy as np
    import concourse.bacc as bacc
    from concourse.bass_utils import run_bass_kernel_spmd as run

    arrays = {}
    for name, a in inputs.items():
        a = np.ascontiguousarray(a)
        if name in ("x", "positions_2"):
            a = a[0]
        elif name == "p":
            a = a[:, 0]
        if name in _ROWS:
            arrays["rows_" + name] = a.reshape(DEPTH, _ROWS[name], P)
        else:
            arrays[name] = a
    arrays.update(shape_constants())
    nc = bacc.Bacc("TRN2", target_bir_lowering=False, num_devices=1)
    A = {}
    feed = {}
    for name, a in arrays.items():
        feed["in_" + name] = np.ascontiguousarray(a)
        A[name] = nc.dram_tensor("in_" + name, a.shape, mybir.dt.from_np(a.dtype), kind="ExternalInput").ap()
    out = nc.dram_tensor("out_h", (SEQ, DM), F32, kind="ExternalOutput").ap()
    two_blocks(nc, A, out)
    r = run(nc, [feed], core_ids=[0])
    return r.results[0]["out_h"].reshape(1, SEQ, DM)
```

```python
import concourse.bass as bass
from concourse import mybir
from contextlib import ExitStack

F32 = mybir.dt.float32
F32R = mybir.dt.float32r
I32 = mybir.dt.int32
ALU = mybir.AluOpType
ACT = mybir.ActivationFunctionType
AX = mybir.AxisListType

P = 128
SEQ, DM, DEPTH = 256, 1024, 2
TT = SEQ // P
EPS = 1e-6
NEG = -1e30
BLK = 512
UNIT = 2048
RING = 3
KC8 = DM // P

HEADS, HD, GROUPS = 8, 64, 2
W1 = 2328
GATE1, U1, V1 = 1280, 1304, 1816
CMP_N, CMP_HID = 15, 256
ROPE_UNITS = 20
W2 = 5808
Z2 = 2736
GQ, GK, GV, GR, GA, CQ, CKV, KR = 512, 768, 1024, 1536, 2048, 2064, 2448, 2704
QK = 96
D_FF = 2816
FB = 256
FSTEPS = D_FF // FB
FUNITS = 3 * FSTEPS
VECS1 = (("pre_mix_g", 8), ("attn_out_g", 4), ("mlp_out_g", 4), ("pre_ffn_g", 8), ("ple_norm_g", 8),
         ("cmp_pe", 32), ("cmp_b1", 4), ("gmlp_bs", 8), ("conv_b", 44), ("conv_w", 132))
VECS2 = (("norm_pre_mix_2", 8), ("norm_pre_ffn_2", 8), ("pool_scale_2", 4), ("gla_norm_2", 4),
         ("mla_q_norm_2", 3), ("mla_kv_norm_2", 2))
NVECS = DEPTH * sum(n for _, n in VECS1 + VECS2)
MASK_COLS = 5 * P + 2 + 2 * TT * CMP_N


class Seen:

    def __init__(self):
        self.n = {}

    def __call__(self, sem, k=1):
        self.n[id(sem)] = self.n.get(id(sem), 0) + k
        return self.n[id(sem)]

    def now(self, sem):
        return self.n.get(id(sem), 0)


def blocks_of(lo, hi):
    return [(a, min(BLK, hi - a)) for a in range(lo, hi, BLK)]


def unit_plan(A):
    units, ffn = [], {}

    def cols(w, k0, k1, c0, n):
        return (w[k0 * P:k1 * P, c0:c0 + n].rearrange("(k p) n -> p k n", p=P), k1 - k0, n)

    def matrix(w, nk, blocks):
        for c0, n in blocks:
            for k0 in range(0, nk, 4):
                units.append(cols(w, k0, min(k0 + 4, nk), c0, n))

    def ffn_units(key, up, down):
        ffn[key] = (len(units), up, down)
        units.extend([None] * FUNITS)

    for l in range(DEPTH):
        matrix(A["w_in"][l], KC8, blocks_of(0, W1))
        for kv in range(2):
            for half in range(2):
                units.append(cols(A["cmp_w1"][l, kv], half * 8, half * 8 + 8, 0, CMP_HID))
        matrix(A["w_o"][l], KC8, blocks_of(0, DM))
        ffn_units(("first", l), A["w_up"][l], A["w_down"][l])
        matrix(A["w_ple_gate"][l], KC8, blocks_of(0, DM))
        units.append(cols(A["w_ple_proj"][l], 0, 2, 0, DM))
    for l in range(DEPTH):
        gate_blocks = blocks_of(Z2, W2)
        matrix(A["w_in_2"][l], KC8, blocks_of(0, Z2) + gate_blocks[0:2])
        matrix(A["w_a_2"][l], 4, blocks_of(0, DM))
        matrix(A["w_in_2"][l], KC8, gate_blocks[2:6])
        matrix(A["w_mla_uq_2"][l], 3, [(0, 384), (384, 384)])
        units.append(cols(A["w_mla_ukv_2"][l], 0, 2, 0, DM))
        matrix(A["w_b_2"][l], 4, blocks_of(0, DM))
        matrix(A["w_c_2"][l], 4, blocks_of(0, DM))
        matrix(A["w_o_2"][l], KC8, blocks_of(0, DM))
        ffn_units(("second", l), A["w_ffn_gu_2"][l], A["w_ffn_down_2"][l])
    return units, ffn


def two_blocks(nc, A, out):
    units, ffn = unit_plan(A)
    ffn_starts = sorted(u for u, _, _ in ffn.values())

    with ExitStack() as ctx:
        def sb(name, shape, dt=F32):
            return ctx.enter_context(nc.sbuf_tensor(name, shape, dt))

        def sem(name):
            return ctx.enter_context(nc.semaphore(name))

        raw = sb("w_raw", [P, RING, UNIT])
        whi = sb("w_hi", [P, RING, UNIT], F32R)
        wlo = sb("w_lo", [P, RING, UNIT], F32R)
        xhi = sb("x_hi", [P, KC8, SEQ], F32R)
        xlo = sb("x_lo", [P, KC8, SEQ], F32R)
        yhi = sb("y_hi", [P, 5, SEQ], F32R)
        ylo = sb("y_lo", [P, 5, SEQ], F32R)
        fhi, flo = (t[:, 0:4].rearrange("p (a c) s -> p a c s", a=2) for t in (yhi, ylo))
        h = sb("h", [P, TT, DM])
        normed = sb("normed", [P, TT, DM])
        merged = sb("merged", [P, TT, DM])
        z = sb("z", [P, TT, Z2])
        area = sb("area", [P, 12288])
        vecs = sb("vecs", [P, NVECS])
        post_g = sb("post_g", [P, 2, DM])
        masks = sb("masks", [P, MASK_COLS])
        ident = masks[:, 0:P]
        causal = masks[:, P:2 * P]
        keep_le = masks[:, 2 * P:3 * P]
        chunk_le = masks[:, 3 * P:4 * P]
        chunk_gt = masks[:, 4 * P:5 * P]
        chunk_of = masks[:, 5 * P:5 * P + 2]
        cmp_mask = (masks[:, 5 * P + 2:MASK_COLS]
                    .rearrange("p (a t n) -> p a t n", a=2, t=TT))
        trig = sb("trig", [P, 256])
        rope2 = sb("rope2", [P, 2, TT, 16])
        ssq = sb("ssq", [P, 8])
        rstd = sb("rstd", [P, 8])
        mix_rstd = sb("mix_rstd", [P, 8])
        half_neg = sb("half_neg", [P, 8])
        stat = sb("stat", [P, TT, 6])
        mean_var = sb("mean_var", [P, TT, 2])
        nmax = sb("nmax", [P, 2, 2])
        esum = sb("esum", [P, TT, HEADS, 3])
        cmax = sb("cmax", [P, TT, HEADS])
        m_sum = sb("m_sum", [P, TT, HEADS])
        zero_row = sb("zero_row", [1, BLK], mybir.dt.bfloat16)
        acc_banks = ctx.enter_context(nc.psum_tensor("acc", [P, 2, TT, BLK], F32))
        acc = acc_banks[:].rearrange("p b t n -> p t b n")
        aux = ctx.enter_context(nc.psum_tensor("aux", [P, 4, BLK], F32))

        def carve(start, n, parts=P):
            return area[0:parts, start:start + n]

        qT = carve(0, 2048, HD).rearrange("p (h s) -> p h s", h=HEADS)
        kT = carve(2048, 1024, HD).rearrange("p (u s) -> p u s", u=4)
        e_buf = carve(3072, 1024).rearrange("p (b n) -> p b n", b=2)
        pT = carve(4096, 1024).rearrange("p (b n) -> p b n", b=2)
        hid = carve(3072, 512, 2 * CMP_N).rearrange("p (k n) -> p k n", k=2)
        ecT = carve(3072, 2048, CMP_N).rearrange("p (t h q) -> p t h q", t=TT, h=HEADS)
        attn = carve(6144, 1024).rearrange("p (t n) -> p t n", t=TT)
        zc2 = carve(6144, 1024).rearrange("p (t u a d) -> p t u a d", t=TT, u=4, a=2)
        ws_raw = carve(7168, 1024).rearrange("p (g s) -> p g s", g=8)
        wsT = carve(8192, 1024).rearrange("p (g s) -> p g s", g=8)
        mlp = carve(9216, 1024).rearrange("p (t n) -> p t n", t=TT)
        x_cmp = carve(10240, 960).rearrange("p (k c g n) -> p k c g n", k=2, c=16, g=GROUPS)
        part = carve(10240, 1024).rearrange("p (a n) -> p a n", a=2)
        hT = carve(11776, 120).rearrange("p (k c n) -> p k c n", k=2, c=2)
        kcT = carve(11896, 30, HD).rearrange("p (g n) -> p g n", g=GROUPS)
        ec = carve(11264, 240).rearrange("p (t h n) -> p t h n", t=TT, h=HEADS)
        factor = carve(11936, 48).rearrange("p (t h b) -> p t h b", t=TT, h=HEADS)
        kcv = carve(12032, 256, CMP_N).rearrange("p (k g d) -> p k g d", k=2, g=GROUPS)
        ple_gate = carve(0, 2048).rearrange("p (t n) -> p t n", t=TT)
        mflat = merged[:].rearrange("p t n -> p (t n)")
        ln_gb = mflat[:, 0:1024].rearrange("p (a n) -> p a n", a=2)
        cmp_w2 = mflat[:, 1024:1280].rearrange("p (k c d) -> p k c d", k=2, c=2)
        cmp_b2 = mflat[0:CMP_N, 1280:1536].rearrange("p (k g d) -> p k g d", k=2, g=GROUPS)
        p_in = mflat[:, 1536:2048].rearrange("p (t n) -> p t n", t=TT)
        zflat = z[:].rearrange("p t n -> p (t n)")
        rope1_cols = z[:, :, W1:W1 + 320]
        rope1 = rope1_cols.rearrange("p t (a u f) -> p t a u f", a=2, u=ROPE_UNITS)
        rope_c = sb("rope_c", [CMP_N, 2, GROUPS, 8])
        rt = carve(3072, 1280).rearrange("p (a t u f) -> p a t u f", a=4, t=TT, u=ROPE_UNITS)
        rt_c = carve(11504, 64, CMP_N).rearrange("p (a g f) -> p a g f", a=4, g=GROUPS)
        gates = carve(0, 6144).rearrange("p (t b n) -> p t b n", t=TT, b=3)
        pool_mat = carve(6144, 2048).rearrange("p (s g t) -> p s g t", s=TT, g=4)
        diffT = carve(8192, 1024).rearrange("p (g t) -> p g t", g=4)
        w_pool = carve(9216, 512).rearrange("p (g d) -> p g d", g=4)
        w_a2 = carve(9728, 256, 16)
        b_gla = carve(9984, 256)
        la, e_cum, e_suf, e_inv = (normed[:].rearrange("p t n -> p (t n)")[:, i * 512:(i + 1) * 512]
                                   .rearrange("p (t n) -> p t n", t=TT) for i in range(4))
        qdT = carve(6144, 1024, HD).rearrange("p (h s) -> p h s", h=4)
        kiT = carve(7168, 1024, HD).rearrange("p (h s) -> p h s", h=4)
        attM = carve(8192, 1024).rearrange("p (t h s) -> p t h s", t=TT, h=4)
        state = carve(9216, 1536, HD).rearrange("p (n h e) -> p n h e", n=3, h=4)
        a1T = carve(10752, 256, 16)
        decay = carve(11008, 16, HD).rearrange("p (h n) -> p h n", h=4)
        o_gla = carve(11264, 1024).rearrange("p (t n) -> p t n", t=TT)
        sq_gla = carve(6144, 1024).rearrange("p (t n) -> p t n", t=TT)
        qf = zflat[:, 0:1536].rearrange("p (t h d) -> p t h d", t=TT, h=HEADS)
        kf = zflat[:, Z2:Z2 + 1536].rearrange("p (t h d) -> p t h d", t=TT, h=HEADS)
        mqT = carve(6144, 2048, QK).rearrange("p (h s) -> p h s", h=HEADS)
        mkT = carve(8192, 2048, QK).rearrange("p (h s) -> p h s", h=HEADS)
        m_v = carve(10240, 1024).rearrange("p (t h d) -> p t h d", t=TT, h=HEADS)
        m_e = carve(11264, 1024).rearrange("p (b n) -> p b n", b=2)
        m_pT = normed[:, :, 0:512]
        hc = carve(0, 2048).rearrange("p (a w c s) -> p a w c s", a=2, w=2, c=2)
        sg = carve(2048, 512).rearrange("p (c s) -> p c s", c=2)
        f_act = carve(2560, 512).rearrange("p (c s) -> p c s", c=2)

        w_loaded = [sem(f"w_loaded{i}") for i in range(RING)]
        hi_ready, lo_ready, unit_done = sem("hi_ready"), sem("lo_ready"), sem("unit_done")
        masks_in, tables_in, vecs_in, h_in, out_done = (
            sem(s) for s in ("masks_in", "tables_in", "vecs_in", "h_in", "out_done"))
        small1_in, small2_in, post_in = sem("small1_in"), sem("small2_in"), sem("post_in")
        ple_in, pool_in, pos_in = sem("ple_in"), sem("pool_in"), sem("pos_in")
        setup_done = sem("setup_done")
        tile_done, half_done = sem("tile_done"), sem("half_done")
        sumsq_ready, rstd_ready, normed_ready = sem("sumsq_ready"), sem("rstd_ready"), sem("normed_ready")
        tp_ready, xhi_ready, x_split = sem("tp_ready"), sem("xhi_ready"), sem("x_split")
        acc_out, h_ready = sem("acc_out"), sem("h_ready")
        zc2_done = sem("zc2_done")
        rope_done, gelu_done, ct_ready, xc_sum, xc_hi = (
            sem("rope_done"), sem("gelu_done"), sem("ct_ready"), sem("xc_sum"), sem("xc_hi"))
        xc_split, qk_ready, qk_out = sem("xc_split"), sem("qk_ready"), sem("qk_out")
        hid_out, hidT_ready = sem("hid_out"), sem("hidT_ready")
        hT_out, kcv_ready, kcv_out, kcT_ready, kcT_out = (
            sem(s) for s in ("hT_out", "kcv_ready", "kcv_out", "kcT_ready", "kcT_out"))
        ws_ready, ws_out, ln_done, mix_ready = sem("ws_ready"), sem("ws_out"), sem("ln_done"), sem("mix_ready")
        ln_var = sem("ln_var")
        sc_ready, sc_shift, sc_exp, ec_ready, ect_ready, ect_out = (
            sem(s) for s in ("sc_ready", "sc_shift", "sc_exp", "ec_ready", "ect_ready", "ect_out"))
        cpv_done, cmp_out, gmlp_out, gate_done = sem("cpv_done"), sem("cmp_out"), sem("gmlp_out"), sem("gate_done")
        s_ready, max_ready, e_ready, pt_ready, pts_ready, pts_ready_dve, pv_done, mixed_ready = (
            sem(s) for s in ("s_ready", "max_ready", "e_ready", "pt_ready", "pts_ready", "pts_ready_dve", "pv_done", "mixed_ready"))
        gu_ready, hc_ready, hc_conv, sg_ready, fa_ready, fhi_ready, f_split = (
            sem(s) for s in ("gu_ready", "hc_ready", "hc_conv", "sg_ready", "fa_ready", "fhi_ready", "f_split"))
        yp_hi, yp_split = sem("yp_hi"), sem("yp_split")
        diff_ready, diff_out, ypool_ready = sem("diff_ready"), sem("diff_out"), sem("ypool_ready")
        a1_ready, a1_out, la_pre, la_x, la_ln, la_ready, cum_ready, exps_ready, qk_dec = (
            sem(s) for s in ("a1_ready", "a1_out", "la_pre", "la_x", "la_ln", "la_ready", "cum_ready",
                             "exps_ready", "qk_dec"))
        gT_ready, gT_out, att_ready, kv_ready, att_out, states_ready, og_ready, sq_out, og_silu = (
            sem(s) for s in ("gT_ready", "gT_out", "att_ready", "kv_ready", "att_out", "states_ready",
                             "og_ready", "sq_out", "og_silu"))
        mrope_done, mT_ready, mT_out = sem("mrope_done"), sem("mT_ready"), sem("mT_out")
        ang_ready, trig_done = sem("ang_ready"), sem("trig_done")

        g_of = {}
        c = 0
        for which, names in (("first", VECS1), ("second", VECS2)):
            for l in range(DEPTH):
                for name, n in names:
                    g_of[which, l, name] = c
                    c += n

        def vec(key, i):
            return vecs[:, g_of[key] + i:g_of[key] + i + 1]

        xhi_flat, xlo_flat = (t[:].rearrange("p k s -> p (k s)") for t in (xhi, xlo))

        def x_cmp_split(flat, kv):
            return flat[:, kv * 1024:kv * 1024 + 480]

        def first_steps():
            steps = []
            for qt in range(TT):
                for hd in range(HEADS):
                    g = hd // (HEADS // GROUPS)
                    lanes = [dict(q=qT[:, hd, qt * P:(qt + 1) * P], k=kT[:, 2 * br + g, :],
                                  v=z[:, :, 896 + 256 * br + g * HD:896 + 256 * br + (g + 1) * HD],
                                  o=aux[:, (1 + br, (3, 0)[br])[qt], hd * HD:(hd + 1) * HD],
                                  sums=esum[:, qt, hd, 1 + br:2 + br]) for br in range(2)]
                    steps.append(dict(qt=qt, nk=(qt + 1) * P, lanes=lanes))
            return steps

        def second_steps():
            steps = []
            for qt in range(TT):
                for h2 in range(0, HEADS, 2):
                    lanes = [dict(q=mqT[:, hd, qt * P:(qt + 1) * P], k=mkT[:, hd, :], v=m_v[:, :, hd, :],
                                  o=aux[:, 1 + qt, hd * HD:(hd + 1) * HD], sums=m_sum[:, qt, hd:hd + 1])
                             for hd in (h2, h2 + 1)]
                    steps.append(dict(qt=qt, nk=(qt + 1) * P, lanes=lanes))
            return steps

        def lanes_of(bank):
            return bank.rearrange("p (a n) -> p a n", a=2)

        def arrival(i, unit):
            return i * 32 + 16 * (unit // RING + 1)

        block = ctx.enter_context(nc.Block())

        @block.sync
        def _(sp):
            def load(u, view, kc, n):
                s = u % RING
                if u >= RING:
                    sp.wait_ge(lo_ready, u - RING + 1)
                sp.dma_start(raw[:, s, 0:kc * n].rearrange("p (k n) -> p k n", k=kc), view).then_inc(w_loaded[s], 16)

            def ffn_loads(u0, up, down):
                def hidden(j, part):
                    return up[:, bass.ds(j * FB + part * D_FF, FB)].rearrange("(k p) n -> p k n", p=P)

                def load_at(u, first, view, kc, n):
                    s = first % RING
                    sp.wait_ge(lo_ready, u - RING + 1)
                    sp.dma_start(raw[:, s, 0:kc * n].rearrange("p (k n) -> p k n", k=kc), view).then_inc(w_loaded[s], 16)

                for part in range(2):
                    load(u0 + part, up[:, part * D_FF:part * D_FF + FB].rearrange("(k p) n -> p k n", p=P), KC8, FB)
                with sp.Fori(0, FSTEPS // 2) as i:
                    for s in range(2):
                        first = u0 + 2 + 3 * s
                        u = i * 6 + first
                        for part in range(2):
                            load_at(u + part, first + part, hidden(i * 2 + (1 + s), part), KC8, FB)
                        load_at(u + 2, first + 2,
                                down[bass.ds((i * 2 + s) * FB, FB), :].rearrange("(k p) n -> p k n", p=P), 2, DM)
                load(u0 + FUNITS - 1, down[(FSTEPS - 1) * FB:D_FF, :].rearrange("(k p) n -> p k n", p=P), 2, DM)

            sp.dma_start(h[:], A["x"].rearrange("(t p) n -> p t n", p=P)).then_inc(h_in, 16)
            starts = {u: (up, down) for u, up, down in ffn.values()}
            for u, unit in enumerate(units):
                if unit is not None:
                    load(u, *unit)
                elif u in starts:
                    ffn_loads(u, *starts[u])
            sp.wait_ge(h_ready, 5 * DEPTH * TT)
            sp.dma_start(out.rearrange("(t p) n -> p t n", p=P), h[:]).then_inc(out_done, 16)
            sp.wait_ge(out_done, 16)

        @block.gpsimd
        def _(pool):
            seen = Seen()
            pool.memset(half_neg[:], -0.5).then_inc(setup_done, 1)
            pool.memset(zero_row[:], 0.0).then_inc(setup_done, 1)
            def inverse_root(n, width, k, dst=rstd):
                pool.wait_ge(sumsq_ready, seen(sumsq_ready, n))
                pool.tensor_scalar(dst[:, 0:k], ssq[:, 0:k], 1.0 / width, EPS, ALU.mult, ALU.add)
                pool.drain()
                pool.tensor_tensor(dst[:, 0:k], dst[:, 0:k], half_neg[:, 0:k], ALU.pow).then_inc(rstd_ready, 1)

            def tile_roots():
                for t in range(TT):
                    pool.wait_ge(sumsq_ready, seen(sumsq_ready))
                    pool.tensor_scalar(rstd[:, t:t + 1], ssq[:, t:t + 1], 1.0 / DM, EPS, ALU.mult, ALU.add)
                    pool.drain()
                    pool.tensor_tensor(rstd[:, t:t + 1], rstd[:, t:t + 1], half_neg[:, 0:1], ALU.pow).then_inc(rstd_ready, 1)

            def residual_roots(counts):
                for t in range(TT):
                    pool.wait_ge(sumsq_ready, seen(sumsq_ready, counts[t]))
                    pool.tensor_tensor(rstd[:, t:t + 1], ssq[:, t:t + 1], ssq[:, 2 + t:3 + t], ALU.add)
                    pool.drain()
                    pool.tensor_scalar(rstd[:, t:t + 1], rstd[:, t:t + 1], 1.0 / DM, EPS, ALU.mult, ALU.add)
                    pool.drain()
                    pool.tensor_tensor(rstd[:, t:t + 1], rstd[:, t:t + 1], half_neg[:, 0:1], ALU.pow).then_inc(rstd_ready, 1)

            def first_small(l):
                pool.dma_start(ws_raw, A["gmlp_ws"][l].rearrange("g t s -> t g s")).then_inc(small1_in, 16)
                for i, name in enumerate(("gmlp_ln_g", "gmlp_ln_b")):
                    pool.dma_start(ln_gb[:, i], A[name][l].partition_broadcast(P)).then_inc(small1_in, 16)
                pool.dma_start(cmp_w2, A["cmp_w2"][l].rearrange("k (c p) d -> p k c d", p=P)).then_inc(small1_in, 16)
                for kv in range(2):
                    for g in range(GROUPS):
                        pool.dma_start(cmp_b2[:, kv, g], A["cmp_b2"][l, kv].partition_broadcast(CMP_N)).then_inc(small1_in, 16)
                pool.dma_start(p_in, A["p"][l].rearrange("(t p) n -> p t n", p=P)).then_inc(small1_in, 16)

            def post_gains(a, b):
                pool.dma_start(post_g[:, 0], a.partition_broadcast(P)).then_inc(post_in, 16)
                pool.dma_start(post_g[:, 1], b.partition_broadcast(P)).then_inc(post_in, 16)

            pool.wait_ge(setup_done, 2)
            for l in range(DEPTH):
                inverse_root(TT, DM, 2)
                if l:
                    pool.wait_ge(h_ready, 3 * TT * l)
                else:
                    pool.dma_start(rope1_cols, A["c_rope1"]).then_inc(tables_in, 16)
                    pool.dma_start(rope_c[:], A["c_rope_c"]).then_inc(tables_in, 16)
                    pool.dma_start(trig[:, 0:2].bitcast(I32), A["positions_2"]).then_inc(pos_in, 16)
                    pool.dma_start(trig[:, 2:18], A["c_inv_freq"].partition_broadcast(P)).then_inc(pos_in, 16)
                first_small(l)
                post_gains(A["post_mix_g"][l], A["post_ffn_g"][l])
                pool.wait_ge(ln_var, seen(ln_var))
                pool.tensor_scalar(rstd[:, 4:6], mean_var[:, :, 1], 1.0, EPS, ALU.mult, ALU.add)
                pool.drain()
                pool.tensor_tensor(rstd[:, 4:6], rstd[:, 4:6], half_neg[:, 0:2], ALU.pow).then_inc(rstd_ready, 1)
                inverse_root(2 * TT, 512, 4)
                residual_roots((3, 1))
                tile_roots()
                residual_roots((2, 2))
                inverse_root(TT, DM, 2)
            for l in range(DEPTH):
                inverse_root(TT, DM, 2)
                pool.wait_ge(h_ready, (3 * DEPTH + 2 * l) * TT)
                post_gains(A["norm_post_mix_2"][l], A["norm_post_ffn_2"][l])
                pool.dma_start(b_gla, A["b_gla_a_2"][l].partition_broadcast(P)).then_inc(small2_in, 16)
                pool.dma_start(w_a2, A["w_gla_a2_2"][l]).then_inc(small2_in, 16)
                pool.dma_start(pool_mat, A["c_pool"]).then_inc(pool_in, 16)
                pool.dma_start(w_pool, A["w_pool_2"][l].rearrange("g c d -> c g d")).then_inc(pool_in, 16)
                pool.wait_ge(sumsq_ready, seen(sumsq_ready, 2 * TT))
                pool.tensor_scalar(mix_rstd[:, 0:2], ssq[:, 0:2], 1.0 / 384, EPS, ALU.mult, ALU.add)
                pool.tensor_scalar(mix_rstd[:, 2:4], ssq[:, 2:4], 1.0 / 256, EPS, ALU.mult, ALU.add)
                pool.drain()
                pool.tensor_tensor(mix_rstd[:, 0:4], mix_rstd[:, 0:4], half_neg[:, 0:4], ALU.pow).then_inc(rstd_ready, 1)
                inverse_root(1, 128, 8, mix_rstd)
                residual_roots((3, 1))
                tile_roots()
                residual_roots((2, 2))

        @block.scalar
        def _(act):
            seen = Seen()
            st = {"split": 0, "unit": 0}

            def split(u):
                s = u % RING
                kc, n = (KC8, FB) if units[u] is None else units[u][1:]
                act.wait_ge(w_loaded[s], 16 * (u // RING + 1))
                if u >= RING:
                    act.wait_ge(unit_done, u - RING + 1)
                act.activation(whi[:, s, 0:kc * n], raw[:, s, 0:kc * n], ACT.Copy).then_inc(hi_ready, 1)

            def split_ahead(more=2):
                top = min(st["unit"] + more, len(units) - 1)
                for f in ffn_starts:
                    if st["split"] <= f + 2:
                        top = min(top, f + 1)
                while st["split"] <= top:
                    split(st["split"])
                    st["split"] += 1

            def sums_of_squares(src, width, at=0, junk=0):
                for t in range(TT):
                    act.activation(normed[:, t, junk:junk + width], src(t), ACT.Square,
                                   accum_out=ssq[:, at + t:at + t + 1]).then_inc(sumsq_ready, 1)

            def x_high(nk, gain, at=0, xhi=xhi):
                for k in range(0, nk, 2):
                    act.wait_ge(tp_ready, seen(tp_ready))
                    bank = aux[:, (seen.now(tp_ready) - 1) % 2, :].rearrange("p (k s) -> p k s", k=2)
                    m = min(2, nk - k)
                    if gain is None:
                        last = act.activation(xhi[:, at + k:at + k + m, :], bank[:, 0:m], ACT.Copy)
                    else:
                        for j in range(m):
                            last = act.activation(xhi[:, at + k + j, :], bank[:, j], ACT.Copy, scale=gain(k + j))
                    last.then_inc(xhi_ready, 1)

            def next_block(n_units=2):
                st["unit"] += n_units
                split_ahead(1)
                act.wait_ge(unit_done, st["unit"])

            def scaled_out(i, n, dst, func):
                if i == 0:
                    act.wait_ge(rstd_ready, seen(rstd_ready))
                for t in range(TT):
                    last = act.activation(dst(t), acc[:, t, i % 2, 0:n], func, scale=rstd[:, t:t + 1])
                last.then_inc(acc_out, 1)

            def residual_sum(t, b):
                act.drain()
                act.activation(aux[:, 2 + b], acc[:, t, b], ACT.Square,
                               accum_out=ssq[:, 2 * b + t:2 * b + t + 1]).then_inc(sumsq_ready, 1)

            def norm_of_h():
                for t in range(TT):
                    act.wait_ge(h_ready, seen(h_ready))
                    act.drain()
                    act.activation(aux[:, 2:4].rearrange("p a n -> p (a n)"), h[:, t], ACT.Square,
                                   accum_out=ssq[:, t:t + 1]).then_inc(sumsq_ready, 1)
                act.wait_ge(rstd_ready, seen(rstd_ready, TT))
                act.activation(normed[:, 1], h[:, 1], ACT.Copy, scale=rstd[:, 1:2]).then_inc(normed_ready, 1)

            def ffn_steps(which, l):
                u0 = ffn[which, l][0]
                st["split"] = u0 + FUNITS
                gu0, cv0, fa0 = seen.now(gu_ready), seen.now(hc_conv), seen.now(fa_ready)
                cb, cw = (g_of["first", l, n] for n in ("conv_b", "conv_w")) if which == "first" else (0, 0)

                def split_at(i, first):
                    act.wait_ge(w_loaded[first % RING], arrival(i, first))
                    act.wait_ge(unit_done, i * 6 + (first - RING + 1))
                    act.activation(whi[:, first % RING], raw[:, first % RING], ACT.Copy).then_inc(hi_ready, 1)

                def hidden(j, par):
                    act.wait_ge(gu_ready, j + (gu0 + 1))
                    if which == "second":
                        act.activation(sg, aux[:, 2 * par].rearrange("p (c s) -> p c s", c=2), ACT.Silu).then_inc(sg_ready, 1)
                    else:
                        for w in range(2):
                            for c2 in range(2):
                                act.activation(hc[:, par, w, c2], aux[:, 2 * par + w, c2 * SEQ:(c2 + 1) * SEQ], ACT.Identity,
                                               scale=vecs[:, bass.ds(j * 2 + (cw + 88 + w * 22 + c2), 1)],
                                               bias=vecs[:, bass.ds(j * 2 + (cb + w * 22 + c2), 1)]).then_inc(hc_ready, 1)
                        act.wait_ge(hc_conv, j + (cv0 + 1))
                        act.activation(sg, hc[:, par, 0], ACT.Silu).then_inc(sg_ready, 1)
                    act.wait_ge(fa_ready, j + (fa0 + 1))
                    act.activation(fhi[:, par], f_act, ACT.Copy).then_inc(fhi_ready, 1)

                with act.Fori(0, FSTEPS // 2) as i:
                    for s in range(2):
                        first = u0 + 2 + 3 * s
                        split_at(i, first)
                        split_at(i, first + 1)
                        hidden(i * 2 + s, s)
                        split_at(i, first + 2)
                split(u0 + FUNITS - 1)
                hidden(FSTEPS - 1, (FSTEPS - 1) % 2)
                for sm in (gu_ready, hc_conv, fa_ready):
                    seen(sm, FSTEPS) if which == "first" or sm is not hc_conv else None
                st["unit"] = u0 + FUNITS
                for t in range(TT):
                    if t == 0:
                        act.wait_ge(tile_done, seen(tile_done))
                    else:
                        act.wait_ge(unit_done, st["unit"])
                    for b in range(2):
                        residual_sum(t, b)
                seen(rstd_ready, TT)

            def attention(steps, e, pt):
                b_max, b_pt, b_pv = seen.now(max_ready), seen.now(pt_ready), seen.now(pv_done)
                for i in range(len(steps) + 1):
                    if i < len(steps):
                        nk = steps[i]["nk"]
                        act.wait_ge(max_ready, b_max + i + 1)
                        if i >= 2:
                            act.wait_ge(pt_ready, b_pt + i - 1)
                        for a, lane in enumerate(steps[i]["lanes"]):
                            last = act.activation(e[:, i % 2, a * 256:a * 256 + nk], acc[:, 0, i % 2, a * 256:a * 256 + nk],
                                                  ACT.Exp, bias=nmax[:, i % 2, a:a + 1], accum_out=lane["sums"])
                        last.then_inc(e_ready, 1)
                    j = i - 1
                    if j >= 0 and j % 2 == 0:
                        nk = steps[j]["nk"]
                        act.wait_ge(pt_ready, b_pt + j + 1)
                        if j >= 2:
                            act.wait_ge(pv_done, b_pv + j - 1)
                        act.activation(pt(j % 2)[:, :, 0:nk], lanes_of(acc[:, 1, j % 2])[:, :, 0:nk], ACT.Copy).then_inc(pts_ready, 1)
                for sm in (max_ready, pt_ready, pv_done):
                    seen(sm, len(steps))

            act.dma_start(masks[:], A["c_masks"]).then_inc(masks_in, 16)
            act.dma_start(vecs[:], A["vecs"]).then_inc(vecs_in, 16)
            act.wait_ge(h_in, 16)
            act.wait_ge(vecs_in, 16)

            for l in range(DEPTH):
                key = lambda name: ("first", l, name)
                if l:
                    act.wait_ge(h_ready, seen(h_ready, TT))
                split_ahead(0)
                x_high(KC8, lambda k: vec(key("pre_mix_g"), k))
                sums_of_squares(lambda t: h[:, t], DM)
                split_ahead()
                for i, (c0, n) in enumerate(blocks_of(0, W1)):
                    next_block()
                    scaled_out(i, n, lambda t: z[:, t, c0:c0 + n], ACT.Copy)
                split_ahead()
                act.drain()
                for t in range(TT):
                    last = act.activation(zc2[:, t], z[:, t, 512:768].rearrange("p (u d) -> p u d", u=4).unsqueeze(2)
                                          .broadcast_to([P, 4, 2, HD]), ACT.Copy)
                last.then_inc(zc2_done, 1)
                if l == 0:
                    act.wait_ge(ang_ready, 1)
                    act.activation(rope2[:].rearrange("p a t f -> p (a t f)"), trig[:, 128:192], ACT.Sin).then_inc(trig_done, 1)
                act.activation(z[:, :, GATE1:U1], z[:, :, GATE1:U1], ACT.Tanh, scale=0.5).then_inc(gate_done, 1)
                act.activation(z[:, :, V1:W1], z[:, :, V1:W1], ACT.Gelu_apprx_tanh).then_inc(gelu_done, 1)
                for kv in range(2):
                    act.wait_ge(xc_sum, seen(xc_sum))
                    act.activation(x_cmp_split(xhi_flat, kv), x_cmp[:, kv].rearrange("p c g n -> p (c g n)"), ACT.Copy).then_inc(xc_hi, 1)
                for i in range(6):
                    act.wait_ge(qk_ready, seen(qk_ready))
                    t, which = i % 2, i // 2
                    src = aux[0:HD, 2 + i % 2, :].rearrange("p (h s) -> p h s", h=4)
                    dst = kT[:, :, t * P:(t + 1) * P] if which == 2 else qT[:, which * 4:which * 4 + 4, t * P:(t + 1) * P]
                    act.activation(dst, src, ACT.Copy, scale=1.0 if which == 2 else HD ** -0.5).then_inc(qk_out, 1)
                act.activation(z[:, :, U1:V1], z[:, :, U1:V1], ACT.Gelu_apprx_tanh).then_inc(gelu_done, 1)
                for kv in range(2):
                    next_block()
                    act.activation(hid[:, kv], acc[0:2 * CMP_N, 0, kv, 0:CMP_HID], ACT.Copy).then_inc(hid_out, 1)
                act.wait_ge(hidT_ready, seen(hidT_ready))
                for kv in range(2):
                    for c2 in range(2):
                        last = act.activation(hT[:, kv, c2], acc[:, 1, kv, c2 * 30:(c2 + 1) * 30], ACT.Gelu_apprx_tanh,
                                              bias=vec(key("cmp_b1"), kv * 2 + c2))
                last.then_inc(hT_out, 1)
                act.wait_ge(kcT_ready, seen(kcT_ready))
                seen(rstd_ready)
                act.activation(kcT, aux[0:HD, 3, 0:30].rearrange("p (g n) -> p g n", g=2), ACT.Copy).then_inc(kcT_out, 1)
                split_ahead()

                act.wait_ge(sc_shift, seen(sc_shift))
                act.activation(ec, ec, ACT.Exp).then_inc(sc_exp, 1)
                act.wait_ge(ect_ready, seen(ect_ready))
                for qt in range(TT):
                    last = act.activation(ecT[:, qt].rearrange("p (a h) q -> p a (h q)", a=2),
                                          acc[0:CMP_N, qt], ACT.Copy)
                last.then_inc(ect_out, 1)
                attention(first_steps(), e_buf, lambda b: lanes_of(pT[:, b]))
                act.wait_ge(mixed_ready, seen(mixed_ready))
                sums_of_squares(lambda t: attn[:, t], 512)
                sums_of_squares(lambda t: mlp[:, t], 512, at=2, junk=512)
                seen(rstd_ready)
                x_high(KC8, lambda k: vec(key("attn_out_g"), k) if k < 4 else vec(key("mlp_out_g"), k - 4))
                next_block()
                for t in range(TT):
                    residual_sum(t, 0)
                st["unit"] += 2
                split_ahead(1)
                act.wait_ge(tile_done, seen(tile_done))
                residual_sum(0, 1)
                act.wait_ge(unit_done, st["unit"])
                residual_sum(1, 1)
                seen(rstd_ready, TT)
                norm_of_h()
                split_ahead()
                x_high(KC8, lambda k: vec(key("pre_ffn_g"), k))
                ffn_steps("first", l)
                act.wait_ge(h_ready, seen(h_ready, TT))
                x_high(KC8, lambda k: vec(key("ple_norm_g"), k))
                sums_of_squares(lambda t: h[:, t], DM)
                for nb in range(2):
                    next_block()
                    scaled_out(nb, BLK, lambda t: ple_gate[:, t, nb * BLK:(nb + 1) * BLK], ACT.Sigmoid)
                x_high(2, None)
                st["unit"] += 1
                split_ahead()

            for l in range(DEPTH):
                key = lambda name: ("second", l, name)
                act.wait_ge(h_ready, seen(h_ready, TT))
                split_ahead(0)
                x_high(KC8, lambda k: vec(key("norm_pre_mix_2"), k))
                sums_of_squares(lambda t: h[:, t], DM)
                split_ahead()
                for i, (c0, n) in enumerate(blocks_of(0, Z2)):
                    next_block()
                    scaled_out(i, n, lambda t: z[:, t, c0:c0 + n], ACT.Copy)
                act.drain()
                sums_of_squares(lambda t: z[:, t, CQ:CKV], 384)
                sums_of_squares(lambda t: z[:, t, CKV:KR], 256, at=2, junk=384)
                seen(rstd_ready)
                split_ahead()

                def gate_block(i, bank=0):
                    next_block()
                    for t in range(TT):
                        last = act.activation(gates[:, t, i // 2, (i % 2) * BLK:(i % 2 + 1) * BLK], acc[:, t, bank, :],
                                              ACT.Sigmoid, scale=rstd[:, t:t + 1])
                    last.then_inc(acc_out, 1)

                act.wait_ge(diff_ready, seen(diff_ready))
                act.activation(diffT.rearrange("p g t -> p (g t)"), aux[:, 0:2, :].rearrange("p a n -> p (a n)"), ACT.Copy).then_inc(diff_out, 1)
                gate_block(0)
                act.wait_ge(ypool_ready, seen(ypool_ready))
                for g in range(4):
                    last = act.activation(yhi[:, g], aux[:, 2 + g // 2, (g % 2) * SEQ:(g % 2 + 1) * SEQ], ACT.Copy,
                                          scale=vec(key("pool_scale_2"), g))
                last.then_inc(yp_hi, 1)
                act.wait_ge(a1_ready, seen(a1_ready))
                act.activation(a1T, aux[0:16, 0, 0:SEQ], ACT.Copy).then_inc(a1_out, 1)
                gate_block(1)
                act.wait_ge(la_x, seen(la_x))
                act.activation(e_cum, la, ACT.Abs)
                act.drain()
                act.activation(e_cum, e_cum, ACT.Exp, scale=-1.0)
                act.drain()
                act.activation(e_cum, e_cum, ACT.Ln, bias=1.0).then_inc(la_ln, 1)
                for nb in range(2):
                    st["unit"] += 1
                split_ahead()
                act.wait_ge(cum_ready, seen(cum_ready))
                cum = aux[:, 0, :].rearrange("p (t n) -> p t n", t=TT)
                act.activation(e_cum, cum, ACT.Exp, scale=1.0 / 16)
                act.activation(e_inv, cum, ACT.Exp, scale=-1.0 / 16)
                act.activation(e_suf, aux[:, 1, :].rearrange("p (t n) -> p t n", t=TT), ACT.Exp, scale=1.0 / 16)
                act.activation(decay, aux[0:HD, 2, 0:16].rearrange("p (h n) -> p h n", h=4), ACT.Exp,
                               scale=1.0 / 16).then_inc(exps_ready, 1)
                gate_block(2)
                for i in range(4):
                    act.wait_ge(gT_ready, seen(gT_ready))
                    dst = (qdT, kiT)[i // 2]
                    act.activation(dst[:, :, (i % 2) * P:(i % 2 + 1) * P],
                                   aux[0:HD, i, :].rearrange("p (h s) -> p h s", h=4), ACT.Copy).then_inc(gT_out, 1)
                gate_block(3, bank=1)
                act.activation(z[:, :, GR:GA], z[:, :, GR:GA], ACT.Silu).then_inc(og_silu, 1)
                gate_block(4)
                act.wait_ge(og_ready, seen(og_ready))
                act.activation(sq_gla, acc[:, :, 1, :], ACT.Square).then_inc(sq_out, 1)
                seen(rstd_ready)
                x_high(5, lambda k: vec(key("mla_q_norm_2"), k) if k < 3 else vec(key("mla_kv_norm_2"), k - 3), xhi=yhi)
                gate_block(5)
                split_ahead()
                x_high(4, lambda k: vec(key("gla_norm_2"), k))
                for nb in range(2):
                    next_block(1)
                    act.activation(qf[:, :, nb * 4:nb * 4 + 4, :], acc[:, :, nb, 0:384].rearrange("p t (h d) -> p t h d", h=4),
                                   ACT.Copy).then_inc(acc_out, 1)
                next_block(1)
                for nb in range(2):
                    src = acc[:, :, nb, :].rearrange("p t (h d) -> p t h d", h=4)
                    act.activation(kf[:, :, nb * 4:nb * 4 + 4, 0:64], src[:, :, :, 0:64], ACT.Copy)
                    act.activation(m_v[:, :, nb * 4:nb * 4 + 4, :], src[:, :, :, 64:128], ACT.Copy).then_inc(acc_out, 1)
                for nb in range(2):
                    st["unit"] += 1
                split_ahead()
                for i in range(8):
                    act.wait_ge(mT_ready, seen(mT_ready))
                    t, hg, which = i % 2, i // 2 % 2, i // 4
                    dst = (mqT, mkT)[which]
                    act.activation(dst[:, hg * 4:hg * 4 + 4, t * P:(t + 1) * P],
                                   aux[0:QK, i % 4, :].rearrange("p (h s) -> p h s", h=4), ACT.Copy,
                                   scale=QK ** -0.5 if which == 0 else 1.0).then_inc(mT_out, 1)
                split_ahead()
                attention(second_steps(), m_e, lambda b: lanes_of(m_pT[:, b]))
                x_high(4, None)
                for nb in range(2):
                    st["unit"] += 1
                split_ahead()
                x_high(KC8, None)
                next_block()
                for t in range(TT):
                    residual_sum(t, 0)
                st["unit"] += 2
                split_ahead(1)
                act.wait_ge(tile_done, seen(tile_done))
                residual_sum(0, 1)
                act.wait_ge(unit_done, st["unit"])
                residual_sum(1, 1)
                seen(rstd_ready, TT)
                norm_of_h()
                split_ahead()
                x_high(KC8, lambda k: vec(key("norm_pre_ffn_2"), k))
                ffn_steps("second", l)

        @block.vector
        def _(dve):
            seen = Seen()
            st = {"split": 0, "unit": 0}

            def split(u):
                s = u % RING
                kc, n = (KC8, FB) if units[u] is None else units[u][1:]
                dve.wait_ge(hi_ready, u + 1)
                dve.tensor_tensor(wlo[:, s, 0:kc * n], raw[:, s, 0:kc * n], whi[:, s, 0:kc * n].bitcast(F32),
                                  ALU.subtract).then_inc(lo_ready, 1)

            def split_ahead(more=2):
                top = min(st["unit"] + more, len(units) - 1)
                for f in ffn_starts:
                    if st["split"] <= f + 2:
                        top = min(top, f + 1)
                while st["split"] <= top:
                    split(st["split"])
                    st["split"] += 1

            def normalize(src, width, at=0, to=0):
                for t in range(TT):
                    last = dve.tensor_scalar(normed[:, t, to:to + width], src(t), rstd[:, at + t:at + t + 1], None, ALU.mult)
                return last

            def x_low(nk, gain, at=0, xhi=xhi, xlo=xlo):
                for k in range(0, nk, 2):
                    dve.wait_ge(xhi_ready, seen(xhi_ready))
                    bank = aux[:, (seen.now(xhi_ready) - 1) % 2, :].rearrange("p (k s) -> p k s", k=2)
                    m = min(2, nk - k)
                    hi = xhi[:, at + k:at + k + m, :].bitcast(F32)
                    if gain is None:
                        last = dve.tensor_tensor(xlo[:, at + k:at + k + m, :], bank[:, 0:m], hi, ALU.subtract)
                    else:
                        for j in range(m):
                            last = dve.scalar_tensor_tensor(xlo[:, at + k + j, :], bank[:, j], gain(k + j), hi[:, j],
                                                            ALU.mult, ALU.subtract)
                    last.then_inc(x_split, 1)

            def gained(i, t, b):
                cols = slice(b * BLK, (b + 1) * BLK)
                dve.wait_ge(sumsq_ready, seen(sumsq_ready))
                last = dve.tensor_tensor(normed[:, t, cols], acc[:, t, b], post_g[:, i, cols], ALU.mult)
                if t == TT - 1:
                    last.then_inc(acc_out, 1)

            def residual():
                dve.drain()
                for t in range(TT):
                    dve.wait_ge(rstd_ready, seen(rstd_ready))
                    dve.scalar_tensor_tensor(h[:, t], normed[:, t], rstd[:, t:t + 1], h[:, t], ALU.mult, ALU.add).then_inc(h_ready, 1)

            def norm_of_h():
                seen(sumsq_ready, TT)
                dve.wait_ge(rstd_ready, seen(rstd_ready))
                dve.tensor_scalar(normed[:, 0], h[:, 0], rstd[:, 0:1], None, ALU.mult).then_inc(normed_ready, 1)
                seen(rstd_ready)

            def ffn_steps(which, l):
                u0 = ffn[which, l][0]
                st["split"] = u0 + FUNITS
                hc0, sg0, fh0 = seen.now(hc_ready), seen.now(sg_ready), seen.now(fhi_ready)
                cw = g_of["first", l, "conv_w"]

                def split_at(i, first):
                    dve.wait_ge(hi_ready, i * 6 + (first + 1))
                    s = first % RING
                    dve.tensor_tensor(wlo[:, s], raw[:, s], whi[:, s].bitcast(F32), ALU.subtract).then_inc(lo_ready, 1)

                def hidden(j, par):
                    if which == "first":
                        dve.wait_ge(hc_ready, j * 4 + (hc0 + 4))
                        for back in (1, 2):
                            for w in range(2):
                                for c2 in range(2):
                                    tile = hc[:, par, w, c2, back:SEQ]
                                    tap = vecs[:, bass.ds(j * 2 + (cw + (2 - back) * 44 + w * 22 + c2), 1)]
                                    last = dve.scalar_tensor_tensor(
                                        tile, aux[:, 2 * par + w, c2 * SEQ:(c2 + 1) * SEQ - back], tap, tile,
                                        ALU.mult, ALU.add)
                            if back == 1:
                                dve.drain()
                        last.then_inc(hc_conv, 1)
                        up = hc[:, par, 1]
                    else:
                        up = aux[:, 2 * par + 1].rearrange("p (c s) -> p c s", c=2)
                        dve.drain()
                    dve.wait_ge(sg_ready, j + (sg0 + 1))
                    dve.tensor_tensor(f_act, up, sg, ALU.mult).then_inc(fa_ready, 1)
                    dve.wait_ge(fhi_ready, j + (fh0 + 1))
                    dve.tensor_tensor(flo[:, par], f_act, fhi[:, par].bitcast(F32), ALU.subtract).then_inc(f_split, 1)

                with dve.Fori(0, FSTEPS // 2) as i:
                    for s in range(2):
                        first = u0 + 2 + 3 * s
                        split_at(i, first)
                        split_at(i, first + 1)
                        hidden(i * 2 + s, s)
                        split_at(i, first + 2)
                split(u0 + FUNITS - 1)
                hidden(FSTEPS - 1, (FSTEPS - 1) % 2)
                if which == "first":
                    seen(hc_ready, 4 * FSTEPS)
                seen(sg_ready, FSTEPS), seen(fhi_ready, FSTEPS)
                st["unit"] = u0 + FUNITS

            def attention(steps, pt, after=None):
                b_s, b_pt, b_pv = seen.now(s_ready), seen.now(pt_ready), seen.now(pv_done)
                for i in range(len(steps) + 1):
                    if i < len(steps):
                        nk, qt = steps[i]["nk"], steps[i]["qt"]
                        dve.wait_ge(s_ready, b_s + i + 1)
                        lanes = lanes_of(acc[:, 0, i % 2])
                        dve.tensor_tensor(lanes[:, :, qt * P:nk], lanes[:, :, qt * P:nk],
                                          causal.unsqueeze(1).broadcast_to([P, 2, P]), ALU.add)
                        dve.drain()
                        dve.tensor_reduce(nmax[:, i % 2], lanes[:, :, 0:nk], AX.X, ALU.max, negate=True).then_inc(max_ready, 1)
                    j = i - 1
                    if j >= 0 and j % 2 == 1:
                        nk = steps[j]["nk"]
                        dve.wait_ge(pt_ready, b_pt + j + 1)
                        if j >= 2:
                            dve.wait_ge(pv_done, b_pv + j - 1)
                        dve.tensor_copy(pt(j % 2)[:, :, 0:nk], lanes_of(acc[:, 1, j % 2])[:, :, 0:nk]).then_inc(pts_ready_dve, 1)
                for sm in (s_ready, pt_ready, pv_done):
                    seen(sm, len(steps))
                dve.wait_ge(pv_done, seen.now(pv_done))

            def rotate(x1, x2, cos, sin, temps):
                a, b, c, d = temps
                dve.tensor_tensor(a, x1, cos, ALU.mult)
                dve.tensor_tensor(b, x2, sin, ALU.mult)
                dve.tensor_tensor(c, x2, cos, ALU.mult)
                dve.tensor_tensor(d, x1, sin, ALU.mult)
                dve.drain()
                dve.tensor_tensor(x1, a, b, ALU.subtract)
                return dve.tensor_tensor(x2, c, d, ALU.add)

            def angles():
                dve.wait_ge(pos_in, 32)
                C1 = 6.28125
                C2 = 0.0019353071693331003
                C3 = 1.0253404e-11
                pos, ang, arg, turns = trig[:, 20:22], trig[:, 64:128], trig[:, 128:192], trig[:, 192:256]
                dve.tensor_copy(pos, trig[:, 0:2].bitcast(I32))
                dve.drain()
                for a in range(2):
                    for t in range(TT):
                        dve.tensor_scalar(ang[:, a * 32 + t * 16:a * 32 + t * 16 + 16], trig[:, 2:18], pos[:, t:t + 1], None, ALU.mult)
                dve.drain()
                dve.tensor_scalar(turns[:, 0:32], ang[:, 0:32], 0.15915494309189535, 0.25, ALU.mult, ALU.add)
                dve.tensor_scalar(turns[:, 32:64], ang[:, 32:64], 0.15915494309189535, None, ALU.mult)
                dve.drain()
                dve.tensor_scalar(turns, turns, 12582912.0, None, ALU.add)
                dve.drain()
                dve.tensor_scalar(turns, turns, 12582912.0, None, ALU.subtract)
                dve.drain()
                dve.scalar_tensor_tensor(arg, turns, -C1, ang, ALU.mult, ALU.add)
                dve.drain()
                dve.scalar_tensor_tensor(arg, turns, -C2, arg, ALU.mult, ALU.add)
                dve.drain()
                dve.scalar_tensor_tensor(arg, turns, -C3, arg, ALU.mult, ALU.add)
                dve.drain()
                dve.tensor_scalar(arg[:, 0:32], arg[:, 0:32], 1.5707963267948966, None, ALU.add)
                dve.drain()
                dve.tensor_scalar(arg, arg, 3.1415925, -3.1415925, ALU.min, ALU.max).then_inc(ang_ready, 1)

            dve.wait_ge(masks_in, 16)
            dve.wait_ge(h_in, 16)
            dve.wait_ge(vecs_in, 16)
            for l in range(DEPTH):
                key = lambda name: ("first", l, name)
                seen(sumsq_ready, TT), seen(rstd_ready)
                split_ahead(0)
                x_low(KC8, lambda k: vec(key("pre_mix_g"), k))
                if l == 0:
                    split_ahead(1)
                    angles()
                for nb in range(5):
                    st["unit"] += 2
                    split_ahead(1)
                split_ahead()
                dve.wait_ge(tables_in, 32)
                dve.wait_ge(acc_out, seen(acc_out, 5))
                dve.wait_ge(zc2_done, seen(zc2_done))
                heads = z[:, :, 0:ROPE_UNITS * HD].rearrange("p t (u d) -> p t u d", d=HD)
                for t in range(TT):
                    rotate(heads[:, t, :, 0:8], heads[:, t, :, 8:16], rope1[:, t, 0], rope1[:, t, 1],
                           [rt[:, a, t] for a in range(4)]).then_inc(rope_done, 1)
                pe0 = g_of["first", l, "cmp_pe"]
                for kv in range(2):
                    dve.wait_ge(ct_ready, seen(ct_ready))
                    for odd in range(2):
                        rows = slice(odd * HD, (odd + 1) * HD)
                        for g in range(GROUPS):
                            src = aux[rows, kv, g * SEQ:(g + 1) * SEQ].rearrange("p (m c i) -> p i c m", c=8, i=2)[:, odd]
                            for back in range(2):
                                pe = vecs[rows, pe0 + kv * 16 + back * 8:pe0 + kv * 16 + back * 8 + 8]
                                last = dve.tensor_tensor(x_cmp[rows, kv, back * 8:back * 8 + 8, g, :],
                                                         src[:, :, back:back + CMP_N],
                                                         pe.unsqueeze(2).broadcast_to([HD, 8, CMP_N]), ALU.add)
                    last.then_inc(xc_sum, 1)
                for kv in range(2):
                    dve.wait_ge(xc_hi, seen(xc_hi))
                    dve.tensor_tensor(x_cmp_split(xlo_flat, kv), x_cmp[:, kv].rearrange("p c g n -> p (c g n)"),
                                      x_cmp_split(xhi_flat, kv).bitcast(F32), ALU.subtract).then_inc(xc_split, 1)
                for kv in range(2):
                    st["unit"] += 2
                    split_ahead(1)
                dve.wait_ge(ws_ready, seen(ws_ready))
                for a in range(2):
                    last = dve.tensor_tensor(wsT[:, a * 4:a * 4 + 4], aux[:, a, :].rearrange("p (g s) -> p g s", g=4),
                                             keep_le.unsqueeze(1).broadcast_to([P, 4, P]), ALU.mult)
                last.then_inc(ws_out, 1)
                dve.wait_ge(small1_in, 16 * 9 * (l + 1))
                dve.wait_ge(gelu_done, seen(gelu_done))
                for t in range(TT):
                    dve.bn_stats(stat[:, t], z[:, t, V1:W1])
                dve.drain()
                for t in range(TT):
                    last = dve.bn_aggr(mean_var[:, t], stat[:, t])
                last.then_inc(ln_var, 1)
                dve.wait_ge(rstd_ready, seen(rstd_ready))
                for t in range(TT):
                    dve.tensor_scalar(z[:, t, V1:W1], z[:, t, V1:W1], mean_var[:, t, 0:1], rstd[:, 4 + t:5 + t],
                                      ALU.subtract, ALU.mult)
                dve.drain()
                v = z[:, :, V1:W1]
                dve.tensor_tensor(v, v, ln_gb[:, 0].unsqueeze(1).broadcast_to([P, TT, 512]), ALU.mult)
                dve.drain()
                dve.tensor_tensor(v, v, ln_gb[:, 1].unsqueeze(1).broadcast_to([P, TT, 512]), ALU.add).then_inc(ln_done, 1)
                dve.wait_ge(gate_done, seen(gate_done))
                dve.tensor_scalar(z[:, :, GATE1:U1], z[:, :, GATE1:U1], 0.5, 0.5, ALU.mult, ALU.add)
                dve.wait_ge(kcv_ready, seen(kcv_ready))
                dve.tensor_tensor(kcv, aux[0:CMP_N, 2, 0:256].rearrange("p (k g d) -> p k g d", k=2, g=GROUPS), cmp_b2, ALU.add)
                dve.drain()
                rotate(kcv[:, 0, :, 0:8], kcv[:, 0, :, 8:16], rope_c[:, 0], rope_c[:, 1],
                       [rt_c[:, a] for a in range(4)]).then_inc(kcv_out, 1)
                dve.wait_ge(mix_ready, seen(mix_ready))
                dve.wait_ge(gelu_done, seen(gelu_done))
                for g in range(8):
                    last = dve.scalar_tensor_tensor(
                        mlp[:, :, g * HD:(g + 1) * HD],
                        aux[:, g // 4, (g % 4) * P:(g % 4 + 1) * P].rearrange("p (t d) -> p t d", t=TT),
                        vec(key("gmlp_bs"), g), z[:, :, U1 + g * HD:U1 + (g + 1) * HD], ALU.add, ALU.mult)
                last.then_inc(gmlp_out, 1)
                dve.wait_ge(sc_ready, seen(sc_ready))
                for t in range(TT):
                    dve.tensor_tensor(ec[:, t], aux[:, 2, t * 120:(t + 1) * 120].rearrange("p (h n) -> p h n", h=HEADS),
                                      cmp_mask[:, 0, t].unsqueeze(1).broadcast_to([P, HEADS, CMP_N]), ALU.add)
                dve.drain()
                dve.tensor_reduce(cmax[:], ec, AX.X, ALU.max)
                dve.drain()
                dve.tensor_tensor(ec, ec, cmax[:].unsqueeze(3).broadcast_to([P, TT, HEADS, CMP_N]), ALU.subtract).then_inc(sc_shift, 1)
                dve.wait_ge(sc_exp, seen(sc_exp))
                for t in range(TT):
                    dve.tensor_tensor(ec[:, t], ec[:, t], cmp_mask[:, 1, t].unsqueeze(1).broadcast_to([P, HEADS, CMP_N]), ALU.mult)
                dve.drain()
                dve.tensor_reduce(esum[:, :, :, 0], ec, AX.X, ALU.add).then_inc(ec_ready, 1)
                dve.drain()
                gate = z[:, :, GATE1:U1].rearrange("p t (h b) -> p t h b", b=3)

                def gate_factor(b0, b1):
                    s, f = esum[:, :, :, b0:b1], factor[:, :, :, b0:b1]
                    dve.tensor_scalar(s, s, 1e-30, None, ALU.max)
                    dve.drain()
                    dve.reciprocal(f, s)
                    dve.drain()
                    dve.tensor_tensor(f, f, gate[:, :, :, b0:b1], ALU.mult)
                    dve.drain()

                def heads_of(ap):
                    return ap.rearrange("p (h d) -> p h d", d=HD)

                def factor_of(t, b):
                    return factor[:, t, :, b:b + 1].broadcast_to([P, HEADS, HD])

                gate_factor(0, 1)
                dve.wait_ge(cpv_done, seen(cpv_done))
                for t in range(TT):
                    last = dve.tensor_tensor(heads_of(attn[:, t]), heads_of(aux[:, 3 - t]), factor_of(t, 0), ALU.mult)
                last.then_inc(cmp_out, 1)
                attention(first_steps(), lambda b: lanes_of(pT[:, b]))
                gate_factor(1, 3)
                for t in range(TT):
                    for b in range(2):
                        o = heads_of(aux[:, (1 + b, (3, 0)[b])[t]])
                        dve.tensor_tensor(heads_of(part[:, b]), o, factor_of(t, 1 + b), ALU.mult)
                    dve.drain()
                    dve.tensor_tensor(attn[:, t], attn[:, t], part[:, 0], ALU.add)
                    dve.drain()
                    last = dve.tensor_tensor(attn[:, t], attn[:, t], part[:, 1], ALU.add)
                    if t == 0:
                        dve.drain()
                last.then_inc(mixed_ready, 1)
                split_ahead()
                seen(sumsq_ready, 2 * TT)
                dve.wait_ge(rstd_ready, seen(rstd_ready))
                normalize(lambda t: attn[:, t], 512)
                normalize(lambda t: mlp[:, t], 512, at=2, to=512).then_inc(normed_ready, 1)
                x_low(KC8, lambda k: vec(key("attn_out_g"), k) if k < 4 else vec(key("mlp_out_g"), k - 4))
                dve.wait_ge(post_in, 32 * (l + 1))
                st["unit"] += 2
                split_ahead(1)
                for t in range(TT):
                    gained(0, t, 0)
                st["unit"] += 2
                split_ahead(1)
                for t in range(TT):
                    gained(0, t, 1)
                residual()
                norm_of_h()
                split_ahead()
                x_low(KC8, lambda k: vec(key("pre_ffn_g"), k))
                ffn_steps("first", l)
                for t in range(TT):
                    for b in range(2):
                        gained(1, t, b)
                residual()
                seen(sumsq_ready, TT), seen(rstd_ready)
                x_low(KC8, lambda k: vec(key("ple_norm_g"), k))
                for nb in range(2):
                    st["unit"] += 2
                    split_ahead(1)
                x_low(2, None)
                st["unit"] += 1
                for nb in range(2):
                    if nb == 0:
                        dve.wait_ge(half_done, seen(half_done))
                    else:
                        dve.wait_ge(unit_done, st["unit"])
                    cols = slice(nb * BLK, (nb + 1) * BLK)
                    dve.tensor_tensor(normed[:, :, cols], acc[:, :, nb, :], ple_gate[:, :, cols], ALU.mult).then_inc(acc_out, 1)
                    dve.drain()
                    dve.tensor_tensor(h[:, :, cols], h[:, :, cols], normed[:, :, cols], ALU.add).then_inc(h_ready, 1)
                seen(acc_out, 2 * 2 + 2 + 2)
                split_ahead()

            for l in range(DEPTH):
                key = lambda name: ("second", l, name)

                def gated(nb, b, first):
                    st["unit"] += 1
                    split_ahead(1)
                    dve.wait_ge(unit_done, st["unit"])
                    cols = slice(nb * BLK, (nb + 1) * BLK)
                    if first:
                        dve.tensor_tensor(merged[:, :, cols], acc[:, :, nb, :], gates[:, :, b, cols], ALU.mult).then_inc(acc_out, 1)
                    else:
                        tmp = o_gla
                        dve.tensor_tensor(tmp, acc[:, :, nb, :], gates[:, :, b, cols], ALU.mult).then_inc(acc_out, 1)
                        dve.drain()
                        dve.tensor_tensor(merged[:, :, cols], merged[:, :, cols], tmp, ALU.add)
                        dve.drain()

                seen(sumsq_ready, TT), seen(rstd_ready)
                split_ahead(0)
                x_low(KC8, lambda k: vec(key("norm_pre_mix_2"), k))
                for nb in range(6):
                    st["unit"] += 2
                    split_ahead(1)
                split_ahead()

                def gate_block():
                    st["unit"] += 2
                    split_ahead(1)

                seen(sumsq_ready, 2 * TT)
                dve.wait_ge(rstd_ready, seen(rstd_ready))
                for t in range(TT):
                    dve.tensor_scalar(z[:, t, CQ:CKV], z[:, t, CQ:CKV], mix_rstd[:, t:t + 1], None, ALU.mult)
                    last = dve.tensor_scalar(z[:, t, CKV:KR], z[:, t, CKV:KR], mix_rstd[:, 2 + t:3 + t], None, ALU.mult)
                last.then_inc(normed_ready, 1)
                gate_block()
                dve.wait_ge(yp_hi, seen(yp_hi))
                for g in range(4):
                    last = dve.scalar_tensor_tensor(ylo[:, g], aux[:, 2 + g // 2, (g % 2) * SEQ:(g % 2 + 1) * SEQ],
                                                    vec(key("pool_scale_2"), g), yhi[:, g].bitcast(F32), ALU.mult, ALU.subtract)
                last.then_inc(yp_split, 1)
                gate_block()
                dve.wait_ge(la_pre, seen(la_pre))
                dve.tensor_tensor(la, aux[:, 1, :].rearrange("p (t n) -> p t n", t=TT),
                                  b_gla.unsqueeze(1).broadcast_to([P, TT, 256]), ALU.add).then_inc(la_x, 1)
                dve.wait_ge(acc_out, seen(acc_out, 6 + 2))
                gated(0, 0, True)
                dve.wait_ge(la_ln, seen(la_ln))
                dve.scalar_tensor_tensor(la, la, 0.0, e_cum, ALU.min, ALU.subtract).then_inc(la_ready, 1)
                gated(1, 0, True)
                split_ahead()
                seen(acc_out, 2)
                dve.memset(attM.rearrange("p t h s -> p (t h s)"), 0.0)
                dve.wait_ge(exps_ready, seen(exps_ready))
                q, k = z[:, :, GQ:GK], z[:, :, GK:GV]
                dve.scalar_tensor_tensor(q, q, 64 ** -0.5, e_cum, ALU.mult, ALU.mult)
                dve.tensor_tensor(e_inv, k, e_inv, ALU.mult)
                dve.tensor_tensor(e_suf, k, e_suf, ALU.mult).then_inc(qk_dec, 1)
                gate_block()
                gate_block()
                dve.wait_ge(att_ready, seen(att_ready))
                for t in range(TT):
                    last = dve.copy_predicated(attM[:, t], chunk_le.bitcast(I32).unsqueeze(1).broadcast_to([P, 4, P]),
                                               acc[:, t, 0].rearrange("p (h s) -> p h s", h=4))
                last.then_inc(att_out, 1)
                dve.wait_ge(kv_ready, seen(kv_ready))
                kv = [aux[0:HD, n, :].rearrange("p (h e) -> p h e", h=4) for n in range(3)]
                dve.tensor_copy(state[:, 0], kv[0])
                dve.drain()
                for n in (1, 2):
                    for hd in range(4):
                        last = dve.scalar_tensor_tensor(state[:, n, hd], state[:, n - 1, hd], decay[:, hd, n:n + 1],
                                                        kv[n][:, hd], ALU.mult, ALU.add)
                    if n == 1:
                        dve.drain()
                last.then_inc(states_ready, 1)
                gate_block()
                dve.wait_ge(sq_out, seen(sq_out))
                dve.tensor_reduce(ssq[:, 0:8], sq_gla.rearrange("p t (h e) -> p (t h) e", h=4), AX.X, ALU.add).then_inc(sumsq_ready, 1)
                seen(sumsq_ready)
                x_low(5, lambda k: vec(key("mla_q_norm_2"), k) if k < 3 else vec(key("mla_kv_norm_2"), k - 3),
                      xhi=yhi, xlo=ylo)
                dve.wait_ge(rstd_ready, seen(rstd_ready))
                for t in range(TT):
                    dve.tensor_tensor(o_gla[:, t].rearrange("p (h e) -> p h e", h=4), acc[:, t, 1].rearrange("p (h e) -> p h e", h=4),
                                      mix_rstd[:, t * 4:t * 4 + 4].unsqueeze(2).broadcast_to([P, 4, P]), ALU.mult)
                dve.drain()
                dve.wait_ge(og_silu, seen(og_silu))
                dve.tensor_tensor(normed[:, :, 0:512], o_gla, z[:, :, GR:GA], ALU.mult).then_inc(normed_ready, 1)
                gate_block()
                split_ahead()
                x_low(4, lambda k: vec(key("gla_norm_2"), k))
                nflat = normed[:].rearrange("p t n -> p (t n)")
                kr = z[:, :, KR:Z2]
                dve.wait_ge(trig_done, 1)
                small = [nflat[:, 1024 + a * 32:1056 + a * 32].rearrange("p (t f) -> p t f", t=TT) for a in range(4)]
                rotate(kr[:, :, 0:16], kr[:, :, 16:32], rope2[:, 0], rope2[:, 1], small)
                dve.drain()
                for nb in range(2):
                    st["unit"] += 1
                    split_ahead(1)
                st["unit"] += 1
                split_ahead(1)
                split_ahead()
                dve.wait_ge(acc_out, seen(acc_out, 4 + 2 + 2))
                big = [nflat[:, a * 256:(a + 1) * 256].rearrange("p (t h f) -> p t h f", t=TT, h=HEADS) for a in range(4)]
                cos, sin = (rope2[:, a].unsqueeze(2).broadcast_to([P, TT, HEADS, 16]) for a in range(2))
                rotate(qf[:, :, :, 64:80], qf[:, :, :, 80:96], cos, sin, big)
                dve.tensor_copy(kf[:, :, :, 64:96], kr.unsqueeze(2).broadcast_to([P, TT, HEADS, 32])).then_inc(mrope_done, 1)
                for nb in range(2):
                    gated(nb, 1, False)
                split_ahead()
                seen(acc_out, 2)
                attention(second_steps(), lambda b: lanes_of(m_pT[:, b]))
                dve.reciprocal(m_sum[:], m_sum[:])
                dve.drain()
                for t in range(TT):
                    last = dve.tensor_tensor(normed[:, t, 512:1024].rearrange("p (h d) -> p h d", d=HD),
                                             aux[:, 1 + t].rearrange("p (h d) -> p h d", d=HD),
                                             m_sum[:, t].unsqueeze(2).broadcast_to([P, HEADS, HD]), ALU.mult)
                last.then_inc(normed_ready, 1)
                x_low(4, None)
                for nb in range(2):
                    gated(nb, 2, False)
                dve.drain().then_inc(normed_ready, 1)
                split_ahead()
                x_low(KC8, None)
                dve.wait_ge(post_in, 32 * (DEPTH + l + 1))
                st["unit"] += 2
                split_ahead(1)
                for t in range(TT):
                    gained(0, t, 0)
                st["unit"] += 2
                split_ahead(1)
                for t in range(TT):
                    gained(0, t, 1)
                residual()
                norm_of_h()
                split_ahead()
                x_low(KC8, lambda k: vec(key("norm_pre_ffn_2"), k))
                ffn_steps("second", l)
                for t in range(TT):
                    for b in range(2):
                        gained(1, t, b)
                residual()
                seen(acc_out, 2 + 2 * 2)

        @block.tensor
        def _(pe):
            seen = Seen()
            st = {"unit": 0}
            out_n = {"n": 0}

            def weights(u):
                return whi[:, u % RING], wlo[:, u % RING]

            def three(o, xs, ws, start, stop, **kw):
                (xh, xl), (wh, wl) = xs, ws
                for n, (x, w) in enumerate(((xh, wh), (xh, wl), (xl, wh))):
                    last = pe.matmul(o, x, w, start=start and n == 0, stop=stop and n == 2, **kw)
                return last

            def project(blocks, x=(xhi, xlo), bank=0, pairs=None, tiles_apart=False):
                base = out_n["n"]
                pe.wait_ge(acc_out, base) if base else None
                for i, unit_cols in enumerate(blocks):
                    if i >= 2:
                        pe.wait_ge(acc_out, base + i - 1)
                    nks = sum(kc for kc, n in unit_cols)
                    k = 0
                    for kc, n in unit_cols:
                        u = st["unit"]
                        pe.wait_ge(lo_ready, u + 1)
                        wh, wl = weights(u)
                        apart = tiles_apart and i == len(blocks) - 1 and k + kc == nks
                        order = ([(c, t) for t in range(TT) for c in range(kc)] if apart
                                 else [(c, t) for c in range(kc) for t in range(TT)])
                        for c, t in order:
                            if i == 0 and pairs and (k + c) % 2 == 0 and t == 0:
                                pe.wait_ge(pairs, seen(pairs))
                            rows = slice(t * P, (t + 1) * P)
                            last = three(acc[:, t, (i + bank) % 2, 0:n], (x[0][:, k + c, rows], x[1][:, k + c, rows]),
                                         (wh[:, c * n:(c + 1) * n], wl[:, c * n:(c + 1) * n]),
                                         k + c == 0, k + c == nks - 1, skip_group_check=True)
                            if apart and (c, t) == (kc - 1, 0):
                                last.then_inc(tile_done, 1)
                        last.then_inc(unit_done, 1)
                        st["unit"] += 1
                        k += kc
                out_n["n"] += len(blocks)

            def two_blocks_unit(at, pairs, x=(xhi, xlo), blocks_apart=False):
                pe.wait_ge(acc_out, out_n["n"])
                u = st["unit"]
                pe.wait_ge(lo_ready, u + 1)
                wh, wl = weights(u)
                if pairs:
                    pe.wait_ge(pairs, seen(pairs))
                for nb in range(2):
                    for c in range(2):
                        cols = slice(c * DM + nb * BLK, c * DM + (nb + 1) * BLK)
                        for t in range(TT):
                            rows = slice(t * P, (t + 1) * P)
                            last = three(acc[:, t, nb, :], (x[0][:, at + c, rows], x[1][:, at + c, rows]),
                                         (wh[:, cols], wl[:, cols]), c == 0, c == 1, skip_group_check=True)
                    if blocks_apart and nb == 0:
                        last.then_inc(half_done, 1)
                last.then_inc(unit_done, 1)
                st["unit"] += 1
                out_n["n"] += 2

            def turn(src, nk, at=0):
                for k in range(0, nk, 2):
                    n = turned["n"]
                    if n >= 2:
                        pe.wait_ge(x_split, n - 1)
                    for j in range(min(2, nk - k)):
                        for t in range(TT):
                            c0 = at + (k + j) * P
                            last = pe.transpose(aux[:, n % 2, j * SEQ + t * P:j * SEQ + (t + 1) * P],
                                                src[:, t, c0:c0 + P], ident)
                    last.then_inc(tp_ready, 1)
                    turned["n"] += 1

            turned = {"n": 0}

            def full(nblocks, nunits_kc=4):
                return [[(4, BLK), (4, BLK)] for _ in range(nblocks)]

            def ffn_steps(which, l):
                u0 = ffn[which, l][0]
                fs0 = seen.now(f_split)
                pe.wait_ge(acc_out, out_n["n"])

                def up(j_unit, u, par):
                    for part in range(2):
                        pe.wait_ge(lo_ready, j_unit + (part + 1))
                        wh, wl = weights(u + part)
                        for c2 in range(2):
                            for k in range(KC8):
                                cols = slice(k * FB + c2 * P, k * FB + (c2 + 1) * P)
                                for n, (w, x) in enumerate(((wh, xhi), (wh, xlo), (wl, xhi))):
                                    last = pe.matmul(aux[:, 2 * par + part, c2 * SEQ:(c2 + 1) * SEQ], w[:, cols], x[:, k],
                                                     start=(k == 0 and n == 0), stop=(k == KC8 - 1 and n == 2),
                                                     skip_group_check=True)
                        last.then_inc(unit_done if part == 0 else gu_ready, 1)

                def down(j, j_unit, u, par, announce, stop=False):
                    pe.wait_ge(lo_ready, j_unit + 1)
                    pe.wait_ge(f_split, j + (fs0 + 1))
                    wh, wl = weights(u)
                    for t in range(TT):
                        rows = slice(t * P, (t + 1) * P)
                        for c2 in range(2):
                            for n, (x, w) in enumerate(((fhi, wh), (fhi, wl), (flo, wh))):
                                for nb in range(2):
                                    cols = slice(c2 * DM + nb * BLK, c2 * DM + (nb + 1) * BLK)
                                    last = pe.matmul(acc[:, t, nb, :], x[:, par, c2, rows], w[:, cols], start=False,
                                                     stop=stop and c2 == 1 and n == 2, skip_group_check=True)
                                    if announce and c2 == 0 and t == 0 and n == 0 and nb == 0:
                                        last.then_inc(unit_done, 1)
                        if stop and t == 0:
                            last.then_inc(tile_done, 1)
                    last.then_inc(unit_done, 1)

                for p in range(KC8 // 2):
                    pe.wait_ge(x_split, seen(x_split))
                up(u0, u0, 0)
                for t in range(TT):
                    for nb in range(2):
                        last = pe.matmul(acc[:, t, nb, :], zero_row[:, 0:P], zero_row[:], start=True, stop=False,
                                         skip_group_check=True)
                last.then_inc(unit_done, 1)
                with pe.Fori(0, FSTEPS // 2) as i:
                    for s in range(2):
                        first = u0 + 2 + 3 * s
                        up(i * 6 + first, first, (1 + s) % 2)
                        down(i * 2 + s, i * 6 + (first + 2), first + 2, s, True)
                down(FSTEPS - 1, u0 + FUNITS - 1, u0 + FUNITS - 1, (FSTEPS - 1) % 2, False, True)
                seen(f_split, FSTEPS)
                st["unit"] = u0 + FUNITS
                out_n["n"] += 2

            def attention(steps, e, pt):
                b_e, b_pts, b_dve = seen.now(e_ready), seen.now(pts_ready), seen.now(pts_ready_dve)
                n = len(steps)
                for i in range(n + 2):
                    if i < n:
                        if i >= 2:
                            pe.wait_ge(e_ready, b_e + i - 1)
                        nk = steps[i]["nk"]
                        for a, lane in enumerate(steps[i]["lanes"]):
                            last = pe.matmul(acc[:, 0, i % 2, a * 256:a * 256 + nk], lane["q"], lane["k"][:, 0:nk],
                                             start=True, stop=True)
                        last.then_inc(s_ready, 1)
                    j = i - 1
                    if 0 <= j < n:
                        pe.wait_ge(e_ready, b_e + j + 1)
                        for a in range(2):
                            for kt in range(steps[j]["nk"] // P):
                                c0 = a * 256 + kt * P
                                last = pe.transpose(acc[:, 1, j % 2, c0:c0 + P], e[:, j % 2, c0:c0 + P], ident)
                        last.then_inc(pt_ready, 1)
                    j = i - 2
                    if 0 <= j < n:
                        if j % 2 == 0:
                            pe.wait_ge(pts_ready, b_pts + j // 2 + 1)
                        else:
                            pe.wait_ge(pts_ready_dve, b_dve + j // 2 + 1)
                        nkt = steps[j]["nk"] // P
                        for a, lane in enumerate(steps[j]["lanes"]):
                            for kt in range(nkt):
                                last = pe.matmul(lane["o"], pt(j % 2)[:, a, kt * P:(kt + 1) * P], lane["v"][:, kt],
                                                 start=(kt == 0), stop=(kt == nkt - 1))
                        last.then_inc(pv_done, 1)
                seen(e_ready, n), seen(pts_ready, n // 2), seen(pts_ready_dve, n // 2)

            pe.wait_ge(masks_in, 16)
            pe.wait_ge(setup_done, 2)

            for l in range(DEPTH):
                if l:
                    pe.wait_ge(h_ready, 3 * TT * l)
                else:
                    pe.wait_ge(h_in, 16)
                turn(h, KC8)
                project([[(4, n), (4, n)] for c0, n in blocks_of(0, W1)], pairs=x_split)
                pe.wait_ge(acc_out, out_n["n"])
                pe.wait_ge(zc2_done, seen(zc2_done))
                for kv in range(2):
                    for g in range(GROUPS):
                        for t in range(TT):
                            last = pe.transpose(aux[:, kv, g * SEQ + t * P:g * SEQ + (t + 1) * P],
                                                zc2[:, t, kv * 2 + g].rearrange("p a d -> p (a d)"), ident)
                    last.then_inc(ct_ready, 1)
                pe.wait_ge(rope_done, seen(rope_done, TT))
                for i in range(6):
                    if i >= 2:
                        pe.wait_ge(qk_out, seen(qk_out))
                    t, which = i % 2, i // 2
                    for j in range(4):
                        c0 = (which * 4 + j) * HD if which < 2 else 768 + (j // 2) * 256 + (j % 2) * HD
                        last = pe.transpose(aux[0:HD, 2 + i % 2, j * P:(j + 1) * P], z[:, t, c0:c0 + HD], ident)
                    last.then_inc(qk_ready, 1)
                for kv in range(2):
                    pe.wait_ge(xc_split, seen(xc_split))
                    for half in range(2):
                        u = st["unit"]
                        pe.wait_ge(lo_ready, u + 1)
                        wh, wl = weights(u)
                        xs = [x_cmp_split(f, kv).rearrange("p (c r) -> p c r", c=16) for f in (xhi_flat, xlo_flat)]
                        for c in range(8):
                            cols = slice(c * CMP_HID, (c + 1) * CMP_HID)
                            last = three(acc[0:2 * CMP_N, 0, kv, 0:CMP_HID], (xs[0][:, half * 8 + c], xs[1][:, half * 8 + c]),
                                         (wh[:, cols], wl[:, cols]), half + c == 0, half == 1 and c == 7,
                                         skip_group_check=True)
                        last.then_inc(unit_done, 1)
                        st["unit"] += 1
                pe.wait_ge(small1_in, 16 * 9 * (l + 1))
                for g in range(8):
                    last = pe.transpose(aux[:, g // 4, (g % 4) * P:(g % 4 + 1) * P], ws_raw[:, g, :], ident)
                last.then_inc(ws_ready, 1)
                pe.wait_ge(hid_out, seen(hid_out, 2))
                for kv in range(2):
                    for c2 in range(2):
                        last = pe.transpose(acc[:, 1, kv, c2 * 30:(c2 + 1) * 30], hid[:, kv, c2 * P:(c2 + 1) * P],
                                            ident[0:2 * CMP_N, 0:2 * CMP_N])
                last.then_inc(hidT_ready, 1)
                pe.wait_ge(hT_out, seen(hT_out))
                pe.wait_ge(qk_out, seen(qk_out, 2))
                for kv in range(2):
                    for g in range(GROUPS):
                        for c2 in range(2):
                            last = pe.matmul(aux[0:CMP_N, 2, (kv * 2 + g) * HD:(kv * 2 + g + 1) * HD],
                                             hT[:, kv, c2, g * CMP_N:(g + 1) * CMP_N], cmp_w2[:, kv, c2, :],
                                             start=(c2 == 0), stop=(c2 == 1))
                last.then_inc(kcv_ready, 1)
                pe.wait_ge(ws_out, seen(ws_out))
                pe.wait_ge(ln_done, seen(ln_done))
                for g in range(8):
                    last = pe.matmul(aux[:, g // 4, (g % 4) * P:(g % 4 + 1) * P], wsT[:, g, :],
                                     z[:, :, V1 + g * HD:V1 + (g + 1) * HD], start=True, stop=True)
                last.then_inc(mix_ready, 1)
                pe.wait_ge(kcv_out, seen(kcv_out))
                for g in range(GROUPS):
                    last = pe.transpose(aux[0:HD, 3, g * CMP_N:(g + 1) * CMP_N], kcv[:, 0, g, :], ident[0:CMP_N, 0:CMP_N])
                last.then_inc(kcT_ready, 1)
                pe.wait_ge(kcT_out, seen(kcT_out))
                for t in range(TT):
                    for hd in range(HEADS):
                        c0 = (t * HEADS + hd) * CMP_N
                        last = pe.matmul(aux[:, 2, c0:c0 + CMP_N], qT[:, hd, t * P:(t + 1) * P], kcT[:, hd // 4, :],
                                         start=True, stop=True)
                last.then_inc(sc_ready, 1)
                pe.wait_ge(ec_ready, seen(ec_ready))
                for t in range(TT):
                    for hd in range(HEADS):
                        last = pe.transpose(acc[0:CMP_N, t, hd // 4, (hd % 4) * P:(hd % 4 + 1) * P], ec[:, t, hd, :], ident)
                last.then_inc(ect_ready, 1)
                pe.wait_ge(ect_out, seen(ect_out))
                for t in range(TT):
                    for hd in range(HEADS):
                        last = pe.matmul(aux[:, 3 - t, hd * HD:(hd + 1) * HD], ecT[:, t, hd, :], kcv[:, 1, hd // 4, :],
                                         start=True, stop=True)
                last.then_inc(cpv_done, 1)
                pe.wait_ge(cmp_out, seen(cmp_out))
                pe.wait_ge(gmlp_out, seen(gmlp_out))
                attention(first_steps(), e_buf, lambda b: lanes_of(pT[:, b]))
                pe.wait_ge(normed_ready, seen(normed_ready))
                turn(normed, KC8)
                project(full(2), pairs=x_split, tiles_apart=True)
                pe.wait_ge(normed_ready, seen(normed_ready, 2))
                turn(normed, KC8)
                ffn_steps("first", l)
                pe.wait_ge(h_ready, (3 * l + 2) * TT)
                turn(h, KC8)
                project(full(2), pairs=x_split)
                turn(p_in, 2)
                two_blocks_unit(0, x_split, blocks_apart=True)

            for l in range(DEPTH):
                pe.wait_ge(h_ready, (3 * DEPTH + 2 * l) * TT)
                turn(h, KC8)
                project([[(4, n), (4, n)] for c0, n in blocks_of(0, Z2)], pairs=x_split)

                def gate_block(bank=0):
                    project(full(1), bank=bank)

                pe.wait_ge(acc_out, out_n["n"])
                pe.wait_ge(pool_in, 32 * (l + 1))
                for g in range(4):
                    for s in range(TT):
                        last = pe.matmul(aux[:, g // 2, (g % 2) * SEQ:(g % 2 + 1) * SEQ], z[:, s, g * P:(g + 1) * P],
                                         pool_mat[:, s, g, :], start=(s == 0), stop=(s == 1))
                last.then_inc(diff_ready, 1)
                gate_block()
                pe.wait_ge(diff_out, seen(diff_out))
                for g in range(4):
                    last = pe.matmul(aux[:, 2 + g // 2, (g % 2) * SEQ:(g % 2 + 1) * SEQ], w_pool[:, g, :], diffT[:, g, :],
                                     start=True, stop=True)
                last.then_inc(ypool_ready, 1)
                for t in range(TT):
                    last = pe.transpose(aux[0:16, 0, t * P:(t + 1) * P], z[:, t, GA:CQ], ident)
                last.then_inc(a1_ready, 1)
                gate_block()
                pe.wait_ge(a1_out, seen(a1_out))
                pe.wait_ge(small2_in, 32 * (l + 1))
                for t in range(TT):
                    last = pe.matmul(aux[:, 1, t * 256:(t + 1) * 256], a1T[:, t * P:(t + 1) * P], w_a2, start=True, stop=True)
                last.then_inc(la_pre, 1)
                pe.wait_ge(yp_split, seen(yp_split))
                project([[(4, BLK)], [(4, BLK)]], x=(yhi, ylo))
                pe.wait_ge(la_ready, seen(la_ready))
                for i, mat in enumerate((chunk_le, chunk_gt)):
                    for t in range(TT):
                        pe.matmul(aux[:, i, t * 256:(t + 1) * 256], mat, la[:, t], start=True, stop=True)
                for hd in range(4):
                    for t in range(TT):
                        last = pe.matmul(aux[0:HD, 2, hd * 4 + t * 2:hd * 4 + t * 2 + 2], la[:, t, hd * HD:(hd + 1) * HD],
                                         chunk_of, start=True, stop=True)
                last.then_inc(cum_ready, 1)
                gate_block()
                pe.wait_ge(qk_dec, seen(qk_dec))
                for i in range(4):
                    src = z[:, i % 2, GQ:GK] if i < 2 else e_inv[:, i % 2]
                    for hd in range(4):
                        last = pe.transpose(aux[0:HD, i, hd * P:(hd + 1) * P], src[:, hd * HD:(hd + 1) * HD], ident)
                    last.then_inc(gT_ready, 1)
                gate_block(bank=1)
                pe.wait_ge(gT_out, seen(gT_out, 4))
                for t in range(TT):
                    rows = slice(t * P, (t + 1) * P)
                    for hd in range(4):
                        last = pe.matmul(acc[:, t, 0, hd * P:(hd + 1) * P], kiT[:, hd, rows], qdT[:, hd, rows], start=True, stop=True)
                last.then_inc(att_ready, 1)
                for n in range(3):
                    rows = slice((n % 2) * 64, (n % 2 + 1) * 64)
                    for hd in range(4):
                        last = pe.matmul(aux[0:HD, n, hd * P:(hd + 1) * P], e_suf[rows, n // 2, hd * HD:(hd + 1) * HD],
                                         z[rows, n // 2, GV + hd * P:GV + (hd + 1) * P], start=True, stop=True)
                last.then_inc(kv_ready, 1)
                pe.wait_ge(att_out, seen(att_out))
                gate_block()
                pe.wait_ge(states_ready, seen(states_ready))
                for t in range(TT):
                    for hd in range(4):
                        cols = slice(hd * P, (hd + 1) * P)
                        pe.matmul(acc[:, t, 1, cols], attM[:, t, hd, :], z[:, t, GV + hd * P:GV + (hd + 1) * P],
                                  start=True, stop=False, skip_group_check=True)
                        for c in range(2):
                            n = 2 * t + c
                            if n:
                                last = pe.matmul(acc[c * 64:(c + 1) * 64, t, 1, cols], qdT[:, hd, n * 64:(n + 1) * 64],
                                                 state[:, n - 1, hd, :], start=False, stop=True, skip_group_check=True)
                last.then_inc(og_ready, 1)
                pe.wait_ge(normed_ready, seen(normed_ready))
                turn(z, 5, at=CQ)
                gate_block()
                pe.wait_ge(normed_ready, seen(normed_ready))
                turn(normed, 4)
                project([[(3, 384)], [(3, 384)]], x=(yhi, ylo), pairs=x_split)
                two_blocks_unit(3, x_split, x=(yhi, ylo))
                project([[(4, BLK)], [(4, BLK)]], pairs=x_split)
                pe.wait_ge(mrope_done, seen(mrope_done))
                for i in range(8):
                    if i >= 4:
                        pe.wait_ge(mT_out, seen(mT_out))
                    t, hg, which = i % 2, i // 2 % 2, i // 4
                    for j in range(4):
                        last = pe.transpose(aux[0:QK, i % 4, j * P:(j + 1) * P], (qf, kf)[which][:, t, hg * 4 + j, :], ident)
                    last.then_inc(mT_ready, 1)
                pe.wait_ge(mT_out, seen(mT_out, 4))
                pe.wait_ge(acc_out, out_n["n"])
                attention(second_steps(), m_e, lambda b: lanes_of(m_pT[:, b]))
                pe.wait_ge(normed_ready, seen(normed_ready))
                turn(normed, 4, at=512)
                project([[(4, BLK)], [(4, BLK)]], pairs=x_split)
                pe.wait_ge(normed_ready, seen(normed_ready))
                turn(merged, KC8)
                project(full(2), pairs=x_split, tiles_apart=True)
                pe.wait_ge(normed_ready, seen(normed_ready, 2))
                turn(normed, KC8)
                ffn_steps("second", l)


def shape_constants():
    import numpy as np
    f = np.float32
    i = np.arange(P)
    c = {}
    same = (i[:, None] // 64) == (i[None, :] // 64)
    tok = np.arange(SEQ).reshape(TT, P)
    ok = (16 * np.arange(CMP_N) + 31)[None, None, :] <= tok.T[:, :, None]
    c["c_masks"] = np.concatenate([
        np.eye(P), np.where(i[None, :] <= i[:, None], 0, NEG), i[:, None] <= i[None, :],
        same & (i[:, None] <= i[None, :]), same & (i[:, None] > i[None, :]),
        (i[:, None] // 64) == np.arange(2)[None, :], np.where(ok, 0, NEG).reshape(P, -1), ok.reshape(P, -1)],
        axis=1).astype(f)
    inv = (f(500000.0) ** (-np.arange(8, dtype=f) / f(8))).astype(f)

    def table(pos):
        ang = pos.astype(f)[:, None] * inv[None, :]
        return np.cos(ang).astype(f), np.sin(ang).astype(f)

    cos, sin = table(np.arange(SEQ))
    t = np.zeros((P, 2, TT, ROPE_UNITS, 8), f)
    t[:, 0] = 1
    for u in list(range(8)) + [12, 13, 16, 17]:
        t[:, 0, :, u] = cos.reshape(TT, P, 8).transpose(1, 0, 2)
        t[:, 1, :, u] = sin.reshape(TT, P, 8).transpose(1, 0, 2)
    c["c_rope1"] = np.ascontiguousarray(t.transpose(0, 2, 1, 3, 4).reshape(P, TT, 320))
    cos, sin = table(np.arange(CMP_N) * 16 + 31)
    c["c_rope_c"] = np.ascontiguousarray(np.stack([np.stack([x, x], 1) for x in (cos, sin)], 1))
    c["c_inv_freq"] = (f(10000.0) ** (-np.arange(0, 32, 2, dtype=f) / f(32))).astype(f)
    s = np.arange(SEQ)
    mats = []
    for w in (2, 4, 8, 16):
        m = ((s[None, :] <= s[:, None]) & (s[None, :] > s[:, None] - w)) / np.minimum(s + 1, w)[:, None] - np.eye(SEQ)
        mats.append(m.T.astype(f))
    c["c_pool"] = np.ascontiguousarray(np.stack(mats, 1).reshape(TT, P, 4, SEQ).transpose(1, 0, 2, 3))
    return c


def kernel(**inputs):
    import numpy as np
    import concourse.bacc as bacc
    from concourse.bass_utils import run_bass_kernel_spmd as run

    arrays = {}
    for name, a in inputs.items():
        a = np.ascontiguousarray(a)
        if name == "x":
            a = a[0]
        elif name == "positions_2":
            a = a[0].reshape(TT, P).T
        elif name == "p":
            a = a[:, 0]
        arrays[name] = a
    rows = [arrays[name].reshape(DEPTH, n, P)[l] for names in (VECS1, VECS2) for l in range(DEPTH) for name, n in names]
    arrays["vecs"] = np.concatenate(rows, axis=0).T
    for name, _ in VECS1 + VECS2:
        del arrays[name]
    arrays.update(shape_constants())
    nc = bacc.Bacc("TRN2", target_bir_lowering=False, num_devices=1)
    A = {}
    feed = {}
    for name, a in arrays.items():
        feed["in_" + name] = np.ascontiguousarray(a)
        A[name] = nc.dram_tensor("in_" + name, a.shape, mybir.dt.from_np(a.dtype), kind="ExternalInput").ap()
    out = nc.dram_tensor("out_h", (SEQ, DM), F32, kind="ExternalOutput").ap()
    two_blocks(nc, A, out)
    r = run(nc, [feed], core_ids=[0])
    return r.results[0]["out_h"].reshape(1, SEQ, DM)
```

```python
import concourse.bass as bass
from concourse import mybir
from contextlib import ExitStack

F32 = mybir.dt.float32
F32R = mybir.dt.float32r
I32 = mybir.dt.int32
ALU = mybir.AluOpType
ACT = mybir.ActivationFunctionType
AX = mybir.AxisListType

P = 128
SEQ, DM, DEPTH = 256, 1024, 2
TT = SEQ // P
EPS = 1e-6
NEG = -1e30
BLK = 512
UNIT = 2048
RING = 3
KC8 = DM // P

HEADS, HD, GROUPS = 8, 64, 2
W1 = 2328
GATE1, U1, V1 = 1280, 1304, 1816
CMP_N, CMP_HID = 15, 256
ROPE_UNITS = 20
W2 = 5808
Z2 = 2736
GQ, GK, GV, GR, GA, CQ, CKV, KR = 512, 768, 1024, 1536, 2048, 2064, 2448, 2704
QK = 96
D_FF = 2816
FB = 256
FSTEPS = D_FF // FB
FUNITS = 3 * FSTEPS
FLOOP = (FSTEPS - 3) // 2
VECS1 = (("pre_mix_g", 8), ("attn_out_g", 4), ("mlp_out_g", 4), ("pre_ffn_g", 8), ("ple_norm_g", 8),
         ("cmp_pe", 32), ("cmp_b1", 4), ("gmlp_bs", 8), ("conv_b", 44), ("conv_w", 132))
VECS2 = (("norm_pre_mix_2", 8), ("norm_pre_ffn_2", 8), ("pool_scale_2", 4), ("gla_norm_2", 4),
         ("mla_q_norm_2", 3), ("mla_kv_norm_2", 2))
NVECS = DEPTH * sum(n for _, n in VECS1 + VECS2)
SMALL1 = 9
MASK_COLS = 5 * P + 2 + 2 * TT * CMP_N


class Seen:

    def __init__(self):
        self.n = {}

    def __call__(self, sem, k=1):
        self.n[id(sem)] = self.n.get(id(sem), 0) + k
        return self.n[id(sem)]

    def now(self, sem):
        return self.n.get(id(sem), 0)


W1_BLOCKS = ((V1, W1 - V1), (0, BLK), (BLK, BLK), (2 * BLK, U1 - 2 * BLK), (U1, V1 - U1))


def blocks_of(lo, hi):
    return [(a, min(BLK, hi - a)) for a in range(lo, hi, BLK)]


def unit_plan():
    units, ffn = [], {}

    def matrix(name, at, nk, blocks, k_starts=(0, 4)):
        for c0, n in blocks:
            for k0 in [k for k in k_starts if k < nk]:
                units.append((name, at, k0 * P, c0, min(4, nk - k0), n))

    def ffn_units(which, l, up, down):
        ffn[which, l] = len(units)

        def hidden(j):
            return [(up, (l,), 0, part * D_FF + j * FB, KC8, FB) for part in range(2)]

        units.extend(hidden(0) + hidden(1))
        for j in range(FSTEPS):
            units.extend(hidden(j + 2) if j + 2 < FSTEPS else [])
            units.append((down, (l,), j * FB, 0, FB // P, DM))

    for l in range(DEPTH):
        matrix("w_in", (l,), KC8, W1_BLOCKS)
        for kv in range(2):
            for half in range(2):
                units.append(("cmp_w1", (l, kv), half * KC8 * P, 0, KC8, CMP_HID))
        matrix("w_o", (l,), KC8, blocks_of(0, DM), k_starts=(4, 0))
        ffn_units("first", l, "w_up", "w_down")
        matrix("w_ple_gate", (l,), KC8, blocks_of(0, DM))
        units.append(("w_ple_proj", (l,), 0, 0, 2, DM))
    for l in range(DEPTH):
        gate_blocks = blocks_of(Z2, W2)
        matrix("w_in_2", (l,), KC8, blocks_of(0, Z2) + gate_blocks[0:2])
        matrix("w_a_2", (l,), 4, blocks_of(0, DM))
        matrix("w_in_2", (l,), KC8, gate_blocks[2:6])
        matrix("w_mla_uq_2", (l,), 3, [(0, 384), (384, 384)])
        units.append(("w_mla_ukv_2", (l,), 0, 0, 2, DM))
        matrix("w_b_2", (l,), 4, blocks_of(0, DM))
        matrix("w_c_2", (l,), 4, blocks_of(0, DM))
        matrix("w_o_2", (l,), KC8, blocks_of(0, DM))
        ffn_units("second", l, "w_ffn_gu_2", "w_ffn_down_2")
    return units, ffn


def two_blocks(nc, A, out):
    units, ffn = unit_plan()
    ffn_starts = sorted(ffn.values())
    size = [(kc, n) for *_, kc, n in units]
    unit_at = [0]
    for kc, n in size:
        unit_at.append(unit_at[-1] + P * kc * n)

    with ExitStack() as ctx:
        def sb(name, shape, dt=F32):
            return ctx.enter_context(nc.sbuf_tensor(name, shape, dt))

        def sem(name):
            return ctx.enter_context(nc.semaphore(name))

        raw = sb("w_raw", [P, RING, UNIT])
        whi = sb("w_hi", [P, RING, UNIT], F32R)
        wlo = sb("w_lo", [P, RING, UNIT], F32R)
        xhi = sb("x_hi", [P, KC8, SEQ], F32R)
        xlo = sb("x_lo", [P, KC8, SEQ], F32R)
        yhi = sb("y_hi", [P, 5, SEQ], F32R)
        ylo = sb("y_lo", [P, 5, SEQ], F32R)
        fhi, flo = (t[:, 0:4].rearrange("p (a c) s -> p a c s", a=2) for t in (yhi, ylo))
        h = sb("h", [P, TT, DM])
        normed = sb("normed", [P, TT, DM])
        merged = sb("merged", [P, TT, DM])
        z = sb("z", [P, TT, Z2])
        area = sb("area", [P, 12288])
        vecs = sb("vecs", [P, NVECS])
        post_g = sb("post_g", [P, 2, DM])
        masks = sb("masks", [P, MASK_COLS])
        ident = masks[:, 0:P]
        causal = masks[:, P:2 * P]
        keep_le = masks[:, 2 * P:3 * P]
        chunk_le = masks[:, 3 * P:4 * P]
        chunk_gt = masks[:, 4 * P:5 * P]
        chunk_of = masks[:, 5 * P:5 * P + 2]
        cmp_mask = (masks[:, 5 * P + 2:MASK_COLS]
                    .rearrange("p (a t n) -> p a t n", a=2, t=TT))
        trig = sb("trig", [P, 256])
        rope2 = sb("rope2", [P, 2, TT, 16])
        ssq = sb("ssq", [P, 8])
        rstd = sb("rstd", [P, 8])
        mix_rstd = sb("mix_rstd", [P, 8])
        half_neg = sb("half_neg", [P, 8])
        stat = sb("stat", [P, TT, 6])
        mean_var = sb("mean_var", [P, TT, 2])
        nmax = sb("nmax", [P, 2, 2])
        esum = sb("esum", [P, TT, HEADS, 3])
        cmax = sb("cmax", [P, TT, HEADS])
        m_sum = sb("m_sum", [P, TT, HEADS])
        zero_row = sb("zero_row", [1, BLK], mybir.dt.bfloat16)
        acc_banks = ctx.enter_context(nc.psum_tensor("acc", [P, 2, TT, BLK], F32))
        acc = acc_banks[:].rearrange("p b t n -> p t b n")
        aux = ctx.enter_context(nc.psum_tensor("aux", [P, 4, BLK], F32))

        def carve(start, n, parts=P):
            return area[0:parts, start:start + n]

        qT = carve(0, 2048, HD).rearrange("p (h s) -> p h s", h=HEADS)
        kT = carve(2048, 1024, HD).rearrange("p (u s) -> p u s", u=4)
        e_buf = carve(3072, 1024).rearrange("p (b n) -> p b n", b=2)
        pT = carve(4096, 1024).rearrange("p (b n) -> p b n", b=2)
        hid = carve(3072, 512, 2 * CMP_N).rearrange("p (k n) -> p k n", k=2)
        ecT = carve(3072, 2048, CMP_N).rearrange("p (t h q) -> p t h q", t=TT, h=HEADS)
        attn = carve(6144, 1024).rearrange("p (t n) -> p t n", t=TT)
        zc2 = carve(6144, 1024).rearrange("p (t u a d) -> p t u a d", t=TT, u=4, a=2)
        ws_raw = carve(7168, 1024).rearrange("p (g s) -> p g s", g=8)
        wsT = carve(8192, 1024).rearrange("p (g s) -> p g s", g=8)
        mlp = carve(9216, 1024).rearrange("p (t n) -> p t n", t=TT)
        x_cmp = carve(10240, 960).rearrange("p (k c g n) -> p k c g n", k=2, c=16, g=GROUPS)
        part = carve(10240, 1024).rearrange("p (a n) -> p a n", a=2)
        hT = carve(11776, 120).rearrange("p (k c n) -> p k c n", k=2, c=2)
        kcT = carve(11896, 30, HD).rearrange("p (g n) -> p g n", g=GROUPS)
        ec = carve(11264, 240).rearrange("p (t h n) -> p t h n", t=TT, h=HEADS)
        factor = carve(11936, 48).rearrange("p (t h b) -> p t h b", t=TT, h=HEADS)
        kcv = carve(12032, 256, CMP_N).rearrange("p (k g d) -> p k g d", k=2, g=GROUPS)
        ple_gate = carve(0, 2048).rearrange("p (t n) -> p t n", t=TT)
        mflat = merged[:].rearrange("p t n -> p (t n)")
        ln_gb = mflat[:, 0:1024].rearrange("p (a n) -> p a n", a=2)
        cmp_w2 = mflat[:, 1024:1280].rearrange("p (k c d) -> p k c d", k=2, c=2)
        cmp_b2 = mflat[0:CMP_N, 1280:1536].rearrange("p (k g d) -> p k g d", k=2, g=GROUPS)
        p_in = mflat[:, 1536:2048].rearrange("p (t n) -> p t n", t=TT)
        zflat = z[:].rearrange("p t n -> p (t n)")
        rope1_cols = z[:, :, W1:W1 + 320]
        rope1 = rope1_cols.rearrange("p t (a u f) -> p t a u f", a=2, u=ROPE_UNITS)
        rope_c = sb("rope_c", [CMP_N, 2, GROUPS, 8])
        rt = carve(3072, 1280).rearrange("p (a t u f) -> p a t u f", a=4, t=TT, u=ROPE_UNITS)
        rt_c = carve(11504, 64, CMP_N).rearrange("p (a g f) -> p a g f", a=4, g=GROUPS)
        gates = carve(0, 6144).rearrange("p (t b n) -> p t b n", t=TT, b=3)
        pool_mat = carve(6144, 2048).rearrange("p (s g t) -> p s g t", s=TT, g=4)
        diffT = carve(8192, 1024).rearrange("p (g t) -> p g t", g=4)
        w_pool = carve(9216, 512).rearrange("p (g d) -> p g d", g=4)
        w_a2 = carve(9728, 256, 16)
        b_gla = carve(9984, 256)
        la, e_cum, e_suf, e_inv = (normed[:].rearrange("p t n -> p (t n)")[:, i * 512:(i + 1) * 512]
                                   .rearrange("p (t n) -> p t n", t=TT) for i in range(4))
        qdT = carve(6144, 1024, HD).rearrange("p (h s) -> p h s", h=4)
        kiT = carve(7168, 1024, HD).rearrange("p (h s) -> p h s", h=4)
        attM = carve(8192, 1024).rearrange("p (t h s) -> p t h s", t=TT, h=4)
        state = carve(9216, 1536, HD).rearrange("p (n h e) -> p n h e", n=3, h=4)
        a1T = carve(10752, 256, 16)
        decay = carve(11008, 16, HD).rearrange("p (h n) -> p h n", h=4)
        o_gla = carve(11264, 1024).rearrange("p (t n) -> p t n", t=TT)
        sq_gla = carve(6144, 1024).rearrange("p (t n) -> p t n", t=TT)
        qf = zflat[:, 0:1536].rearrange("p (t h d) -> p t h d", t=TT, h=HEADS)
        kf = zflat[:, Z2:Z2 + 1536].rearrange("p (t h d) -> p t h d", t=TT, h=HEADS)
        mqT = carve(6144, 2048, QK).rearrange("p (h s) -> p h s", h=HEADS)
        mkT = carve(8192, 2048, QK).rearrange("p (h s) -> p h s", h=HEADS)
        m_v = carve(10240, 1024).rearrange("p (t h d) -> p t h d", t=TT, h=HEADS)
        m_e = carve(11264, 1024).rearrange("p (b n) -> p b n", b=2)
        m_pT = normed[:, :, 0:512]
        hc = carve(0, 2048).rearrange("p (a w c s) -> p a w c s", a=2, w=2, c=2)
        sg = carve(2048, 512).rearrange("p (c s) -> p c s", c=2)
        f_act = carve(2560, 512).rearrange("p (c s) -> p c s", c=2)

        w_loaded = [sem(f"w_loaded{i}") for i in range(RING)]
        hi_ready, lo_ready, unit_done = sem("hi_ready"), sem("lo_ready"), sem("unit_done")
        masks_in, tables_in, vecs_in, h_in, out_done = (
            sem(s) for s in ("masks_in", "tables_in", "vecs_in", "h_in", "out_done"))
        small1_in, small2_in, post_in = sem("small1_in"), sem("small2_in"), sem("post_in")
        pool_in, pos_in = sem("pool_in"), sem("pos_in")
        setup_done = sem("setup_done")
        tile_done, half_done = sem("tile_done"), sem("half_done")
        sumsq_ready, rstd_ready, normed_ready = sem("sumsq_ready"), sem("rstd_ready"), sem("normed_ready")
        tp_ready, xhi_ready, x_split = sem("tp_ready"), sem("xhi_ready"), sem("x_split")
        acc_out, h_ready = sem("acc_out"), sem("h_ready")
        zc2_done = sem("zc2_done")
        rope_done, ct_ready, xc_sum, xc_hi = (sem(s) for s in ("rope_done", "ct_ready", "xc_sum", "xc_hi"))
        xc_split, qk_ready, qk_out = sem("xc_split"), sem("qk_ready"), sem("qk_out")
        hid_out, hidT_ready = sem("hid_out"), sem("hidT_ready")
        hT_out, kcv_ready, kcv_out, kcT_ready, kcT_out = (
            sem(s) for s in ("hT_out", "kcv_ready", "kcv_out", "kcT_ready", "kcT_out"))
        ws_ready, ws_out, ln_done, mix_ready = sem("ws_ready"), sem("ws_out"), sem("ln_done"), sem("mix_ready")
        ln_var = sem("ln_var")
        sc_ready, sc_shift, sc_exp, ec_ready, ect_ready, ect_out = (
            sem(s) for s in ("sc_ready", "sc_shift", "sc_exp", "ec_ready", "ect_ready", "ect_out"))
        cpv_done, cmp_out, gmlp_out, gate_done = sem("cpv_done"), sem("cmp_out"), sem("gmlp_out"), sem("gate_done")
        s_ready, max_ready, e_ready, pt_ready, pts_ready, pts_ready_dve, pv_done, mixed_ready = (
            sem(s) for s in ("s_ready", "max_ready", "e_ready", "pt_ready", "pts_ready", "pts_ready_dve", "pv_done", "mixed_ready"))
        gu_ready, hc_ready, hc_conv, sg_ready, fa_ready, fhi_ready, f_split = (
            sem(s) for s in ("gu_ready", "hc_ready", "hc_conv", "sg_ready", "fa_ready", "fhi_ready", "f_split"))
        yp_hi, yp_split = sem("yp_hi"), sem("yp_split")
        diff_ready, diff_out, ypool_ready = sem("diff_ready"), sem("diff_out"), sem("ypool_ready")
        a1_ready, a1_out, la_pre, la_x, la_ln, la_ready, cum_ready, exps_ready, qk_dec = (
            sem(s) for s in ("a1_ready", "a1_out", "la_pre", "la_x", "la_ln", "la_ready", "cum_ready",
                             "exps_ready", "qk_dec"))
        gT_ready, gT_out, att_ready, kv_ready, att_out, states_ready, og_ready, sq_out, og_silu = (
            sem(s) for s in ("gT_ready", "gT_out", "att_ready", "kv_ready", "att_out", "states_ready",
                             "og_ready", "sq_out", "og_silu"))
        mrope_done, mT_ready, mT_out = sem("mrope_done"), sem("mT_ready"), sem("mT_out")
        ang_ready, trig_done = sem("ang_ready"), sem("trig_done")

        g_of = {}
        c = 0
        for which, names in (("first", VECS1), ("second", VECS2)):
            for l in range(DEPTH):
                for name, n in names:
                    g_of[which, l, name] = c
                    c += n

        def vec(key, i):
            return vecs[:, g_of[key] + i:g_of[key] + i + 1]

        xhi_flat, xlo_flat = (t[:].rearrange("p k s -> p (k s)") for t in (xhi, xlo))

        def x_cmp_split(flat, kv):
            return flat[:, kv * 1024:kv * 1024 + 480]

        def first_steps():
            steps = []
            for qt in range(TT):
                for hd in range(HEADS):
                    g = hd // (HEADS // GROUPS)
                    lanes = [dict(q=qT[:, hd, qt * P:(qt + 1) * P], k=kT[:, 2 * br + g, :],
                                  v=z[:, :, 896 + 256 * br + g * HD:896 + 256 * br + (g + 1) * HD],
                                  o=aux[:, (1 + br, (3, 0)[br])[qt], hd * HD:(hd + 1) * HD],
                                  sums=esum[:, qt, hd, 1 + br:2 + br]) for br in range(2)]
                    steps.append(dict(qt=qt, nk=(qt + 1) * P, lanes=lanes))
            return steps

        def second_steps():
            steps = []
            for qt in reversed(range(TT)):
                for h2 in range(0, HEADS, 2):
                    lanes = [dict(q=mqT[:, hd, qt * P:(qt + 1) * P], k=mkT[:, hd, :], v=m_v[:, :, hd, :],
                                  o=aux[:, 1 + qt, hd * HD:(hd + 1) * HD], sums=m_sum[:, qt, hd:hd + 1])
                             for hd in (h2, h2 + 1)]
                    steps.append(dict(qt=qt, nk=(qt + 1) * P, lanes=lanes))
            return steps

        def aux_banks(n):
            return aux[:, n % 2, :]

        def acc_second(n):
            return acc[:, n % 2, 1, :]

        def lanes_of(bank):
            return bank.rearrange("p (a n) -> p a n", a=2)

        def arrival(i, unit):
            return i * 32 + 16 * (unit // RING + 1)

        block = ctx.enter_context(nc.Block())

        @block.sync
        def _(sp):
            def load(u):
                s, n = u % RING, size[u][0] * size[u][1]
                if u >= RING:
                    sp.wait_ge(lo_ready, u - RING + 1)
                sp.dma_start(raw[:, s, 0:n], A["weights"][unit_at[u]:unit_at[u + 1]].rearrange("(p n) -> p n", p=P)).then_inc(w_loaded[s], 16)

            def ffn_loads(u0):
                for u in range(u0, u0 + 4):
                    load(u)
                with sp.Fori(0, FLOOP) as i:
                    for u in range(u0 + 4, u0 + 10):
                        sp.wait_ge(lo_ready, i * 6 + (u - RING + 1))
                        sp.dma_start(raw[:, u % RING], A["weights"][bass.ds(i * (6 * P * UNIT) + unit_at[u], P * UNIT)]
                                     .rearrange("(p n) -> p n", p=P)).then_inc(w_loaded[u % RING], 16)
                for u in range(u0 + 4 + 6 * FLOOP, u0 + FUNITS):
                    load(u)

            sp.dma_start(h[:], A["x"].rearrange("(t p) n -> p t n", p=P)).then_inc(h_in, 16)
            sp.wait_ge(vecs_in, 16)
            u = 0
            while u < len(units):
                if u in ffn_starts:
                    ffn_loads(u)
                    u += FUNITS
                else:
                    load(u)
                    u += 1
            sp.wait_ge(h_ready, 5 * DEPTH * TT)
            sp.dma_start(out.rearrange("(t p) n -> p t n", p=P), h[:]).then_inc(out_done, 16)
            sp.wait_ge(out_done, 16)

        @block.gpsimd
        def _(pool):
            seen = Seen()
            pool.memset(half_neg[:], -0.5).then_inc(setup_done, 1)
            pool.memset(zero_row[:], 0.0).then_inc(setup_done, 1)
            def inverse_root(n, width, k, at=0, dst=rstd):
                pool.wait_ge(sumsq_ready, seen(sumsq_ready, n))
                cols = slice(at, at + k)
                pool.tensor_scalar(dst[:, cols], ssq[:, cols], 1.0 / width, EPS, ALU.mult, ALU.add)
                pool.drain()
                pool.tensor_tensor(dst[:, cols], dst[:, cols], half_neg[:, cols], ALU.pow).then_inc(rstd_ready, 1)

            def tile_roots():
                for t in range(TT):
                    pool.wait_ge(sumsq_ready, seen(sumsq_ready))
                    pool.tensor_scalar(rstd[:, t:t + 1], ssq[:, t:t + 1], 1.0 / DM, EPS, ALU.mult, ALU.add)
                    pool.drain()
                    pool.tensor_tensor(rstd[:, t:t + 1], rstd[:, t:t + 1], half_neg[:, 0:1], ALU.pow).then_inc(rstd_ready, 1)

            def residual_roots(counts):
                for t in range(TT):
                    pool.wait_ge(sumsq_ready, seen(sumsq_ready, counts[t]))
                    pool.tensor_tensor(rstd[:, t:t + 1], ssq[:, t:t + 1], ssq[:, 2 + t:3 + t], ALU.add)
                    pool.drain()
                    pool.tensor_scalar(rstd[:, t:t + 1], rstd[:, t:t + 1], 1.0 / DM, EPS, ALU.mult, ALU.add)
                    pool.drain()
                    pool.tensor_tensor(rstd[:, t:t + 1], rstd[:, t:t + 1], half_neg[:, 0:1], ALU.pow).then_inc(rstd_ready, 1)

            def first_small(l):
                pool.dma_start(ws_raw, A["gmlp_ws"][l].rearrange("g t s -> t g s")).then_inc(small1_in, 16)
                for i, name in enumerate(("gmlp_ln_g", "gmlp_ln_b")):
                    pool.dma_start(ln_gb[:, i], A[name][l].partition_broadcast(P)).then_inc(small1_in, 16)
                pool.dma_start(cmp_w2, A["cmp_w2"][l].rearrange("k (c p) d -> p k c d", p=P)).then_inc(small1_in, 16)
                for kv in range(2):
                    for g in range(GROUPS):
                        pool.dma_start(cmp_b2[:, kv, g], A["cmp_b2"][l, kv].partition_broadcast(CMP_N)).then_inc(small1_in, 16)
                pool.dma_start(p_in, A["p"][l].rearrange("(t p) n -> p t n", p=P)).then_inc(small1_in, 16)

            def post_gains(a, b):
                pool.dma_start(post_g[:, 0], a.partition_broadcast(P)).then_inc(post_in, 16)
                pool.dma_start(post_g[:, 1], b.partition_broadcast(P)).then_inc(post_in, 16)

            pool.dma_start(rope1_cols, A["c_rope1"]).then_inc(tables_in, 16)
            pool.dma_start(rope_c[:], A["c_rope_c"]).then_inc(tables_in, 16)
            pool.dma_start(trig[:, 0:2].bitcast(I32), A["positions_2"]).then_inc(pos_in, 16)
            pool.dma_start(trig[:, 2:18], A["c_inv_freq"].partition_broadcast(P)).then_inc(pos_in, 16)
            pool.wait_ge(setup_done, 2)
            for l in range(DEPTH):
                inverse_root(TT, DM, 2)
                pool.wait_ge(ln_var, seen(ln_var))
                pool.tensor_scalar(rstd[:, 4:6], mean_var[:, :, 1], 1.0, EPS, ALU.mult, ALU.add)
                pool.drain()
                pool.tensor_tensor(rstd[:, 4:6], rstd[:, 4:6], half_neg[:, 0:2], ALU.pow).then_inc(rstd_ready, 1)
                if l:
                    pool.wait_ge(h_ready, 3 * TT * l)
                first_small(l)
                post_gains(A["post_mix_g"][l], A["post_ffn_g"][l])
                inverse_root(TT, 512, 2, 2)
                inverse_root(1, 512, 1, 0)
                inverse_root(1, 512, 1, 1)
                residual_roots((3, 1))
                tile_roots()
                residual_roots((2, 2))
                inverse_root(TT, DM, 2)
            for l in range(DEPTH):
                inverse_root(TT, DM, 2)
                pool.wait_ge(h_ready, (3 * DEPTH + 2 * l) * TT)
                post_gains(A["norm_post_mix_2"][l], A["norm_post_ffn_2"][l])
                pool.dma_start(b_gla, A["b_gla_a_2"][l].partition_broadcast(P)).then_inc(small2_in, 16)
                pool.dma_start(w_a2, A["w_gla_a2_2"][l]).then_inc(small2_in, 16)
                pool.dma_start(pool_mat, A["c_pool"]).then_inc(pool_in, 16)
                pool.dma_start(w_pool, A["w_pool_2"][l].rearrange("g c d -> c g d")).then_inc(pool_in, 16)
                pool.wait_ge(sumsq_ready, seen(sumsq_ready, 2 * TT))
                pool.tensor_scalar(mix_rstd[:, 0:2], ssq[:, 0:2], 1.0 / 384, EPS, ALU.mult, ALU.add)
                pool.tensor_scalar(mix_rstd[:, 2:4], ssq[:, 2:4], 1.0 / 256, EPS, ALU.mult, ALU.add)
                pool.drain()
                pool.tensor_tensor(mix_rstd[:, 0:4], mix_rstd[:, 0:4], half_neg[:, 0:4], ALU.pow).then_inc(rstd_ready, 1)
                inverse_root(1, 128, 8, dst=mix_rstd)
                residual_roots((3, 1))
                tile_roots()
                residual_roots((2, 2))

        @block.scalar
        def _(act):
            seen = Seen()
            st = {"split": 0, "unit": 0}

            def split(u):
                s = u % RING
                kc, n = size[u]
                act.wait_ge(w_loaded[s], 16 * (u // RING + 1))
                if u >= RING:
                    act.wait_ge(unit_done, u - RING + 1)
                act.activation(whi[:, s, 0:kc * n], raw[:, s, 0:kc * n], ACT.Copy).then_inc(hi_ready, 1)

            def split_ahead(more=2):
                top = min(st["unit"] + more, len(units) - 1)
                for f in ffn_starts:
                    if st["split"] <= f + 2:
                        top = min(top, f + 1)
                while st["split"] <= top:
                    split(st["split"])
                    st["split"] += 1

            def sums_of_squares(src, width, at=0, junk=0):
                for t in range(TT):
                    act.activation(normed[:, t, junk:junk + width], src(t), ACT.Square,
                                   accum_out=ssq[:, at + t:at + t + 1]).then_inc(sumsq_ready, 1)

            def x_high(nk, gain, at=0, xhi=xhi, banks=aux_banks):
                for k in range(0, nk, 2):
                    act.wait_ge(tp_ready, seen(tp_ready))
                    bank = banks(seen.now(tp_ready) - 1).rearrange("p (k s) -> p k s", k=2)
                    m = min(2, nk - k)
                    if gain is None:
                        last = act.activation(xhi[:, at + k:at + k + m, :], bank[:, 0:m], ACT.Copy)
                    else:
                        for j in range(m):
                            last = act.activation(xhi[:, at + k + j, :], bank[:, j], ACT.Copy, scale=gain(k + j))
                    last.then_inc(xhi_ready, 1)

            def next_block(n_units=2):
                st["unit"] += n_units
                split_ahead(1)
                act.wait_ge(unit_done, st["unit"])

            def scaled_out(i, n, dst, func):
                if i == 0:
                    act.wait_ge(rstd_ready, seen(rstd_ready))
                for t in range(TT):
                    last = act.activation(dst(t), acc[:, t, i % 2, 0:n], func, scale=rstd[:, t:t + 1])
                last.then_inc(acc_out, 1)

            def residual_sum(t, b):
                act.drain()
                act.activation(aux[:, 2 + b], acc[:, t, b], ACT.Square,
                               accum_out=ssq[:, 2 * b + t:2 * b + t + 1]).then_inc(sumsq_ready, 1)

            def norm_of_h():
                for t in range(TT):
                    act.wait_ge(h_ready, seen(h_ready))
                    act.drain()
                    act.activation(aux[:, 2:4].rearrange("p a n -> p (a n)"), h[:, t], ACT.Square,
                                   accum_out=ssq[:, t:t + 1]).then_inc(sumsq_ready, 1)
                seen(rstd_ready, TT)

            def ffn_steps(which, l):
                u0 = ffn[which, l]
                st["split"] = u0 + FUNITS
                gu0, cv0, fa0 = seen.now(gu_ready), seen.now(hc_conv), seen.now(fa_ready)
                cb, cw = (g_of["first", l, n] for n in ("conv_b", "conv_w")) if which == "first" else (0, 0)

                def split_at(i, first):
                    act.wait_ge(w_loaded[first % RING], arrival(i, first))
                    act.wait_ge(unit_done, i * 6 + (first - RING + 1))
                    act.activation(whi[:, first % RING], raw[:, first % RING], ACT.Copy).then_inc(hi_ready, 1)

                def hidden(j, par, free=None):
                    act.wait_ge(gu_ready, j + (gu0 + 1))
                    if which == "second":
                        act.activation(sg, aux[:, 2 - 2 * par].rearrange("p (c s) -> p c s", c=2), ACT.Silu).then_inc(sg_ready, 1)
                    else:
                        for w in range(2):
                            for c2 in range(2):
                                act.activation(hc[:, par, w, c2], aux[:, 2 - 2 * par + w, c2 * SEQ:(c2 + 1) * SEQ], ACT.Identity,
                                               scale=vecs[:, bass.ds(j * 2 + (cw + 88 + w * 22 + c2), 1)],
                                               bias=vecs[:, bass.ds(j * 2 + (cb + w * 22 + c2), 1)]).then_inc(hc_ready, 1)
                        act.wait_ge(hc_conv, j + (cv0 + 1))
                        act.activation(sg, hc[:, par, 0], ACT.Silu).then_inc(sg_ready, 1)
                    act.wait_ge(fa_ready, j + (fa0 + 1))
                    if free:
                        act.wait_ge(unit_done, free)
                    act.activation(fhi[:, par], f_act, ACT.Copy).then_inc(fhi_ready, 1)

                split(u0 + 2), split(u0 + 3)
                hidden(0, 0)
                with act.Fori(0, FLOOP) as i:
                    for s in range(2):
                        for u in range(u0 + 4 + 3 * s, u0 + 7 + 3 * s):
                            split_at(i, u)
                        hidden(i * 2 + (s + 1), (s + 1) % 2)
                for u in range(u0 + FUNITS - 5, u0 + FUNITS - 2):
                    split(u)
                hidden(FSTEPS - 2, 1)
                split(u0 + FUNITS - 2), split(u0 + FUNITS - 1)
                hidden(FSTEPS - 1, 0, free=u0 + FUNITS - 2)
                for sm in (gu_ready, hc_conv, fa_ready):
                    seen(sm, FSTEPS) if which == "first" or sm is not hc_conv else None
                st["unit"] = u0 + FUNITS
                split_ahead(1)
                for t in range(TT):
                    if t == 0:
                        act.wait_ge(tile_done, seen(tile_done))
                    else:
                        act.wait_ge(unit_done, st["unit"])
                    for b in range(2):
                        residual_sum(t, b)
                seen(rstd_ready, TT)

            def attention(steps, e, pt, between={}):
                b_max, b_pt, b_pv = seen.now(max_ready), seen.now(pt_ready), seen.now(pv_done)
                for i in range(len(steps) + 1):
                    if i < len(steps):
                        nk = steps[i]["nk"]
                        act.wait_ge(max_ready, b_max + i + 1)
                        if i >= 2:
                            act.wait_ge(pt_ready, b_pt + i - 1)
                        for a, lane in enumerate(steps[i]["lanes"]):
                            last = act.activation(e[:, i % 2, a * 256:a * 256 + nk], acc[:, 0, i % 2, a * 256:a * 256 + nk],
                                                  ACT.Exp, bias=nmax[:, i % 2, a:a + 1], accum_out=lane["sums"])
                        last.then_inc(e_ready, 1)
                    j = i - 1
                    if j >= 0 and j % 2 == 0:
                        nk = steps[j]["nk"]
                        act.wait_ge(pt_ready, b_pt + j + 1)
                        if j >= 2:
                            act.wait_ge(pv_done, b_pv + j - 1)
                        act.activation(pt(j % 2)[:, :, 0:nk], lanes_of(acc[:, 1, j % 2])[:, :, 0:nk], ACT.Copy).then_inc(pts_ready, 1)
                    if i in between:
                        between[i]()
                for sm in (max_ready, pt_ready, pv_done):
                    seen(sm, len(steps))

            act.dma_start(vecs[:], A["vecs"]).then_inc(vecs_in, 16)
            act.dma_start(masks[:], A["c_masks"]).then_inc(masks_in, 16)
            act.wait_ge(h_in, 16)
            act.wait_ge(vecs_in, 16)

            for l in range(DEPTH):
                key = lambda name: ("first", l, name)
                if l:
                    act.wait_ge(h_ready, seen(h_ready, TT))
                if l:
                    split_ahead(0)
                x_high(KC8, lambda k: vec(key("pre_mix_g"), k))
                split_ahead(0)
                sums_of_squares(lambda t: h[:, t], DM)
                split_ahead()
                for i, (c0, n) in enumerate(W1_BLOCKS[:-1]):
                    next_block()
                    scaled_out(i, n, lambda t: z[:, t, c0:c0 + n], ACT.Copy if i else ACT.Gelu_apprx_tanh)
                seen(rstd_ready)
                split_ahead()
                act.drain()
                for t in range(TT):
                    last = act.activation(zc2[:, t], z[:, t, 512:768].rearrange("p (u d) -> p u d", u=4).unsqueeze(2)
                                          .broadcast_to([P, 4, 2, HD]), ACT.Copy)
                last.then_inc(zc2_done, 1)
                if l == 0:
                    act.wait_ge(ang_ready, 1)
                    act.activation(rope2[:].rearrange("p a t f -> p (a t f)"), trig[:, 128:192], ACT.Sin).then_inc(trig_done, 1)
                next_block()
                scaled_out(len(W1_BLOCKS) - 1, BLK, lambda t: z[:, t, U1:V1], ACT.Gelu_apprx_tanh)
                act.activation(z[:, :, GATE1:U1], z[:, :, GATE1:U1], ACT.Tanh, scale=0.5).then_inc(gate_done, 1)
                for kv in range(2):
                    act.wait_ge(xc_sum, seen(xc_sum))
                    act.activation(x_cmp_split(xhi_flat, kv), x_cmp[:, kv].rearrange("p c g n -> p (c g n)"), ACT.Copy).then_inc(xc_hi, 1)
                for i in range(6):
                    act.wait_ge(qk_ready, seen(qk_ready))
                    t, which = i % 2, i // 2
                    src = aux[0:HD, 2 + i % 2, :].rearrange("p (h s) -> p h s", h=4)
                    dst = kT[:, :, t * P:(t + 1) * P] if which == 2 else qT[:, which * 4:which * 4 + 4, t * P:(t + 1) * P]
                    act.activation(dst, src, ACT.Copy, scale=1.0 if which == 2 else HD ** -0.5).then_inc(qk_out, 1)
                for kv in range(2):
                    next_block()
                    act.activation(hid[:, kv], acc[0:2 * CMP_N, 0, kv, 0:CMP_HID], ACT.Copy).then_inc(hid_out, 1)
                act.wait_ge(hidT_ready, seen(hidT_ready))
                for kv in range(2):
                    for c2 in range(2):
                        last = act.activation(hT[:, kv, c2], acc[:, 1, kv, c2 * 30:(c2 + 1) * 30], ACT.Gelu_apprx_tanh,
                                              bias=vec(key("cmp_b1"), kv * 2 + c2))
                last.then_inc(hT_out, 1)
                act.wait_ge(kcT_ready, seen(kcT_ready))
                act.activation(kcT, aux[0:HD, 3, 0:30].rearrange("p (g n) -> p g n", g=2), ACT.Copy).then_inc(kcT_out, 1)
                split_ahead()

                act.wait_ge(sc_shift, seen(sc_shift))
                act.activation(ec, ec, ACT.Exp).then_inc(sc_exp, 1)
                for t in range(TT):
                    act.wait_ge(ect_ready, seen(ect_ready))
                    for b in range(2):
                        last = act.activation(ecT[:, t, b * 4:b * 4 + 4].rearrange("p h q -> p (h q)"),
                                              acc[0:CMP_N, t, b], ACT.Copy)
                    last.then_inc(ect_out, 1)

                def gated_sums():
                    act.wait_ge(gmlp_out, seen(gmlp_out))
                    sums_of_squares(lambda t: mlp[:, t], 512, at=2, junk=512)

                def attention_sum(t):
                    act.wait_ge(mixed_ready, seen(mixed_ready))
                    act.activation(normed[:, t, 0:512], attn[:, t], ACT.Square,
                                   accum_out=ssq[:, t:t + 1]).then_inc(sumsq_ready, 1)

                attention(first_steps(), e_buf, lambda b: lanes_of(pT[:, b]),
                          {0: gated_sums, HEADS + 4: lambda: attention_sum(0)})
                x_high(4, lambda k: vec(key("mlp_out_g"), k), banks=acc_second)
                attention_sum(1)
                seen(rstd_ready, 3)
                x_high(4, lambda k: vec(key("attn_out_g"), k), at=4)
                next_block()
                for t in range(TT):
                    residual_sum(t, 0)
                st["unit"] += 2
                split_ahead(1)
                act.wait_ge(tile_done, seen(tile_done))
                residual_sum(0, 1)
                act.wait_ge(unit_done, st["unit"])
                residual_sum(1, 1)
                seen(rstd_ready, TT)
                norm_of_h()
                split_ahead()
                x_high(KC8, lambda k: vec(key("pre_ffn_g"), k))
                ffn_steps("first", l)
                act.wait_ge(h_ready, seen(h_ready, TT))
                x_high(KC8, lambda k: vec(key("ple_norm_g"), k))
                sums_of_squares(lambda t: h[:, t], DM)
                for nb in range(2):
                    next_block()
                    scaled_out(nb, BLK, lambda t: ple_gate[:, t, nb * BLK:(nb + 1) * BLK], ACT.Sigmoid)
                x_high(2, None)
                st["unit"] += 1
                split_ahead()

            for l in range(DEPTH):
                key = lambda name: ("second", l, name)
                act.wait_ge(h_ready, seen(h_ready, TT))
                split_ahead(0)
                x_high(KC8, lambda k: vec(key("norm_pre_mix_2"), k))
                sums_of_squares(lambda t: h[:, t], DM)
                split_ahead()
                for i, (c0, n) in enumerate(blocks_of(0, Z2)):
                    next_block()
                    scaled_out(i, n, lambda t: z[:, t, c0:c0 + n], ACT.Copy)
                act.drain()
                sums_of_squares(lambda t: z[:, t, CQ:CKV], 384)
                sums_of_squares(lambda t: z[:, t, CKV:KR], 256, at=2, junk=384)
                seen(rstd_ready)
                split_ahead()

                def gate_block(i, bank=0):
                    next_block()
                    for t in range(TT):
                        last = act.activation(gates[:, t, i // 2, (i % 2) * BLK:(i % 2 + 1) * BLK], acc[:, t, bank, :],
                                              ACT.Sigmoid, scale=rstd[:, t:t + 1])
                    last.then_inc(acc_out, 1)

                act.wait_ge(diff_ready, seen(diff_ready))
                act.activation(diffT.rearrange("p g t -> p (g t)"), aux[:, 0:2, :].rearrange("p a n -> p (a n)"), ACT.Copy).then_inc(diff_out, 1)
                gate_block(0)
                act.wait_ge(ypool_ready, seen(ypool_ready))
                for g in range(4):
                    last = act.activation(yhi[:, g], aux[:, 2 + g // 2, (g % 2) * SEQ:(g % 2 + 1) * SEQ], ACT.Copy,
                                          scale=vec(key("pool_scale_2"), g))
                last.then_inc(yp_hi, 1)
                act.wait_ge(a1_ready, seen(a1_ready))
                act.activation(a1T, aux[0:16, 0, 0:SEQ], ACT.Copy).then_inc(a1_out, 1)
                gate_block(1)
                act.wait_ge(la_x, seen(la_x))
                act.activation(e_cum, la, ACT.Abs)
                act.drain()
                act.activation(e_cum, e_cum, ACT.Exp, scale=-1.0)
                act.drain()
                act.activation(e_cum, e_cum, ACT.Ln, bias=1.0).then_inc(la_ln, 1)
                for nb in range(2):
                    st["unit"] += 1
                split_ahead()
                act.wait_ge(cum_ready, seen(cum_ready))
                cum = aux[:, 0, :].rearrange("p (t n) -> p t n", t=TT)
                act.activation(e_cum, cum, ACT.Exp, scale=1.0 / 16)
                act.activation(e_inv, cum, ACT.Exp, scale=-1.0 / 16)
                act.activation(e_suf, aux[:, 1, :].rearrange("p (t n) -> p t n", t=TT), ACT.Exp, scale=1.0 / 16)
                act.activation(decay, aux[0:HD, 2, 0:16].rearrange("p (h n) -> p h n", h=4), ACT.Exp,
                               scale=1.0 / 16).then_inc(exps_ready, 1)
                gate_block(2)
                for i in range(4):
                    act.wait_ge(gT_ready, seen(gT_ready))
                    dst = (qdT, kiT)[i // 2]
                    act.activation(dst[:, :, (i % 2) * P:(i % 2 + 1) * P],
                                   aux[0:HD, i, :].rearrange("p (h s) -> p h s", h=4), ACT.Copy).then_inc(gT_out, 1)
                gate_block(3, bank=1)
                act.activation(z[:, :, GR:GA], z[:, :, GR:GA], ACT.Silu).then_inc(og_silu, 1)
                gate_block(4)
                act.wait_ge(og_ready, seen(og_ready))
                act.activation(sq_gla, acc[:, :, 1, :], ACT.Square).then_inc(sq_out, 1)
                seen(rstd_ready)
                x_high(5, lambda k: vec(key("mla_q_norm_2"), k) if k < 3 else vec(key("mla_kv_norm_2"), k - 3), xhi=yhi)
                gate_block(5)
                split_ahead()
                x_high(4, lambda k: vec(key("gla_norm_2"), k))
                for nb in range(2):
                    next_block(1)
                    act.activation(qf[:, :, nb * 4:nb * 4 + 4, :], acc[:, :, nb, 0:384].rearrange("p t (h d) -> p t h d", h=4),
                                   ACT.Copy).then_inc(acc_out, 1)
                next_block(1)
                for nb in range(2):
                    src = acc[:, :, nb, :].rearrange("p t (h d) -> p t h d", h=4)
                    act.activation(kf[:, :, nb * 4:nb * 4 + 4, 0:64], src[:, :, :, 0:64], ACT.Copy)
                    act.activation(m_v[:, :, nb * 4:nb * 4 + 4, :], src[:, :, :, 64:128], ACT.Copy).then_inc(acc_out, 1)
                for nb in range(2):
                    st["unit"] += 1
                split_ahead()
                for i in range(8):
                    act.wait_ge(mT_ready, seen(mT_ready))
                    t, hg, which = i % 2, i // 2 % 2, i // 4
                    dst = (mqT, mkT)[which]
                    act.activation(dst[:, hg * 4:hg * 4 + 4, t * P:(t + 1) * P],
                                   aux[0:QK, i % 4, :].rearrange("p (h s) -> p h s", h=4), ACT.Copy,
                                   scale=QK ** -0.5 if which == 0 else 1.0).then_inc(mT_out, 1)
                split_ahead()
                attention(second_steps(), m_e, lambda b: lanes_of(m_pT[:, b]))
                x_high(4, None)
                for nb in range(2):
                    st["unit"] += 1
                split_ahead()
                x_high(KC8, None)
                next_block()
                for t in range(TT):
                    residual_sum(t, 0)
                st["unit"] += 2
                split_ahead(1)
                act.wait_ge(tile_done, seen(tile_done))
                residual_sum(0, 1)
                act.wait_ge(unit_done, st["unit"])
                residual_sum(1, 1)
                seen(rstd_ready, TT)
                norm_of_h()
                split_ahead()
                x_high(KC8, lambda k: vec(key("norm_pre_ffn_2"), k))
                ffn_steps("second", l)

        @block.vector
        def _(dve):
            seen = Seen()
            st = {"split": 0, "unit": 0}

            def split(u):
                s = u % RING
                kc, n = size[u]
                dve.wait_ge(hi_ready, u + 1)
                dve.tensor_tensor(wlo[:, s, 0:kc * n], raw[:, s, 0:kc * n], whi[:, s, 0:kc * n].bitcast(F32),
                                  ALU.subtract).then_inc(lo_ready, 1)

            def split_ahead(more=2):
                top = min(st["unit"] + more, len(units) - 1)
                for f in ffn_starts:
                    if st["split"] <= f + 2:
                        top = min(top, f + 1)
                while st["split"] <= top:
                    split(st["split"])
                    st["split"] += 1

            def normalize(src, width, at=0, to=0):
                for t in range(TT):
                    last = dve.tensor_scalar(normed[:, t, to:to + width], src(t), rstd[:, at + t:at + t + 1], None, ALU.mult)
                return last

            def x_low(nk, gain, at=0, xhi=xhi, xlo=xlo, banks=aux_banks):
                for k in range(0, nk, 2):
                    dve.wait_ge(xhi_ready, seen(xhi_ready))
                    bank = banks(seen.now(xhi_ready) - 1).rearrange("p (k s) -> p k s", k=2)
                    m = min(2, nk - k)
                    hi = xhi[:, at + k:at + k + m, :].bitcast(F32)
                    if gain is None:
                        last = dve.tensor_tensor(xlo[:, at + k:at + k + m, :], bank[:, 0:m], hi, ALU.subtract)
                    else:
                        for j in range(m):
                            last = dve.scalar_tensor_tensor(xlo[:, at + k + j, :], bank[:, j], gain(k + j), hi[:, j],
                                                            ALU.mult, ALU.subtract)
                    last.then_inc(x_split, 1)

            def gained(i, t, b):
                cols = slice(b * BLK, (b + 1) * BLK)
                dve.wait_ge(sumsq_ready, seen(sumsq_ready))
                last = dve.tensor_tensor(normed[:, t, cols], acc[:, t, b], post_g[:, i, cols], ALU.mult)
                if t == TT - 1:
                    last.then_inc(acc_out, 1)

            def residual(t):
                dve.drain()
                dve.wait_ge(rstd_ready, seen(rstd_ready))
                dve.scalar_tensor_tensor(h[:, t], normed[:, t], rstd[:, t:t + 1], h[:, t], ALU.mult, ALU.add).then_inc(h_ready, 1)

            def norm_of_h():
                seen(sumsq_ready, TT)
                for t in range(TT):
                    dve.wait_ge(rstd_ready, seen(rstd_ready))
                    dve.tensor_scalar(normed[:, t], h[:, t], rstd[:, t:t + 1], None, ALU.mult).then_inc(normed_ready, 1)

            def ffn_steps(which, l):
                u0 = ffn[which, l]
                st["split"] = u0 + FUNITS
                hc0, sg0, fh0 = seen.now(hc_ready), seen.now(sg_ready), seen.now(fhi_ready)
                cw = g_of["first", l, "conv_w"]

                def split_at(i, first):
                    dve.wait_ge(hi_ready, i * 6 + (first + 1))
                    s = first % RING
                    dve.tensor_tensor(wlo[:, s], raw[:, s], whi[:, s].bitcast(F32), ALU.subtract).then_inc(lo_ready, 1)

                def hidden(j, par):
                    if which == "first":
                        dve.wait_ge(hc_ready, j * 4 + (hc0 + 4))
                        for back in (1, 2):
                            for w in range(2):
                                for c2 in range(2):
                                    tile = hc[:, par, w, c2, back:SEQ]
                                    tap = vecs[:, bass.ds(j * 2 + (cw + (2 - back) * 44 + w * 22 + c2), 1)]
                                    last = dve.scalar_tensor_tensor(
                                        tile, aux[:, 2 - 2 * par + w, c2 * SEQ:(c2 + 1) * SEQ - back], tap, tile,
                                        ALU.mult, ALU.add)
                            if back == 1:
                                dve.drain()
                        last.then_inc(hc_conv, 1)
                        up = hc[:, par, 1]
                    else:
                        up = aux[:, 3 - 2 * par].rearrange("p (c s) -> p c s", c=2)
                        dve.drain()
                    dve.wait_ge(sg_ready, j + (sg0 + 1))
                    dve.tensor_tensor(f_act, up, sg, ALU.mult).then_inc(fa_ready, 1)
                    dve.wait_ge(fhi_ready, j + (fh0 + 1))
                    dve.tensor_tensor(flo[:, par], f_act, fhi[:, par].bitcast(F32), ALU.subtract).then_inc(f_split, 1)

                split(u0 + 2), split(u0 + 3)
                hidden(0, 0)
                with dve.Fori(0, FLOOP) as i:
                    for s in range(2):
                        for u in range(u0 + 4 + 3 * s, u0 + 7 + 3 * s):
                            split_at(i, u)
                        hidden(i * 2 + (s + 1), (s + 1) % 2)
                for u in range(u0 + FUNITS - 5, u0 + FUNITS - 2):
                    split(u)
                hidden(FSTEPS - 2, 1)
                split(u0 + FUNITS - 2), split(u0 + FUNITS - 1)
                hidden(FSTEPS - 1, 0)
                if which == "first":
                    seen(hc_ready, 4 * FSTEPS)
                seen(sg_ready, FSTEPS), seen(fhi_ready, FSTEPS)
                st["unit"] = u0 + FUNITS
                split_ahead(1)

            def attention(steps, pt, between={}):
                b_s, b_pt, b_pv = seen.now(s_ready), seen.now(pt_ready), seen.now(pv_done)
                for i in range(len(steps) + 1):
                    if i < len(steps):
                        nk, qt = steps[i]["nk"], steps[i]["qt"]
                        dve.wait_ge(s_ready, b_s + i + 1)
                        lanes = lanes_of(acc[:, 0, i % 2])
                        dve.tensor_tensor(lanes[:, :, qt * P:nk], lanes[:, :, qt * P:nk],
                                          causal.unsqueeze(1).broadcast_to([P, 2, P]), ALU.add)
                        dve.drain()
                        dve.tensor_reduce(nmax[:, i % 2], lanes[:, :, 0:nk], AX.X, ALU.max, negate=True).then_inc(max_ready, 1)
                    j = i - 1
                    if j >= 0 and j % 2 == 1:
                        nk = steps[j]["nk"]
                        dve.wait_ge(pt_ready, b_pt + j + 1)
                        if j >= 2:
                            dve.wait_ge(pv_done, b_pv + j - 1)
                        dve.tensor_copy(pt(j % 2)[:, :, 0:nk], lanes_of(acc[:, 1, j % 2])[:, :, 0:nk]).then_inc(pts_ready_dve, 1)
                    if i in between:
                        between[i]()
                for sm in (s_ready, pt_ready, pv_done):
                    seen(sm, len(steps))

            def rotate(x1, x2, cos, sin, temps):
                a, b, c, d = temps
                dve.tensor_tensor(a, x1, cos, ALU.mult)
                dve.tensor_tensor(b, x2, sin, ALU.mult)
                dve.tensor_tensor(c, x2, cos, ALU.mult)
                dve.tensor_tensor(d, x1, sin, ALU.mult)
                dve.drain()
                dve.tensor_tensor(x1, a, b, ALU.subtract)
                return dve.tensor_tensor(x2, c, d, ALU.add)

            def angles():
                dve.wait_ge(pos_in, 32)
                C1 = 6.28125
                C2 = 0.0019353071693331003
                C3 = 1.0253404e-11
                pos, ang, arg, turns = trig[:, 20:22], trig[:, 64:128], trig[:, 128:192], trig[:, 192:256]
                dve.tensor_copy(pos, trig[:, 0:2].bitcast(I32))
                dve.drain()
                for a in range(2):
                    for t in range(TT):
                        dve.tensor_scalar(ang[:, a * 32 + t * 16:a * 32 + t * 16 + 16], trig[:, 2:18], pos[:, t:t + 1], None, ALU.mult)
                dve.drain()
                dve.tensor_scalar(turns[:, 0:32], ang[:, 0:32], 0.15915494309189535, 0.25, ALU.mult, ALU.add)
                dve.tensor_scalar(turns[:, 32:64], ang[:, 32:64], 0.15915494309189535, None, ALU.mult)
                dve.drain()
                dve.tensor_scalar(turns, turns, 12582912.0, None, ALU.add)
                dve.drain()
                dve.tensor_scalar(turns, turns, 12582912.0, None, ALU.subtract)
                dve.drain()
                dve.scalar_tensor_tensor(arg, turns, -C1, ang, ALU.mult, ALU.add)
                dve.drain()
                dve.scalar_tensor_tensor(arg, turns, -C2, arg, ALU.mult, ALU.add)
                dve.drain()
                dve.scalar_tensor_tensor(arg, turns, -C3, arg, ALU.mult, ALU.add)
                dve.drain()
                dve.tensor_scalar(arg[:, 0:32], arg[:, 0:32], 1.5707963267948966, None, ALU.add)
                dve.drain()
                dve.tensor_scalar(arg, arg, 3.1415925, -3.1415925, ALU.min, ALU.max).then_inc(ang_ready, 1)

            dve.wait_ge(masks_in, 16)
            dve.wait_ge(h_in, 16)
            dve.wait_ge(vecs_in, 16)
            for l in range(DEPTH):
                key = lambda name: ("first", l, name)
                seen(sumsq_ready, TT), seen(rstd_ready)
                if l:
                    split_ahead(0)
                x_low(KC8, lambda k: vec(key("pre_mix_g"), k))
                split_ahead(0)
                if l == 0:
                    split_ahead(1)
                    angles()
                for i in range(4):
                    st["unit"] += 2
                    split_ahead(1)
                    if i == 1:
                        dve.wait_ge(acc_out, seen(acc_out))
                        for t in range(TT):
                            dve.bn_stats(stat[:, t], z[:, t, V1:W1])
                        dve.drain()
                        for t in range(TT):
                            last = dve.bn_aggr(mean_var[:, t], stat[:, t])
                        last.then_inc(ln_var, 1)
                    elif i == 2:
                        dve.wait_ge(rstd_ready, seen(rstd_ready))
                        for t in range(TT):
                            dve.tensor_scalar(z[:, t, V1:W1], z[:, t, V1:W1], mean_var[:, t, 0:1], rstd[:, 4 + t:5 + t],
                                              ALU.subtract, ALU.mult)
                split_ahead()
                dve.wait_ge(tables_in, 32)
                dve.wait_ge(acc_out, seen(acc_out, 3))
                dve.wait_ge(zc2_done, seen(zc2_done))
                heads = z[:, :, 0:ROPE_UNITS * HD].rearrange("p t (u d) -> p t u d", d=HD)
                for t in range(TT):
                    rotate(heads[:, t, :, 0:8], heads[:, t, :, 8:16], rope1[:, t, 0], rope1[:, t, 1],
                           [rt[:, a, t] for a in range(4)]).then_inc(rope_done, 1)
                st["unit"] += 2
                split_ahead(1)
                pe0 = g_of["first", l, "cmp_pe"]
                for kv in range(2):
                    dve.wait_ge(ct_ready, seen(ct_ready))
                    for odd in range(2):
                        rows = slice(odd * HD, (odd + 1) * HD)
                        for g in range(GROUPS):
                            src = aux[rows, kv, g * SEQ:(g + 1) * SEQ].rearrange("p (m c i) -> p i c m", c=8, i=2)[:, odd]
                            for back in range(2):
                                pe = vecs[rows, pe0 + kv * 16 + back * 8:pe0 + kv * 16 + back * 8 + 8]
                                last = dve.tensor_tensor(x_cmp[rows, kv, back * 8:back * 8 + 8, g, :],
                                                         src[:, :, back:back + CMP_N],
                                                         pe.unsqueeze(2).broadcast_to([HD, 8, CMP_N]), ALU.add)
                    last.then_inc(xc_sum, 1)
                for kv in range(2):
                    dve.wait_ge(xc_hi, seen(xc_hi))
                    dve.tensor_tensor(x_cmp_split(xlo_flat, kv), x_cmp[:, kv].rearrange("p c g n -> p (c g n)"),
                                      x_cmp_split(xhi_flat, kv).bitcast(F32), ALU.subtract).then_inc(xc_split, 1)
                st["unit"] += 2
                split_ahead(1)
                dve.wait_ge(small1_in, 16 * SMALL1 * (l + 1))
                v = z[:, :, V1:W1]
                dve.tensor_tensor(v, v, ln_gb[:, 0].unsqueeze(1).broadcast_to([P, TT, 512]), ALU.mult)
                dve.drain()
                dve.tensor_tensor(v, v, ln_gb[:, 1].unsqueeze(1).broadcast_to([P, TT, 512]), ALU.add).then_inc(ln_done, 1)
                dve.wait_ge(ws_ready, seen(ws_ready))
                for a in range(2):
                    last = dve.tensor_tensor(wsT[:, a * 4:a * 4 + 4], aux[:, a, :].rearrange("p (g s) -> p g s", g=4),
                                             keep_le.unsqueeze(1).broadcast_to([P, 4, P]), ALU.mult)
                last.then_inc(ws_out, 1)
                st["unit"] += 2
                split_ahead(1)
                dve.wait_ge(gate_done, seen(gate_done))
                dve.tensor_scalar(z[:, :, GATE1:U1], z[:, :, GATE1:U1], 0.5, 0.5, ALU.mult, ALU.add)
                dve.wait_ge(kcv_ready, seen(kcv_ready))
                dve.tensor_tensor(kcv, aux[0:CMP_N, 2, 0:256].rearrange("p (k g d) -> p k g d", k=2, g=GROUPS), cmp_b2, ALU.add)
                dve.drain()
                rotate(kcv[:, 0, :, 0:8], kcv[:, 0, :, 8:16], rope_c[:, 0], rope_c[:, 1],
                       [rt_c[:, a] for a in range(4)]).then_inc(kcv_out, 1)
                dve.wait_ge(sc_ready, seen(sc_ready))
                for t in range(TT):
                    dve.tensor_tensor(ec[:, t], aux[:, 2, t * 120:(t + 1) * 120].rearrange("p (h n) -> p h n", h=HEADS),
                                      cmp_mask[:, 0, t].unsqueeze(1).broadcast_to([P, HEADS, CMP_N]), ALU.add)
                dve.drain()
                dve.tensor_reduce(cmax[:], ec, AX.X, ALU.max)
                dve.drain()
                dve.tensor_tensor(ec, ec, cmax[:].unsqueeze(3).broadcast_to([P, TT, HEADS, CMP_N]), ALU.subtract).then_inc(sc_shift, 1)
                dve.wait_ge(sc_exp, seen(sc_exp))
                for t in range(TT):
                    dve.tensor_tensor(ec[:, t], ec[:, t], cmp_mask[:, 1, t].unsqueeze(1).broadcast_to([P, HEADS, CMP_N]), ALU.mult)
                dve.drain()
                dve.tensor_reduce(esum[:, :, :, 0], ec, AX.X, ALU.add).then_inc(ec_ready, 1)
                dve.drain()
                gate = z[:, :, GATE1:U1].rearrange("p t (h b) -> p t h b", b=3)

                def gate_factor(b0, b1, t):
                    s, f = esum[:, t, :, b0:b1], factor[:, t, :, b0:b1]
                    dve.tensor_scalar(s, s, 1e-30, None, ALU.max)
                    dve.drain()
                    dve.reciprocal(f, s)
                    dve.drain()
                    dve.tensor_tensor(f, f, gate[:, t, :, b0:b1], ALU.mult)
                    dve.drain()

                def heads_of(ap):
                    return ap.rearrange("p (h d) -> p h d", d=HD)

                def factor_of(t, b):
                    return factor[:, t, :, b:b + 1].broadcast_to([P, HEADS, HD])

                for t in range(TT):
                    gate_factor(0, 1, t)
                dve.wait_ge(mix_ready, seen(mix_ready))
                dve.wait_ge(acc_out, seen(acc_out))
                for g in range(8):
                    last = dve.scalar_tensor_tensor(
                        mlp[:, :, g * HD:(g + 1) * HD],
                        aux[:, g // 4, (g % 4) * P:(g % 4 + 1) * P].rearrange("p (t d) -> p t d", t=TT),
                        vec(key("gmlp_bs"), g), z[:, :, U1 + g * HD:U1 + (g + 1) * HD], ALU.add, ALU.mult)
                last.then_inc(gmlp_out, 1)
                dve.wait_ge(cpv_done, seen(cpv_done))
                for t in range(TT):
                    last = dve.tensor_tensor(heads_of(attn[:, t]), heads_of(aux[:, 3 - t]), factor_of(t, 0), ALU.mult)
                last.then_inc(cmp_out, 1)
                def normalize_mlp():
                    dve.wait_ge(rstd_ready, seen(rstd_ready))
                    normalize(lambda t: mlp[:, t], 512, at=2, to=512).then_inc(normed_ready, 1)

                def branches(t):
                    dve.wait_ge(pv_done, pv0 + (t + 1) * HEADS)
                    gate_factor(1, 3, t)
                    for b in range(2):
                        o = heads_of(aux[:, (1 + b, (3, 0)[b])[t]])
                        dve.tensor_tensor(heads_of(part[:, b]), o, factor_of(t, 1 + b), ALU.mult)
                    dve.drain()
                    dve.tensor_tensor(attn[:, t], attn[:, t], part[:, 0], ALU.add)
                    dve.drain()
                    dve.tensor_tensor(attn[:, t], attn[:, t], part[:, 1], ALU.add).then_inc(mixed_ready, 1)

                def normalize_attention(t):
                    dve.wait_ge(rstd_ready, seen(rstd_ready))
                    dve.tensor_scalar(normed[:, t, 0:512], attn[:, t], rstd[:, t:t + 1], None, ALU.mult).then_inc(normed_ready, 1)

                pv0 = seen.now(pv_done)
                attention(first_steps(), lambda b: lanes_of(pT[:, b]),
                          {2: normalize_mlp, 4: split_ahead, HEADS + 2: lambda: branches(0), 2 * HEADS - 1: lambda: normalize_attention(0)})
                x_low(4, lambda k: vec(key("mlp_out_g"), k), banks=acc_second)
                branches(1)
                seen(sumsq_ready, 2 * TT)
                normalize_attention(1)
                x_low(4, lambda k: vec(key("attn_out_g"), k), at=4)
                dve.wait_ge(post_in, 32 * (l + 1))
                st["unit"] += 2
                split_ahead(1)
                for t in range(TT):
                    gained(0, t, 0)
                st["unit"] += 2
                split_ahead(1)
                for t in range(TT):
                    gained(0, t, 1)
                    residual(t)
                norm_of_h()
                split_ahead()
                x_low(KC8, lambda k: vec(key("pre_ffn_g"), k))
                ffn_steps("first", l)
                for t in range(TT):
                    for b in range(2):
                        gained(1, t, b)
                    residual(t)
                seen(sumsq_ready, TT), seen(rstd_ready)
                x_low(KC8, lambda k: vec(key("ple_norm_g"), k))
                for nb in range(2):
                    st["unit"] += 2
                    split_ahead(1)
                x_low(2, None)
                st["unit"] += 1
                split_ahead(1)
                for nb in range(2):
                    if nb == 0:
                        dve.wait_ge(half_done, seen(half_done))
                    else:
                        dve.wait_ge(unit_done, st["unit"])
                    cols = slice(nb * BLK, (nb + 1) * BLK)
                    dve.tensor_tensor(normed[:, :, cols], acc[:, :, nb, :], ple_gate[:, :, cols], ALU.mult).then_inc(acc_out, 1)
                    dve.drain()
                    dve.tensor_tensor(h[:, :, cols], h[:, :, cols], normed[:, :, cols], ALU.add).then_inc(h_ready, 1)
                seen(acc_out, 2 * 2 + 2 + 2)
                split_ahead()

            for l in range(DEPTH):
                key = lambda name: ("second", l, name)

                def gated(nb, b, first):
                    st["unit"] += 1
                    split_ahead(1)
                    dve.wait_ge(unit_done, st["unit"])
                    cols = slice(nb * BLK, (nb + 1) * BLK)
                    if first:
                        dve.tensor_tensor(merged[:, :, cols], acc[:, :, nb, :], gates[:, :, b, cols], ALU.mult).then_inc(acc_out, 1)
                    else:
                        tmp = o_gla
                        dve.tensor_tensor(tmp, acc[:, :, nb, :], gates[:, :, b, cols], ALU.mult).then_inc(acc_out, 1)
                        dve.drain()
                        dve.tensor_tensor(merged[:, :, cols], merged[:, :, cols], tmp, ALU.add)
                        dve.drain()

                seen(sumsq_ready, TT), seen(rstd_ready)
                split_ahead(0)
                x_low(KC8, lambda k: vec(key("norm_pre_mix_2"), k))
                for nb in range(6):
                    st["unit"] += 2
                    split_ahead(1)
                split_ahead()

                def gate_block():
                    st["unit"] += 2
                    split_ahead(1)

                seen(sumsq_ready, 2 * TT)
                dve.wait_ge(rstd_ready, seen(rstd_ready))
                for t in range(TT):
                    dve.tensor_scalar(z[:, t, CQ:CKV], z[:, t, CQ:CKV], mix_rstd[:, t:t + 1], None, ALU.mult)
                    last = dve.tensor_scalar(z[:, t, CKV:KR], z[:, t, CKV:KR], mix_rstd[:, 2 + t:3 + t], None, ALU.mult)
                last.then_inc(normed_ready, 1)
                gate_block()
                dve.wait_ge(yp_hi, seen(yp_hi))
                for g in range(4):
                    last = dve.scalar_tensor_tensor(ylo[:, g], aux[:, 2 + g // 2, (g % 2) * SEQ:(g % 2 + 1) * SEQ],
                                                    vec(key("pool_scale_2"), g), yhi[:, g].bitcast(F32), ALU.mult, ALU.subtract)
                last.then_inc(yp_split, 1)
                gate_block()
                dve.wait_ge(la_pre, seen(la_pre))
                dve.tensor_tensor(la, aux[:, 1, :].rearrange("p (t n) -> p t n", t=TT),
                                  b_gla.unsqueeze(1).broadcast_to([P, TT, 256]), ALU.add).then_inc(la_x, 1)
                dve.wait_ge(acc_out, seen(acc_out, 6 + 2))
                gated(0, 0, True)
                dve.wait_ge(la_ln, seen(la_ln))
                dve.scalar_tensor_tensor(la, la, 0.0, e_cum, ALU.min, ALU.subtract).then_inc(la_ready, 1)
                gated(1, 0, True)
                split_ahead()
                seen(acc_out, 2)
                dve.memset(attM.rearrange("p t h s -> p (t h s)"), 0.0)
                dve.wait_ge(exps_ready, seen(exps_ready))
                q, k = z[:, :, GQ:GK], z[:, :, GK:GV]
                dve.scalar_tensor_tensor(q, q, 64 ** -0.5, e_cum, ALU.mult, ALU.mult)
                dve.tensor_tensor(e_inv, k, e_inv, ALU.mult)
                dve.tensor_tensor(e_suf, k, e_suf, ALU.mult).then_inc(qk_dec, 1)
                gate_block()
                gate_block()
                dve.wait_ge(att_ready, seen(att_ready))
                for t in range(TT):
                    last = dve.copy_predicated(attM[:, t], chunk_le.bitcast(I32).unsqueeze(1).broadcast_to([P, 4, P]),
                                               acc[:, t, 0].rearrange("p (h s) -> p h s", h=4))
                last.then_inc(att_out, 1)
                dve.wait_ge(kv_ready, seen(kv_ready))
                kv = [aux[0:HD, n, :].rearrange("p (h e) -> p h e", h=4) for n in range(3)]
                dve.tensor_copy(state[:, 0], kv[0])
                dve.drain()
                for n in (1, 2):
                    for hd in range(4):
                        last = dve.scalar_tensor_tensor(state[:, n, hd], state[:, n - 1, hd], decay[:, hd, n:n + 1],
                                                        kv[n][:, hd], ALU.mult, ALU.add)
                    if n == 1:
                        dve.drain()
                last.then_inc(states_ready, 1)
                gate_block()
                dve.wait_ge(sq_out, seen(sq_out))
                dve.tensor_reduce(ssq[:, 0:8], sq_gla.rearrange("p t (h e) -> p (t h) e", h=4), AX.X, ALU.add).then_inc(sumsq_ready, 1)
                seen(sumsq_ready)
                x_low(5, lambda k: vec(key("mla_q_norm_2"), k) if k < 3 else vec(key("mla_kv_norm_2"), k - 3),
                      xhi=yhi, xlo=ylo)
                dve.wait_ge(rstd_ready, seen(rstd_ready))
                for t in range(TT):
                    dve.tensor_tensor(o_gla[:, t].rearrange("p (h e) -> p h e", h=4), acc[:, t, 1].rearrange("p (h e) -> p h e", h=4),
                                      mix_rstd[:, t * 4:t * 4 + 4].unsqueeze(2).broadcast_to([P, 4, P]), ALU.mult)
                dve.drain()
                dve.wait_ge(og_silu, seen(og_silu))
                dve.tensor_tensor(normed[:, :, 0:512], o_gla, z[:, :, GR:GA], ALU.mult).then_inc(normed_ready, 1)
                gate_block()
                split_ahead()
                x_low(4, lambda k: vec(key("gla_norm_2"), k))
                nflat = normed[:].rearrange("p t n -> p (t n)")
                kr = z[:, :, KR:Z2]
                dve.wait_ge(trig_done, 1)
                small = [nflat[:, 1024 + a * 32:1056 + a * 32].rearrange("p (t f) -> p t f", t=TT) for a in range(4)]
                rotate(kr[:, :, 0:16], kr[:, :, 16:32], rope2[:, 0], rope2[:, 1], small)
                dve.drain()
                for nb in range(2):
                    st["unit"] += 1
                    split_ahead(1)
                st["unit"] += 1
                split_ahead(1)
                split_ahead()
                dve.wait_ge(acc_out, seen(acc_out, 4 + 2 + 2))
                big = [nflat[:, a * 256:(a + 1) * 256].rearrange("p (t h f) -> p t h f", t=TT, h=HEADS) for a in range(4)]
                cos, sin = (rope2[:, a].unsqueeze(2).broadcast_to([P, TT, HEADS, 16]) for a in range(2))
                rotate(qf[:, :, :, 64:80], qf[:, :, :, 80:96], cos, sin, big)
                dve.tensor_copy(kf[:, :, :, 64:96], kr.unsqueeze(2).broadcast_to([P, TT, HEADS, 32])).then_inc(mrope_done, 1)
                for nb in range(2):
                    gated(nb, 1, False)
                split_ahead()
                seen(acc_out, 2)
                attention(second_steps(), lambda b: lanes_of(m_pT[:, b]))
                dve.wait_ge(pv_done, seen.now(pv_done))
                dve.reciprocal(m_sum[:], m_sum[:])
                dve.drain()
                for t in range(TT):
                    last = dve.tensor_tensor(normed[:, t, 512:1024].rearrange("p (h d) -> p h d", d=HD),
                                             aux[:, 1 + t].rearrange("p (h d) -> p h d", d=HD),
                                             m_sum[:, t].unsqueeze(2).broadcast_to([P, HEADS, HD]), ALU.mult)
                last.then_inc(normed_ready, 1)
                x_low(4, None)
                for nb in range(2):
                    gated(nb, 2, False)
                    dve.drain().then_inc(normed_ready, 1)
                x_low(KC8, None)
                split_ahead()
                dve.wait_ge(post_in, 32 * (DEPTH + l + 1))
                st["unit"] += 2
                split_ahead(1)
                for t in range(TT):
                    gained(0, t, 0)
                st["unit"] += 2
                split_ahead(1)
                for t in range(TT):
                    gained(0, t, 1)
                    residual(t)
                norm_of_h()
                split_ahead()
                x_low(KC8, lambda k: vec(key("norm_pre_ffn_2"), k))
                ffn_steps("second", l)
                for t in range(TT):
                    for b in range(2):
                        gained(1, t, b)
                    residual(t)
                seen(acc_out, 2 + 2 * 2)

        @block.tensor
        def _(pe):
            seen = Seen()
            st = {"unit": 0}
            out_n = {"n": 0}

            def weights(u):
                return whi[:, u % RING], wlo[:, u % RING]

            def three(o, xs, ws, start, stop, **kw):
                (xh, xl), (wh, wl) = xs, ws
                for n, (x, w) in enumerate(((xh, wh), (xh, wl), (xl, wh))):
                    last = pe.matmul(o, x, w, start=start and n == 0, stop=stop and n == 2, **kw)
                return last

            def project(blocks, x=(xhi, xlo), bank=0, pairs=None, tiles_apart=False, then=None):
                base = out_n["n"]
                pe.wait_ge(acc_out, base) if base else None
                for i, unit_cols in enumerate(blocks):
                    if i >= 2:
                        pe.wait_ge(acc_out, base + i - 1)
                    nks = sum(kc for kc, n in unit_cols)
                    k = 0
                    for kc, n in unit_cols:
                        u = st["unit"]
                        pe.wait_ge(lo_ready, u + 1)
                        wh, wl = weights(u)
                        apart = tiles_apart and i == len(blocks) - 1 and k + kc == nks
                        order = ([(c, t) for t in range(TT) for c in range(kc)] if apart
                                 else [(c, t) for c in range(kc) for t in range(TT)])
                        for c, t in order:
                            if i == 0 and pairs and (k + c) % 2 == 0 and t == 0:
                                pe.wait_ge(pairs, seen(pairs))
                            rows = slice(t * P, (t + 1) * P)
                            last = three(acc[:, t, (i + bank) % 2, 0:n], (x[0][:, k + c, rows], x[1][:, k + c, rows]),
                                         (wh[:, c * n:(c + 1) * n], wl[:, c * n:(c + 1) * n]),
                                         k + c == 0, k + c == nks - 1, skip_group_check=True)
                            if apart and (c, t) == (kc - 1, 0):
                                last.then_inc(tile_done, 1)
                        last.then_inc(unit_done, 1)
                        st["unit"] += 1
                        k += kc
                        if then and k == kc and i == 0:
                            then()
                out_n["n"] += len(blocks)

            def two_blocks_unit(at, pairs, x=(xhi, xlo), blocks_apart=False):
                pe.wait_ge(acc_out, out_n["n"])
                u = st["unit"]
                pe.wait_ge(lo_ready, u + 1)
                wh, wl = weights(u)
                if pairs:
                    pe.wait_ge(pairs, seen(pairs))
                for nb in range(2):
                    for c in range(2):
                        cols = slice(c * DM + nb * BLK, c * DM + (nb + 1) * BLK)
                        for t in range(TT):
                            rows = slice(t * P, (t + 1) * P)
                            last = three(acc[:, t, nb, :], (x[0][:, at + c, rows], x[1][:, at + c, rows]),
                                         (wh[:, cols], wl[:, cols]), c == 0, c == 1, skip_group_check=True)
                    if blocks_apart and nb == 0:
                        last.then_inc(half_done, 1)
                last.then_inc(unit_done, 1)
                st["unit"] += 1
                out_n["n"] += 2

            def turn(src, nk, at=0, banks=aux_banks):
                for k in range(0, nk, 2):
                    n = turned["n"]
                    if n >= 2:
                        pe.wait_ge(x_split, n - 1)
                    for j in range(min(2, nk - k)):
                        for t in range(TT):
                            c0 = at + (k + j) * P
                            last = pe.transpose(banks(n)[:, j * SEQ + t * P:j * SEQ + (t + 1) * P],
                                                src[:, t, c0:c0 + P], ident)
                    last.then_inc(tp_ready, 1)
                    turned["n"] += 1

            turned = {"n": 0}

            def full(nblocks):
                return [[(4, BLK), (4, BLK)] for _ in range(nblocks)]

            def ffn_steps(which, l):
                u0 = ffn[which, l]
                fs0 = seen.now(f_split)
                pe.wait_ge(acc_out, out_n["n"])

                def up(j_unit, u, par, pairs=None, announce=False):
                    for part in range(2):
                        pe.wait_ge(lo_ready, j_unit + (part + 1))
                        wh, wl = weights(u + part)
                        by_chunk = pairs is not None and part == 0
                        order = ([(c2, k) for k in range(KC8) for c2 in range(2)] if by_chunk
                                 else [(c2, k) for c2 in range(2) for k in range(KC8)])
                        if by_chunk:
                            pe.matmul(aux[:, 2 - 2 * par + part, :], zero_row[:, 0:P], zero_row[:], start=True, stop=False,
                                      skip_group_check=True)
                        for c2, k in order:
                            if by_chunk and k % 2 == 0 and c2 == 0:
                                pe.wait_ge(pairs, seen(pairs))
                            cols = slice(k * FB + c2 * P, k * FB + (c2 + 1) * P)
                            for n, (w, x) in enumerate(((wh, xhi), (wh, xlo), (wl, xhi))):
                                last = pe.matmul(aux[:, 2 - 2 * par + part, c2 * SEQ:(c2 + 1) * SEQ], w[:, cols], x[:, k],
                                                 start=(k == 0 and n == 0 and not by_chunk), stop=(k == KC8 - 1 and n == 2),
                                                 skip_group_check=True)
                                if announce and part == 0 and c2 == 0 and k == 0 and n == 0:
                                    last.then_inc(unit_done, 1)
                        last.then_inc(unit_done if part == 0 else gu_ready, 1)

                def down(j, j_unit, u, par, announce, stop=False):
                    pe.wait_ge(lo_ready, j_unit + 1)
                    pe.wait_ge(f_split, j + (fs0 + 1))
                    wh, wl = weights(u)
                    for t in range(TT):
                        rows = slice(t * P, (t + 1) * P)
                        for c2 in range(2):
                            for n, (x, w) in enumerate(((fhi, wh), (fhi, wl), (flo, wh))):
                                for nb in range(2):
                                    cols = slice(c2 * DM + nb * BLK, c2 * DM + (nb + 1) * BLK)
                                    last = pe.matmul(acc[:, t, nb, :], x[:, par, c2, rows], w[:, cols], start=False,
                                                     stop=stop and c2 == 1 and n == 2, skip_group_check=True)
                                    if announce and c2 == 0 and t == 0 and n == 0 and nb == 0:
                                        last.then_inc(unit_done, 1)
                        if stop and t == 0:
                            last.then_inc(tile_done, 1)
                    last.then_inc(unit_done, 1)

                up(u0, u0, 0, pairs=x_split)
                up(u0 + 2, u0 + 2, 1, announce=True)
                for t in range(TT):
                    for nb in range(2):
                        last = pe.matmul(acc[:, t, nb, :], zero_row[:, 0:P], zero_row[:], start=True, stop=False,
                                         skip_group_check=True)
                last.then_inc(unit_done, 1)

                def step(j, j_unit, u, par):
                    pe.wait_ge(f_split, j + (fs0 + 1))
                    up(j_unit, u, par)
                    down(j, j_unit + 2, u + 2, par, True)

                with pe.Fori(0, FLOOP) as i:
                    for s in range(2):
                        first = u0 + 4 + 3 * s
                        step(i * 2 + s, i * 6 + first, first, s)
                step(FSTEPS - 3, u0 + FUNITS - 5, u0 + FUNITS - 5, 0)
                down(FSTEPS - 2, u0 + FUNITS - 2, u0 + FUNITS - 2, 1, False)
                down(FSTEPS - 1, u0 + FUNITS - 1, u0 + FUNITS - 1, 0, False, True)
                seen(f_split, FSTEPS)
                st["unit"] = u0 + FUNITS
                out_n["n"] += 2

            def attention(steps, e, pt, before_sums=None):
                b_e, b_pts, b_dve = seen.now(e_ready), seen.now(pts_ready), seen.now(pts_ready_dve)
                n = len(steps)
                for i in range(n + 2):
                    if i < n:
                        if i >= 2:
                            pe.wait_ge(e_ready, b_e + i - 1)
                        nk = steps[i]["nk"]
                        for a, lane in enumerate(steps[i]["lanes"]):
                            last = pe.matmul(acc[:, 0, i % 2, a * 256:a * 256 + nk], lane["q"], lane["k"][:, 0:nk],
                                             start=True, stop=True)
                        last.then_inc(s_ready, 1)
                    j = i - 1
                    if 0 <= j < n:
                        pe.wait_ge(e_ready, b_e + j + 1)
                        for a in range(2):
                            for kt in range(steps[j]["nk"] // P):
                                c0 = a * 256 + kt * P
                                last = pe.transpose(acc[:, 1, j % 2, c0:c0 + P], e[:, j % 2, c0:c0 + P], ident)
                        last.then_inc(pt_ready, 1)
                    j = i - 2
                    if j == 0 and before_sums:
                        before_sums()
                    if 0 <= j < n:
                        if j % 2 == 0:
                            pe.wait_ge(pts_ready, b_pts + j // 2 + 1)
                        else:
                            pe.wait_ge(pts_ready_dve, b_dve + j // 2 + 1)
                        nkt = steps[j]["nk"] // P
                        for a, lane in enumerate(steps[j]["lanes"]):
                            for kt in range(nkt):
                                last = pe.matmul(lane["o"], pt(j % 2)[:, a, kt * P:(kt + 1) * P], lane["v"][:, kt],
                                                 start=(kt == 0), stop=(kt == nkt - 1))
                        last.then_inc(pv_done, 1)
                seen(e_ready, n), seen(pts_ready, n // 2), seen(pts_ready_dve, n // 2)

            pe.wait_ge(masks_in, 16)
            pe.wait_ge(setup_done, 2)

            for l in range(DEPTH):
                if l:
                    pe.wait_ge(h_ready, 3 * TT * l)
                else:
                    pe.wait_ge(h_in, 16)
                turn(h, KC8)
                project([[(4, n), (4, n)] for c0, n in W1_BLOCKS[:-1]], pairs=x_split)
                project(full(1))
                pe.wait_ge(zc2_done, seen(zc2_done))
                for kv in range(2):
                    for g in range(GROUPS):
                        for t in range(TT):
                            last = pe.transpose(aux[:, kv, g * SEQ + t * P:g * SEQ + (t + 1) * P],
                                                zc2[:, t, kv * 2 + g].rearrange("p a d -> p (a d)"), ident)
                    last.then_inc(ct_ready, 1)
                pe.wait_ge(rope_done, seen(rope_done, TT))
                for i in range(6):
                    if i >= 2:
                        pe.wait_ge(qk_out, seen(qk_out))
                    t, which = i % 2, i // 2
                    for j in range(4):
                        c0 = (which * 4 + j) * HD if which < 2 else 768 + (j // 2) * 256 + (j % 2) * HD
                        last = pe.transpose(aux[0:HD, 2 + i % 2, j * P:(j + 1) * P], z[:, t, c0:c0 + HD], ident)
                    last.then_inc(qk_ready, 1)
                pe.wait_ge(acc_out, out_n["n"])
                for kv in range(2):
                    pe.wait_ge(xc_split, seen(xc_split))
                    if kv == 0:
                        pe.wait_ge(small1_in, 16 * SMALL1 * (l + 1))
                        for g in range(8):
                            last = pe.transpose(aux[:, g // 4, (g % 4) * P:(g % 4 + 1) * P], ws_raw[:, g, :], ident)
                        last.then_inc(ws_ready, 1)
                    for half in range(2):
                        u = st["unit"]
                        pe.wait_ge(lo_ready, u + 1)
                        wh, wl = weights(u)
                        xs = [x_cmp_split(f, kv).rearrange("p (c r) -> p c r", c=16) for f in (xhi_flat, xlo_flat)]
                        for c in range(8):
                            cols = slice(c * CMP_HID, (c + 1) * CMP_HID)
                            last = three(acc[0:2 * CMP_N, 0, kv, 0:CMP_HID], (xs[0][:, half * 8 + c], xs[1][:, half * 8 + c]),
                                         (wh[:, cols], wl[:, cols]), half + c == 0, half == 1 and c == 7,
                                         skip_group_check=True)
                        last.then_inc(unit_done, 1)
                        st["unit"] += 1
                pe.wait_ge(hid_out, seen(hid_out, 2))
                for kv in range(2):
                    for c2 in range(2):
                        last = pe.transpose(acc[:, 1, kv, c2 * 30:(c2 + 1) * 30], hid[:, kv, c2 * P:(c2 + 1) * P],
                                            ident[0:2 * CMP_N, 0:2 * CMP_N])
                last.then_inc(hidT_ready, 1)
                pe.wait_ge(hT_out, seen(hT_out))
                pe.wait_ge(qk_out, seen(qk_out, 2))
                for kv in range(2):
                    for g in range(GROUPS):
                        for c2 in range(2):
                            last = pe.matmul(aux[0:CMP_N, 2, (kv * 2 + g) * HD:(kv * 2 + g + 1) * HD],
                                             hT[:, kv, c2, g * CMP_N:(g + 1) * CMP_N], cmp_w2[:, kv, c2, :],
                                             start=(c2 == 0), stop=(c2 == 1))
                last.then_inc(kcv_ready, 1)
                pe.wait_ge(kcv_out, seen(kcv_out))
                for g in range(GROUPS):
                    last = pe.transpose(aux[0:HD, 3, g * CMP_N:(g + 1) * CMP_N], kcv[:, 0, g, :], ident[0:CMP_N, 0:CMP_N])
                last.then_inc(kcT_ready, 1)
                pe.wait_ge(kcT_out, seen(kcT_out))
                for t in range(TT):
                    for hd in range(HEADS):
                        c0 = (t * HEADS + hd) * CMP_N
                        last = pe.matmul(aux[:, 2, c0:c0 + CMP_N], qT[:, hd, t * P:(t + 1) * P], kcT[:, hd // 4, :],
                                         start=True, stop=True)
                last.then_inc(sc_ready, 1)
                pe.wait_ge(ws_out, seen(ws_out))
                pe.wait_ge(ln_done, seen(ln_done))
                for g in range(8):
                    last = pe.matmul(aux[:, g // 4, (g % 4) * P:(g % 4 + 1) * P], wsT[:, g, :],
                                     z[:, :, V1 + g * HD:V1 + (g + 1) * HD], start=True, stop=True)
                last.then_inc(mix_ready, 1)
                pe.wait_ge(ec_ready, seen(ec_ready))
                for t in range(TT):
                    for hd in range(HEADS):
                        last = pe.transpose(acc[0:CMP_N, t, hd // 4, (hd % 4) * P:(hd % 4 + 1) * P], ec[:, t, hd, :], ident)
                    last.then_inc(ect_ready, 1)
                for t in range(TT):
                    pe.wait_ge(ect_out, seen(ect_out))
                    for hd in range(HEADS):
                        last = pe.matmul(aux[:, 3 - t, hd * HD:(hd + 1) * HD], ecT[:, t, hd, :], kcv[:, 1, hd // 4, :],
                                         start=True, stop=True)
                last.then_inc(cpv_done, 1)

                def mixers_out():
                    pe.wait_ge(cmp_out, seen(cmp_out))
                    pe.wait_ge(gmlp_out, seen(gmlp_out))

                attention(first_steps(), e_buf, lambda b: lanes_of(pT[:, b]), mixers_out)
                pe.wait_ge(normed_ready, seen(normed_ready))
                turn(normed, 4, at=512, banks=acc_second)

                def turn_attention():
                    pe.wait_ge(normed_ready, seen(normed_ready, TT))
                    turn(normed, 4)

                project(full(2), pairs=x_split, tiles_apart=True, then=turn_attention)
                pe.wait_ge(normed_ready, seen(normed_ready, 2))
                turn(normed, KC8)
                ffn_steps("first", l)
                pe.wait_ge(h_ready, (3 * l + 2) * TT)
                turn(h, KC8)
                project(full(2), pairs=x_split)
                turn(p_in, 2)
                two_blocks_unit(0, x_split, blocks_apart=True)

            for l in range(DEPTH):
                pe.wait_ge(h_ready, (3 * DEPTH + 2 * l) * TT)
                turn(h, KC8)
                project([[(4, n), (4, n)] for c0, n in blocks_of(0, Z2)], pairs=x_split)

                def gate_block(bank=0):
                    project(full(1), bank=bank)

                pe.wait_ge(acc_out, out_n["n"])
                pe.wait_ge(pool_in, 32 * (l + 1))
                for g in range(4):
                    for s in range(TT):
                        last = pe.matmul(aux[:, g // 2, (g % 2) * SEQ:(g % 2 + 1) * SEQ], z[:, s, g * P:(g + 1) * P],
                                         pool_mat[:, s, g, :], start=(s == 0), stop=(s == 1))
                last.then_inc(diff_ready, 1)
                gate_block()
                pe.wait_ge(diff_out, seen(diff_out))
                for g in range(4):
                    last = pe.matmul(aux[:, 2 + g // 2, (g % 2) * SEQ:(g % 2 + 1) * SEQ], w_pool[:, g, :], diffT[:, g, :],
                                     start=True, stop=True)
                last.then_inc(ypool_ready, 1)
                for t in range(TT):
                    last = pe.transpose(aux[0:16, 0, t * P:(t + 1) * P], z[:, t, GA:CQ], ident)
                last.then_inc(a1_ready, 1)
                gate_block()
                pe.wait_ge(a1_out, seen(a1_out))
                pe.wait_ge(small2_in, 32 * (l + 1))
                for t in range(TT):
                    last = pe.matmul(aux[:, 1, t * 256:(t + 1) * 256], a1T[:, t * P:(t + 1) * P], w_a2, start=True, stop=True)
                last.then_inc(la_pre, 1)
                pe.wait_ge(yp_split, seen(yp_split))
                project([[(4, BLK)], [(4, BLK)]], x=(yhi, ylo))
                pe.wait_ge(la_ready, seen(la_ready))
                for i, mat in enumerate((chunk_le, chunk_gt)):
                    for t in range(TT):
                        pe.matmul(aux[:, i, t * 256:(t + 1) * 256], mat, la[:, t], start=True, stop=True)
                for hd in range(4):
                    for t in range(TT):
                        last = pe.matmul(aux[0:HD, 2, hd * 4 + t * 2:hd * 4 + t * 2 + 2], la[:, t, hd * HD:(hd + 1) * HD],
                                         chunk_of, start=True, stop=True)
                last.then_inc(cum_ready, 1)
                gate_block()
                pe.wait_ge(qk_dec, seen(qk_dec))
                for i in range(4):
                    src = z[:, i % 2, GQ:GK] if i < 2 else e_inv[:, i % 2]
                    for hd in range(4):
                        last = pe.transpose(aux[0:HD, i, hd * P:(hd + 1) * P], src[:, hd * HD:(hd + 1) * HD], ident)
                    last.then_inc(gT_ready, 1)
                gate_block(bank=1)
                pe.wait_ge(gT_out, seen(gT_out, 4))
                for t in range(TT):
                    rows = slice(t * P, (t + 1) * P)
                    for hd in range(4):
                        last = pe.matmul(acc[:, t, 0, hd * P:(hd + 1) * P], kiT[:, hd, rows], qdT[:, hd, rows], start=True, stop=True)
                last.then_inc(att_ready, 1)
                for n in range(3):
                    rows = slice((n % 2) * 64, (n % 2 + 1) * 64)
                    for hd in range(4):
                        last = pe.matmul(aux[0:HD, n, hd * P:(hd + 1) * P], e_suf[rows, n // 2, hd * HD:(hd + 1) * HD],
                                         z[rows, n // 2, GV + hd * P:GV + (hd + 1) * P], start=True, stop=True)
                last.then_inc(kv_ready, 1)
                pe.wait_ge(att_out, seen(att_out))
                gate_block()
                pe.wait_ge(states_ready, seen(states_ready))
                for t in range(TT):
                    for hd in range(4):
                        cols = slice(hd * P, (hd + 1) * P)
                        pe.matmul(acc[:, t, 1, cols], attM[:, t, hd, :], z[:, t, GV + hd * P:GV + (hd + 1) * P],
                                  start=True, stop=False, skip_group_check=True)
                        for c in range(2):
                            n = 2 * t + c
                            if n:
                                last = pe.matmul(acc[c * 64:(c + 1) * 64, t, 1, cols], qdT[:, hd, n * 64:(n + 1) * 64],
                                                 state[:, n - 1, hd, :], start=False, stop=True, skip_group_check=True)
                last.then_inc(og_ready, 1)
                pe.wait_ge(normed_ready, seen(normed_ready))
                turn(z, 5, at=CQ)
                gate_block()
                pe.wait_ge(normed_ready, seen(normed_ready))
                turn(normed, 4)
                project([[(3, 384)], [(3, 384)]], x=(yhi, ylo), pairs=x_split)
                two_blocks_unit(3, x_split, x=(yhi, ylo))
                project([[(4, BLK)], [(4, BLK)]], pairs=x_split)
                pe.wait_ge(mrope_done, seen(mrope_done))
                for i in range(8):
                    if i >= 4:
                        pe.wait_ge(mT_out, seen(mT_out))
                    t, hg, which = i % 2, i // 2 % 2, i // 4
                    for j in range(4):
                        last = pe.transpose(aux[0:QK, i % 4, j * P:(j + 1) * P], (qf, kf)[which][:, t, hg * 4 + j, :], ident)
                    last.then_inc(mT_ready, 1)
                pe.wait_ge(mT_out, seen(mT_out, 4))
                pe.wait_ge(acc_out, out_n["n"])
                attention(second_steps(), m_e, lambda b: lanes_of(m_pT[:, b]))
                pe.wait_ge(normed_ready, seen(normed_ready))
                turn(normed, 4, at=512)
                project([[(4, BLK)], [(4, BLK)]], pairs=x_split)
                for nb in range(2):
                    pe.wait_ge(normed_ready, seen(normed_ready))
                    turn(merged, 4, at=nb * BLK)
                project(full(2), pairs=x_split, tiles_apart=True)
                pe.wait_ge(normed_ready, seen(normed_ready, 2))
                turn(normed, KC8)
                ffn_steps("second", l)


def shape_constants():
    import numpy as np
    f = np.float32
    i = np.arange(P)
    c = {}
    same = (i[:, None] // 64) == (i[None, :] // 64)
    tok = np.arange(SEQ).reshape(TT, P)
    ok = (16 * np.arange(CMP_N) + 31)[None, None, :] <= tok.T[:, :, None]
    c["c_masks"] = np.concatenate([
        np.eye(P), np.where(i[None, :] <= i[:, None], 0, NEG), i[:, None] <= i[None, :],
        same & (i[:, None] <= i[None, :]), same & (i[:, None] > i[None, :]),
        (i[:, None] // 64) == np.arange(2)[None, :], np.where(ok, 0, NEG).reshape(P, -1), ok.reshape(P, -1)],
        axis=1).astype(f)
    inv = (f(500000.0) ** (-np.arange(8, dtype=f) / f(8))).astype(f)

    def table(pos):
        ang = pos.astype(f)[:, None] * inv[None, :]
        return np.cos(ang).astype(f), np.sin(ang).astype(f)

    cos, sin = table(np.arange(SEQ))
    t = np.zeros((P, 2, TT, ROPE_UNITS, 8), f)
    t[:, 0] = 1
    for u in list(range(8)) + [12, 13, 16, 17]:
        t[:, 0, :, u] = cos.reshape(TT, P, 8).transpose(1, 0, 2)
        t[:, 1, :, u] = sin.reshape(TT, P, 8).transpose(1, 0, 2)
    c["c_rope1"] = np.ascontiguousarray(t.transpose(0, 2, 1, 3, 4).reshape(P, TT, 320))
    cos, sin = table(np.arange(CMP_N) * 16 + 31)
    c["c_rope_c"] = np.ascontiguousarray(np.stack([np.stack([x, x], 1) for x in (cos, sin)], 1))
    c["c_inv_freq"] = (f(10000.0) ** (-np.arange(0, 32, 2, dtype=f) / f(32))).astype(f)
    s = np.arange(SEQ)
    mats = []
    for w in (2, 4, 8, 16):
        m = ((s[None, :] <= s[:, None]) & (s[None, :] > s[:, None] - w)) / np.minimum(s + 1, w)[:, None] - np.eye(SEQ)
        mats.append(m.T.astype(f))
    c["c_pool"] = np.ascontiguousarray(np.stack(mats, 1).reshape(TT, P, 4, SEQ).transpose(1, 0, 2, 3))
    return c


def kernel(**inputs):
    import numpy as np
    import concourse.bacc as bacc
    from concourse.bass_utils import run_bass_kernel_spmd as run

    arrays = {}
    for name, a in inputs.items():
        a = np.ascontiguousarray(a)
        if name == "x":
            a = a[0]
        elif name == "positions_2":
            a = a[0].reshape(TT, P).T
        elif name == "p":
            a = a[:, 0]
        arrays[name] = a
    rows = [arrays[name].reshape(DEPTH, n, P)[l] for names in (VECS1, VECS2) for l in range(DEPTH) for name, n in names]
    arrays["vecs"] = np.concatenate(rows, axis=0).T
    for name, _ in VECS1 + VECS2:
        del arrays[name]
    rows = []
    for name, at, r0, c0, kc, n in unit_plan()[0]:
        rows.append(arrays[name][at][r0:r0 + kc * P, c0:c0 + n].reshape(kc, P, n).transpose(1, 0, 2).reshape(-1))
    for name in {unit[0] for unit in unit_plan()[0]}:
        del arrays[name]
    arrays["weights"] = np.concatenate(rows)
    arrays.update(shape_constants())
    nc = bacc.Bacc("TRN2", target_bir_lowering=False, num_devices=1)
    A = {}
    feed = {}
    for name, a in arrays.items():
        feed["in_" + name] = np.ascontiguousarray(a)
        A[name] = nc.dram_tensor("in_" + name, a.shape, mybir.dt.from_np(a.dtype), kind="ExternalInput").ap()
    out = nc.dram_tensor("out_h", (SEQ, DM), F32, kind="ExternalOutput").ap()
    two_blocks(nc, A, out)
    r = run(nc, [feed], core_ids=[0])
    return r.results[0]["out_h"].reshape(1, SEQ, DM)
```
